# Optimizing a Trainium2 kernel written in Bass

```python
import math
import jax, jax.numpy as jnp
from jax import lax
import numpy as np

D_MODEL = 1024
BATCH = 1
SEQ = 512
DEPTH = 2

N_EVEN = (DEPTH + 1) // 2
N_ODD = DEPTH // 2
MIX_WIDTH = D_MODEL
HALF = MIX_WIDTH // 2

ML_HEADS = 4
ML_HD = HALF // ML_HEADS
ML_CHUNK = 64
FOX_HEADS = 8
FOX_HD = HALF // FOX_HEADS
FOX_QBLOCK = 128
SSM_HEADDIM = 64
SSM_HEADS = HALF // SSM_HEADDIM
SSM_GROUPS = 2
SSM_HPG = SSM_HEADS // SSM_GROUPS
SSM_STATE = 128
SSM_CONV = 4
SSM_CHUNK = 128
SSM_CONV_CH = HALF + 2 * SSM_GROUPS * SSM_STATE
POOL_WINDOWS = (2, 4, 8, 16)
POOL_GROUPS = 4
POOL_GW = HALF // POOL_GROUPS
D_FF = 256 * ((8 * D_MODEL // 3 + 255) // 256)
FFN_CONV = 3

EVEN_IN = 4 * HALF + 2 * ML_HEADS + 3 * HALF + FOX_HEADS
ODD_IN = HALF + SSM_CONV_CH + SSM_HEADS + HALF
LN_EPS = 1e-5
ALPHA = (2.0 * DEPTH) ** 0.25
BETA = (8.0 * DEPTH) ** -0.25


def split_sizes(x, sizes):
    offs = []
    acc = 0
    for s in sizes[:-1]:
        acc += s
        offs.append(acc)
    return jnp.split(x, offs, axis=-1)

def layer_norm(x, g, b):
    xf = x.astype(jnp.float32)
    mu = xf.mean(-1, keepdims=True)
    var = jnp.square(xf - mu).mean(-1, keepdims=True)
    return ((xf - mu) * lax.rsqrt(var + LN_EPS) * g.astype(jnp.float32) + b.astype(jnp.float32)).astype(x.dtype)

def rms_norm(x, g):
    xf = x.astype(jnp.float32)
    return xf * lax.rsqrt(jnp.square(xf).mean(-1, keepdims=True) + LN_EPS) * g.astype(jnp.float32)

def causal_dwconv(x, w, b):
    k, c = w.shape
    y = lax.conv_general_dilated(x, w[:, None, :].astype(x.dtype), window_strides=(1,), padding=[(k - 1, 0)], dimension_numbers=('NWC', 'WIO', 'NWC'), feature_group_count=c)
    return y + b.astype(x.dtype)

def mlstm_chunkwise(q, k, v, i_pre, f_pre):
    b, h, s, d = q.shape
    L = ML_CHUNK
    nc = s // L
    q = q.astype(jnp.float32) * (d ** -0.5)
    k = k.astype(jnp.float32)
    v = v.astype(jnp.float32)
    ig = i_pre.astype(jnp.float32)
    logf = jax.nn.log_sigmoid(f_pre.astype(jnp.float32))

    def to_chunks(t):
        return jnp.moveaxis(t.reshape(b, h, nc, L, *t.shape[3:]), 2, 0)

    causal = jnp.tril(jnp.ones((L, L), dtype=bool))

    def step(carry, inp):
        c_st, n_st, m_st = carry
        qq, kk, vv, ii, ff = inp
        bcum = jnp.cumsum(ff, axis=-1)
        a = bcum + m_st[..., None]
        dmat = jnp.where(causal, bcum[..., :, None] - bcum[..., None, :] + ii[..., None, :], -jnp.inf)
        mt = jnp.maximum(a, dmat.max(-1))
        w_intra = jnp.exp(dmat - mt[..., None])
        w_inter = jnp.exp(a - mt)
        qk = jnp.einsum('bhld,bhsd->bhls', qq, kk) * w_intra
        num = jnp.einsum('bhls,bhsd->bhld', qk, vv) + w_inter[..., None] * jnp.einsum('bhvk,bhlk->bhlv', c_st, qq)
        den = qk.sum(-1) + w_inter * jnp.einsum('bhk,bhlk->bhl', n_st, qq)
        h_out = num / jnp.maximum(jnp.abs(den), jnp.exp(-mt))[..., None]
        btot = bcum[..., -1]
        g_log = btot[..., None] - bcum + ii
        m_new = jnp.maximum(btot + m_st, g_log.max(-1))
        ws = jnp.exp(g_log - m_new[..., None])
        decay = jnp.exp(btot + m_st - m_new)
        c_new = decay[..., None, None] * c_st + jnp.einsum('bhl,bhlv,bhlk->bhvk', ws, vv, kk)
        n_new = decay[..., None] * n_st + jnp.einsum('bhl,bhlk->bhk', ws, kk)
        return (c_new, n_new, m_new), h_out

    init = (jnp.zeros((b, h, d, d), jnp.float32), jnp.zeros((b, h, d), jnp.float32), jnp.zeros((b, h), jnp.float32))
    _, hs = lax.scan(step, init, (to_chunks(q), to_chunks(k), to_chunks(v), to_chunks(ig), to_chunks(logf)))
    return jnp.moveaxis(hs, 0, 2).reshape(b, h, s, d)

def forgetting_attention(q, k, v, f_pre):
    b, h, s, d = q.shape
    F = jnp.cumsum(jax.nn.log_sigmoid(f_pre.astype(jnp.float32)), axis=-1)
    nb = s // FOX_QBLOCK
    kpos = jnp.arange(s)
    scale = d ** -0.5

    def block(i):
        start = i * FOX_QBLOCK
        qb = lax.dynamic_slice_in_dim(q, start, FOX_QBLOCK, axis=2)
        fq = lax.dynamic_slice_in_dim(F, start, FOX_QBLOCK, axis=2)
        qpos = start + jnp.arange(FOX_QBLOCK)
        logits = jnp.einsum('bhqd,bhkd->bhqk', qb, k).astype(jnp.float32) * scale + fq[..., :, None] - F[..., None, :]
        logits = jnp.where(kpos[None, :] <= qpos[:, None], logits, -jnp.inf)
        p = jax.nn.softmax(logits, axis=-1)
        return jnp.einsum('bhqk,bhkd->bhqd', p.astype(v.dtype), v)

    out = lax.map(block, jnp.arange(nb))
    return jnp.moveaxis(out, 0, 2).reshape(b, h, s, d)

def segsum(a):
    L = a.shape[-1]
    cs = jnp.cumsum(a, axis=-1)
    mask = jnp.tril(jnp.ones((L, L), dtype=bool))
    return jnp.where(mask, cs[..., :, None] - cs[..., None, :], -jnp.inf)

def ssd_chunked(x, dt_a, bm, cm):
    b, s, g, e, p = x.shape
    L = SSM_CHUNK
    nc = s // L
    x = x.reshape(b, nc, L, g, e, p)
    bm = bm.reshape(b, nc, L, g, -1)
    cm = cm.reshape(b, nc, L, g, -1)
    a = jnp.moveaxis(dt_a.reshape(b, nc, L, g, e), (1, 2), (3, 4))
    a_cs = jnp.cumsum(a, axis=-1)
    lmat = jnp.exp(segsum(a))
    cb = jnp.einsum('bclgn,bcsgn->bgcls', cm, bm)
    y_diag = jnp.einsum('bgcls,bgecls,bcsgep->bclgep', cb, lmat, x)
    decay_states = jnp.exp(a_cs[..., -1:] - a_cs)
    states = jnp.einsum('bclgn,bgecl,bclgep->bcgepn', bm, decay_states, x)
    chunk_decay = jnp.exp(a_cs[..., -1])

    def step(hst, inp):
        st, dec = inp
        return dec[..., None, None] * hst + st, hst

    h0 = jnp.zeros((b, g, e, p, states.shape[-1]), jnp.float32)
    _, prev = lax.scan(step, h0, (jnp.moveaxis(states, 1, 0), jnp.moveaxis(chunk_decay, 3, 0)))
    y_off = jnp.einsum('bclgn,cbgepn,bgecl->bclgep', cm, prev, jnp.exp(a_cs))
    return (y_diag + y_off).reshape(b, s, g, e, p)

def multiscale_pool(u, w_grp, b_grp, scale):
    b, s, c = u.shape
    uf = u.astype(jnp.float32)
    csz = jnp.concatenate([jnp.zeros((b, 1, c), jnp.float32), jnp.cumsum(uf, axis=1)], axis=1)
    t = jnp.arange(s)
    outs = []
    for gi, w in enumerate(POOL_WINDOWS):
        lo_c, hi_c = gi * POOL_GW, (gi + 1) * POOL_GW
        cg = csz[:, :, lo_c:hi_c]
        lo = jnp.maximum(t + 1 - w, 0)
        wsum = cg[:, 1:] - jnp.take(cg, lo, axis=1)
        cnt = jnp.minimum(t + 1, w).astype(jnp.float32)
        outs.append(wsum / cnt[None, :, None] - uf[:, :, lo_c:hi_c])
    pooled = jnp.stack(outs, axis=2)
    y = jnp.einsum('bsgc,gcd->bsgd', pooled, w_grp.astype(jnp.float32)).reshape(b, s, c) + b_grp.astype(jnp.float32)
    return y * scale.astype(jnp.float32)

def head_norm(h, g):
    nh, d = h.shape[1], h.shape[3]
    mu = h.mean(-1, keepdims=True)
    var = jnp.square(h - mu).mean(-1, keepdims=True)
    return (h - mu) * lax.rsqrt(var + LN_EPS) * g.astype(jnp.float32).reshape(nh, 1, d)

def even_mixer(x, w_in, b_in, ml_norm, w_out):
    b, s, _ = x.shape
    u = x @ w_in + b_in
    mq, mk, mv, mo, mi, mf, fq, fk, fv, ff = split_sizes(u, [HALF, HALF, HALF, HALF, ML_HEADS, ML_HEADS, HALF, HALF, HALF, FOX_HEADS])

    def heads(t, nh):
        return t.reshape(b, s, nh, -1).transpose(0, 2, 1, 3)

    h_ml = mlstm_chunkwise(heads(mq, ML_HEADS), heads(mk, ML_HEADS), heads(mv, ML_HEADS), mi.transpose(0, 2, 1), mf.transpose(0, 2, 1))
    h_ml = head_norm(h_ml, ml_norm).transpose(0, 2, 1, 3).reshape(b, s, HALF)
    h_ml = (jax.nn.sigmoid(mo.astype(jnp.float32)) * h_ml).astype(x.dtype)
    h_fx = forgetting_attention(heads(fq, FOX_HEADS), heads(fk, FOX_HEADS), heads(fv, FOX_HEADS), ff.transpose(0, 2, 1))
    h_fx = h_fx.transpose(0, 2, 1, 3).reshape(b, s, HALF).astype(x.dtype)
    return jnp.concatenate([h_ml, h_fx], axis=-1) @ w_out

def odd_mixer(x, w_in, conv_w, conv_b, dt_bias, a_log, d_skip, ssm_norm, pool_w, pool_b, pool_scale, w_out):
    b, s, _ = x.shape
    u = x @ w_in
    z, xbc, dt_raw, pool_in = split_sizes(u, [HALF, SSM_CONV_CH, SSM_HEADS, HALF])
    xbc = jax.nn.silu(causal_dwconv(xbc, conv_w, conv_b)).astype(jnp.float32)
    xs, bm, cm = split_sizes(xbc, [HALF, SSM_GROUPS * SSM_STATE, SSM_GROUPS * SSM_STATE])
    dt = jax.nn.softplus(dt_raw.astype(jnp.float32) + dt_bias.astype(jnp.float32))
    a = -jnp.exp(a_log.astype(jnp.float32)).reshape(SSM_GROUPS, SSM_HPG)
    xh = xs.reshape(b, s, SSM_GROUPS, SSM_HPG, SSM_HEADDIM)
    dth = dt.reshape(b, s, SSM_GROUPS, SSM_HPG)
    y = ssd_chunked(xh * dth[..., None], dth * a, bm.reshape(b, s, SSM_GROUPS, SSM_STATE), cm.reshape(b, s, SSM_GROUPS, SSM_STATE))
    y = y + d_skip.astype(jnp.float32).reshape(SSM_GROUPS, SSM_HPG, 1) * xh
    y = rms_norm(y.reshape(b, s, HALF) * jax.nn.silu(z.astype(jnp.float32)), ssm_norm).astype(x.dtype)
    p = multiscale_pool(pool_in, pool_w, pool_b, pool_scale).astype(x.dtype)
    return jnp.concatenate([y, p], axis=-1) @ w_out

def conv_ffn(x, w_up, conv_w, conv_b, w_down):
    h = causal_dwconv(x @ w_up, conv_w, conv_b)
    val, gate = jnp.split(h, 2, axis=-1)
    return (jax.nn.silu(gate) * val) @ w_down

def first_inputs(seed: int = 0) -> dict:
    key = jax.random.key(seed)
    ks = jax.random.split(key, 40)
    E, O, L = N_EVEN, N_ODD, DEPTH
    nrm = lambda k, shape, sc: jax.random.normal(k, shape, jnp.float32) * sc
    x = nrm(ks[0], (BATCH, SEQ, D_MODEL), 1.0)
    ev_w_in = nrm(ks[1], (E, D_MODEL, EVEN_IN), D_MODEL ** -0.5)
    ev_b_in = jnp.concatenate([
        nrm(ks[2], (E, 4 * HALF), 0.02),
        nrm(ks[3], (E, ML_HEADS), 0.1),
        3.0 + 3.0 * jax.random.uniform(ks[4], (E, ML_HEADS), jnp.float32),
        nrm(ks[5], (E, 3 * HALF), 0.02),
        1.0 + 3.0 * jax.random.uniform(ks[6], (E, FOX_HEADS), jnp.float32)], axis=-1)
    ev_ml_norm = 1.0 + nrm(ks[7], (E, HALF), 0.02)
    ev_w_out = nrm(ks[8], (E, MIX_WIDTH, D_MODEL), MIX_WIDTH ** -0.5 * BETA)
    od_w_in = nrm(ks[9], (O, D_MODEL, ODD_IN), D_MODEL ** -0.5)
    od_conv_w = nrm(ks[10], (O, SSM_CONV, SSM_CONV_CH), SSM_CONV ** -0.5)
    od_conv_b = nrm(ks[11], (O, SSM_CONV_CH), 0.02)
    dt0 = jnp.exp(jax.random.uniform(ks[12], (O, SSM_HEADS), jnp.float32, math.log(1e-3), math.log(1e-1)))
    od_dt_bias = dt0 + jnp.log(-jnp.expm1(-dt0))
    od_a_log = jnp.log(jax.random.uniform(ks[13], (O, SSM_HEADS), jnp.float32, 1.0, 16.0))
    od_d_skip = 1.0 + nrm(ks[14], (O, SSM_HEADS), 0.02)
    od_ssm_norm = 1.0 + nrm(ks[15], (O, HALF), 0.02)
    od_pool_w = nrm(ks[16], (O, POOL_GROUPS, POOL_GW, POOL_GW), POOL_GW ** -0.5)
    od_pool_b = nrm(ks[17], (O, HALF), 0.02)
    od_pool_scale = 1.0 + nrm(ks[18], (O, HALF), 0.1)
    od_w_out = nrm(ks[19], (O, MIX_WIDTH, D_MODEL), MIX_WIDTH ** -0.5 * BETA)
    ffn_w_up = nrm(ks[20], (L, D_MODEL, 2 * D_FF), D_MODEL ** -0.5)
    ffn_conv_w = nrm(ks[21], (L, FFN_CONV, 2 * D_FF), FFN_CONV ** -0.5)
    ffn_conv_b = nrm(ks[22], (L, 2 * D_FF), 0.02)
    ffn_w_down = nrm(ks[23], (L, D_FF, D_MODEL), D_FF ** -0.5 * BETA)
    ln1_g = 1.0 + nrm(ks[24], (L, D_MODEL), 0.02)
    ln1_b = nrm(ks[25], (L, D_MODEL), 0.02)
    ln2_g = 1.0 + nrm(ks[26], (L, D_MODEL), 0.02)
    ln2_b = nrm(ks[27], (L, D_MODEL), 0.02)
    return {'x': x, 'ev_w_in': ev_w_in, 'ev_b_in': ev_b_in, 'ev_ml_norm': ev_ml_norm, 'ev_w_out': ev_w_out,
            'od_w_in': od_w_in, 'od_conv_w': od_conv_w, 'od_conv_b': od_conv_b, 'od_dt_bias': od_dt_bias,
            'od_a_log': od_a_log, 'od_d_skip': od_d_skip, 'od_ssm_norm': od_ssm_norm, 'od_pool_w': od_pool_w,
            'od_pool_b': od_pool_b, 'od_pool_scale': od_pool_scale, 'od_w_out': od_w_out,
            'ffn_w_up': ffn_w_up, 'ffn_conv_w': ffn_conv_w, 'ffn_conv_b': ffn_conv_b, 'ffn_w_down': ffn_w_down,
            'ln1_g': ln1_g, 'ln1_b': ln1_b, 'ln2_g': ln2_g, 'ln2_b': ln2_b}

def first_block(x, ev_w_in, ev_b_in, ev_ml_norm, ev_w_out, od_w_in, od_conv_w, od_conv_b, od_dt_bias, od_a_log, od_d_skip, od_ssm_norm, od_pool_w, od_pool_b, od_pool_scale, od_w_out, ffn_w_up, ffn_conv_w, ffn_conv_b, ffn_w_down, ln1_g, ln1_b, ln2_g, ln2_b):
    for layer in range(DEPTH):
        j = layer // 2
        if layer % 2 == 0:
            y = even_mixer(x, ev_w_in[j], ev_b_in[j], ev_ml_norm[j], ev_w_out[j])
        else:
            y = odd_mixer(x, od_w_in[j], od_conv_w[j], od_conv_b[j], od_dt_bias[j], od_a_log[j], od_d_skip[j], od_ssm_norm[j], od_pool_w[j], od_pool_b[j], od_pool_scale[j], od_w_out[j])
        x = layer_norm(ALPHA * x + y, ln1_g[layer], ln1_b[layer])
        f = conv_ffn(x, ffn_w_up[layer], ffn_conv_w[layer], ffn_conv_b[layer], ffn_w_down[layer])
        x = layer_norm(ALPHA * x + f, ln2_g[layer], ln2_b[layer])
    return x


DEPTH_2 = 1

GDN_HEADS = 8
GDN_DK = 128
GDN_DV = 128
GDN_CONV = 4
GDN_CHUNK = 64
DSA_HEADS = 8
DSA_KV_HEADS = 2
DSA_DH = 128
IDX_HEADS = 8
IDX_DIM = 64
TOPK_MAX = 256
Q_BLOCK = 128
D_FF_2 = 2816
EPS = 1e-6

GDN_QK_W = GDN_HEADS * GDN_DK
GDN_V_W = GDN_HEADS * GDN_DV
GDN_CONV_CH = 2 * GDN_QK_W + GDN_V_W
DSA_Q_W = DSA_HEADS * DSA_DH
DSA_KV_W = DSA_KV_HEADS * DSA_DH
IDX_Q_W = IDX_HEADS * IDX_DIM
IN_SPLITS = (GDN_CONV_CH, GDN_V_W, GDN_HEADS, GDN_HEADS,
             DSA_Q_W, DSA_KV_W, DSA_KV_W, IDX_Q_W, IDX_DIM, IDX_HEADS,
             D_MODEL, D_MODEL)
N_IN = GDN_CONV_CH + GDN_V_W + 2 * GDN_HEADS + DSA_Q_W + 2 * DSA_KV_W + IDX_Q_W + IDX_DIM + IDX_HEADS + 2 * D_MODEL


def rmsnorm(x, g):
    xf = x.astype(jnp.float32)
    y = xf * lax.rsqrt(jnp.mean(xf * xf, axis=-1, keepdims=True) + EPS)
    return (y * g.astype(jnp.float32)).astype(x.dtype)

def layernorm_nobias(x, g):
    xf = x.astype(jnp.float32)
    xc = xf - jnp.mean(xf, axis=-1, keepdims=True)
    y = xc * lax.rsqrt(jnp.mean(xc * xc, axis=-1, keepdims=True) + EPS)
    return (y * g.astype(jnp.float32)).astype(x.dtype)

def l2norm(x):
    xf = x.astype(jnp.float32)
    return xf * lax.rsqrt(jnp.sum(xf * xf, axis=-1, keepdims=True) + EPS)

def causal_dwconv_2(x, w):
    width, ch = w.shape
    return lax.conv_general_dilated(
        x, w[:, None, :].astype(x.dtype), window_strides=(1,),
        padding=[(width - 1, 0)], dimension_numbers=("NWC", "WIO", "NWC"),
        feature_group_count=ch)

def gated_delta_rule_chunked(q, k, v, g, beta):
    B, S, H, dk = q.shape
    dv = v.shape[-1]
    C = GDN_CHUNK
    N = S // C
    q = q * (dk ** -0.5)

    def chunks(t):
        return jnp.swapaxes(t.reshape((B, N, C) + t.shape[2:]), 2, 3)

    qc, kc, vc, gc, bc = chunks(q), chunks(k), chunks(v), chunks(g), chunks(beta)
    G = jnp.cumsum(gc, axis=-1)
    tri = jnp.tril(jnp.ones((C, C), dtype=bool))
    strict = jnp.tril(jnp.ones((C, C), dtype=bool), -1)
    gamma = jnp.exp(jnp.where(tri, G[..., :, None] - G[..., None, :], -jnp.inf))
    kb = kc * bc[..., None]
    A = jnp.where(strict, jnp.einsum("bnhid,bnhjd->bnhij", kb, kc) * gamma, 0.0)
    eye = jnp.eye(C, dtype=jnp.float32)
    T = lax.linalg.triangular_solve(A + eye, jnp.broadcast_to(eye, A.shape),
                                    left_side=True, lower=True)
    eG = jnp.exp(G)[..., None]
    u = jnp.einsum("bnhij,bnhje->bnhie", T, vc * bc[..., None])
    w = jnp.einsum("bnhij,bnhjd->bnhid", T, kb * eG)
    qg = qc * eG
    kd = kc * jnp.exp(G[..., -1:] - G)[..., None]
    att = jnp.einsum("bnhid,bnhjd->bnhij", qc, kc) * gamma
    dlast = jnp.exp(G[..., -1])

    def step(state, inp):
        u_i, w_i, qg_i, kd_i, att_i, dl_i = inp
        v_new = u_i - jnp.einsum("bhcd,bhde->bhce", w_i, state)
        o = jnp.einsum("bhcd,bhde->bhce", qg_i, state) + jnp.einsum("bhij,bhje->bhie", att_i, v_new)
        state = state * dl_i[..., None, None] + jnp.einsum("bhcd,bhce->bhde", kd_i, v_new)
        return state, o

    xs = (jnp.swapaxes(u, 0, 1), jnp.swapaxes(w, 0, 1), jnp.swapaxes(qg, 0, 1),
          jnp.swapaxes(kd, 0, 1), jnp.swapaxes(att, 0, 1), jnp.swapaxes(dlast, 0, 1))
    s0 = jnp.zeros((B, H, dk, dv), jnp.float32)
    _, o = lax.scan(step, s0, xs)
    return jnp.transpose(o, (1, 0, 3, 2, 4)).reshape(B, S, H, dv)

def dsa_sparse_attention(q, k, v, iq, ik, iw):
    B, S, Hq, dh = q.shape
    L, Hkv = k.shape[1], k.shape[2]
    k_top = min(TOPK_MAX, L // 4)
    rep = Hq // Hkv
    nb = S // Q_BLOCK
    key_pos = jnp.arange(L, dtype=jnp.int32)
    starts = jnp.arange(nb, dtype=jnp.int32) * Q_BLOCK
    iw = iw * ((IDX_HEADS ** -0.5) * (IDX_DIM ** -0.5))

    def blocks(t):
        return jnp.swapaxes(t.reshape((B, nb, Q_BLOCK) + t.shape[2:]), 0, 1)

    def one_block(args):
        q_b, iq_b, iw_b, start = args
        t_pos = start + jnp.arange(Q_BLOCK, dtype=jnp.int32)
        causal = key_pos[None, :] <= t_pos[:, None]
        rel = jax.nn.relu(jnp.einsum("bqhd,bsd->bqhs", iq_b, ik))
        score = jnp.einsum("bqh,bqhs->bqs", iw_b, rel).astype(jnp.float32)
        score = jnp.where(causal[None], score, -jnp.inf)
        _, idx = lax.top_k(score, k_top)
        valid = idx <= t_pos[None, :, None]
        k_sel = jax.vmap(lambda kb, ib: kb[ib])(k, idx)
        v_sel = jax.vmap(lambda vb, ib: vb[ib])(v, idx)
        qg = q_b.reshape(B, Q_BLOCK, Hkv, rep, dh)
        logits = jnp.einsum("bqgrd,bqkgd->bqgrk", qg, k_sel).astype(jnp.float32) * (dh ** -0.5)
        logits = jnp.where(valid[:, :, None, None, :], logits, -jnp.inf)
        p = jax.nn.softmax(logits, axis=-1).astype(v.dtype)
        o = jnp.einsum("bqgrk,bqkgd->bqgrd", p, v_sel)
        return o.reshape(B, Q_BLOCK, Hq * dh)

    out = lax.map(one_block, (blocks(q), blocks(iq), blocks(iw), starts))
    return jnp.swapaxes(out, 0, 1).reshape(B, S, Hq * dh)

def second_inputs(seed: int = 0) -> dict:
    key = jax.random.key(seed)
    ks = jax.random.split(key, 16)
    f32 = jnp.float32

    def nrm(k, shape, scale):
        return jax.random.normal(k, shape, f32) * scale

    x = nrm(ks[0], (BATCH, SEQ, D_MODEL), 1.0)
    norm1_g = 1.0 + nrm(ks[1], (DEPTH_2, D_MODEL), 0.02)
    w_in = nrm(ks[2], (DEPTH_2, D_MODEL, N_IN), D_MODEL ** -0.5)
    gdn_conv_w = nrm(ks[3], (DEPTH_2, GDN_CONV, GDN_CONV_CH), GDN_CONV ** -0.5)
    gdn_a_log = jnp.log(jax.random.uniform(ks[4], (DEPTH_2, GDN_HEADS), f32, 1.0, 16.0))
    dt = jnp.exp(jax.random.uniform(ks[5], (DEPTH_2, GDN_HEADS), f32, math.log(1e-3), math.log(1e-1)))
    gdn_dt_bias = dt + jnp.log(-jnp.expm1(-dt))
    gdn_norm_g = 1.0 + nrm(ks[6], (DEPTH_2, GDN_DV), 0.02)
    idx_k_norm_g = 1.0 + nrm(ks[7], (DEPTH_2, IDX_DIM), 0.02)
    branch_gate_b = nrm(ks[8], (DEPTH_2, 2 * D_MODEL), 0.02)
    w_out = nrm(ks[9], (DEPTH_2, D_MODEL, D_MODEL), D_MODEL ** -0.5)
    norm2_g = 1.0 + nrm(ks[10], (DEPTH_2, D_MODEL), 0.02)
    ffn_w_up = nrm(ks[11], (DEPTH_2, D_MODEL, 2 * D_FF_2), D_MODEL ** -0.5)
    ffn_conv_w = nrm(ks[12], (DEPTH_2, FFN_CONV, 2 * D_FF_2), FFN_CONV ** -0.5)
    ffn_conv_b = nrm(ks[13], (DEPTH_2, 2 * D_FF_2), 0.02)
    ffn_w_down = nrm(ks[14], (DEPTH_2, D_FF_2, D_MODEL), D_FF_2 ** -0.5)
    final_g = 1.0 + nrm(ks[15], (D_MODEL,), 0.02)
    return {"x": x, "norm1_g": norm1_g, "w_in": w_in, "gdn_conv_w": gdn_conv_w,
            "gdn_a_log": gdn_a_log, "gdn_dt_bias": gdn_dt_bias, "gdn_norm_g": gdn_norm_g,
            "idx_k_norm_g": idx_k_norm_g, "branch_gate_b": branch_gate_b, "w_out": w_out,
            "norm2_g": norm2_g, "ffn_w_up": ffn_w_up, "ffn_conv_w": ffn_conv_w,
            "ffn_conv_b": ffn_conv_b, "ffn_w_down": ffn_w_down, "final_g": final_g}

def second_block(x, norm1_g, w_in, gdn_conv_w, gdn_a_log, gdn_dt_bias, gdn_norm_g,
              idx_k_norm_g, branch_gate_b, w_out, norm2_g, ffn_w_up, ffn_conv_w,
              ffn_conv_b, ffn_w_down, final_g):
    B, S, _ = x.shape
    offsets = [int(o) for o in np.cumsum(IN_SPLITS)[:-1]]
    h = x
    for l in range(DEPTH_2):
        u = rmsnorm(h, norm1_g[l])
        proj = jnp.einsum("bsd,de->bse", u, w_in[l])
        (g_qkv, g_z, g_a, g_b, d_q, d_k, d_v, i_q, i_k, i_w, gate_a, gate_b) = jnp.split(proj, offsets, axis=-1)

        qkv = jax.nn.silu(causal_dwconv_2(g_qkv, gdn_conv_w[l]))
        gq, gk, gv = jnp.split(qkv, [GDN_QK_W, 2 * GDN_QK_W], axis=-1)
        gq = l2norm(gq.reshape(B, S, GDN_HEADS, GDN_DK))
        gk = l2norm(gk.reshape(B, S, GDN_HEADS, GDN_DK))
        gv = gv.reshape(B, S, GDN_HEADS, GDN_DV).astype(jnp.float32)
        beta = jax.nn.sigmoid(g_b.astype(jnp.float32))
        logdecay = -jnp.exp(gdn_a_log[l].astype(jnp.float32)) * jax.nn.softplus(
            g_a.astype(jnp.float32) + gdn_dt_bias[l].astype(jnp.float32))
        o_gdn = gated_delta_rule_chunked(gq, gk, gv, logdecay, beta)
        z = g_z.reshape(B, S, GDN_HEADS, GDN_DV).astype(jnp.float32)
        o_gdn = (rmsnorm(o_gdn, gdn_norm_g[l]) * jax.nn.silu(z)).reshape(B, S, GDN_V_W).astype(x.dtype)

        o_dsa = dsa_sparse_attention(
            d_q.reshape(B, S, DSA_HEADS, DSA_DH),
            d_k.reshape(B, S, DSA_KV_HEADS, DSA_DH),
            d_v.reshape(B, S, DSA_KV_HEADS, DSA_DH),
            i_q.reshape(B, S, IDX_HEADS, IDX_DIM),
            layernorm_nobias(i_k, idx_k_norm_g[l]),
            i_w)

        gb = branch_gate_b[l]
        mixed = (jax.nn.sigmoid(gate_a + gb[:D_MODEL]) * o_gdn
                 + jax.nn.sigmoid(gate_b + gb[D_MODEL:]) * o_dsa)
        h = h + jnp.einsum("bse,ed->bsd", mixed, w_out[l])

        hn = rmsnorm(h, norm2_g[l])
        up = causal_dwconv_2(jnp.einsum("bsd,df->bsf", hn, ffn_w_up[l]), ffn_conv_w[l]) + ffn_conv_b[l]
        f_gate, f_val = jnp.split(up, [D_FF_2], axis=-1)
        h = h + jnp.einsum("bsf,fd->bsd", jax.nn.silu(f_gate) * f_val, ffn_w_down[l])
    return rmsnorm(h, final_g)


def setup_inputs(seed=0):
    out = dict(first_inputs(seed))
    for name, value in second_inputs(seed + 1).items():
        if name != "x":
            out[name + "_2"] = value
    return out


def reference(
    x, ev_w_in, ev_b_in, ev_ml_norm, ev_w_out, od_w_in, od_conv_w, od_conv_b, od_dt_bias,
    od_a_log, od_d_skip, od_ssm_norm, od_pool_w, od_pool_b, od_pool_scale, od_w_out, ffn_w_up,
    ffn_conv_w, ffn_conv_b, ffn_w_down, ln1_g, ln1_b, ln2_g, ln2_b, norm1_g_2, w_in_2,
    gdn_conv_w_2, gdn_a_log_2, gdn_dt_bias_2, gdn_norm_g_2, idx_k_norm_g_2, branch_gate_b_2,
    w_out_2, norm2_g_2, ffn_w_up_2, ffn_conv_w_2, ffn_conv_b_2, ffn_w_down_2, final_g_2,
):
    x = first_block(
        x, ev_w_in, ev_b_in, ev_ml_norm, ev_w_out, od_w_in, od_conv_w, od_conv_b, od_dt_bias,
        od_a_log, od_d_skip, od_ssm_norm, od_pool_w, od_pool_b, od_pool_scale, od_w_out,
        ffn_w_up, ffn_conv_w, ffn_conv_b, ffn_w_down, ln1_g, ln1_b, ln2_g, ln2_b,
    )
    return second_block(
        x, norm1_g_2, w_in_2, gdn_conv_w_2, gdn_a_log_2, gdn_dt_bias_2, gdn_norm_g_2,
        idx_k_norm_g_2, branch_gate_b_2, w_out_2, norm2_g_2, ffn_w_up_2, ffn_conv_w_2,
        ffn_conv_b_2, ffn_w_down_2, final_g_2,
    )


_drawn_inputs = setup_inputs


def setup_inputs(seed=0):
    import zlib

    import numpy as np

    out = dict(_drawn_inputs(seed))
    spreads = {}
    factors = {'ev_ml_norm': 8.0,
     'od_conv_b': 5.307,
     'od_d_skip': 7.016,
     'od_ssm_norm': 6.774,
     'od_pool_b': 6.859,
     'ffn_conv_b': 4.346,
     'norm1_g_2': 3.493,
     'gdn_norm_g_2': 7.94,
     'idx_k_norm_g_2': 6.529,
     'branch_gate_b_2': 8.0,
     'norm2_g_2': 11.831,
     'ffn_conv_b_2': 11.519,
     'final_g_2': 8.267}
    for name, (base, spread) in spreads.items():
        noise = np.random.default_rng([zlib.crc32(name.encode()), seed]).standard_normal(out[name].shape)
        drawn = base * np.exp(spread * noise) if base else spread * noise
        out[name] = __import__('jax').numpy.asarray(drawn.astype(out[name].dtype))
    for name, factor in factors.items():
        out[name] = (out[name] * factor).astype(out[name].dtype)
    return out
```

```python
from contextlib import ExitStack

import numpy as np
import concourse.bass as bass
from concourse import mybir

ALU = mybir.AluOpType
ACT = mybir.ActivationFunctionType
F32 = mybir.dt.float32
BF16 = mybir.dt.bfloat16
AX_X = mybir.AxisListType.X

P = 128
SEQ = 512
TILES = SEQ // P
DM = 1024
DC = DM // P
D_FF = 2816
FC = D_FF // P
HALF = 512
DEPTH = 2
ALPHA = (2.0 * DEPTH) ** 0.25
LN_EPS = 1e-5
RMS_EPS = 1e-6
NEG = -1e30
TAKEN = -3e38
TOPK = min(256, SEQ // 4)
RING = 4
ML_HEADS, FOX_HEADS, SSM_HEADS, GDN_HEADS, DSA_HEADS, IDX_HEADS = 4, 8, 8, 8, 8, 8
POOL_WINDOWS = (2, 4, 8, 16)
LEVELS = 7

RUNS = [
    ("small0", 1), ("mq", 4), ("mk", 4), ("mv", 4), ("fq", 4), ("fk", 4), ("fv", 4), ("mo", 4), ("out0", 8),
    ("up0", 2 * FC), ("down0", FC),
    ("small1", 1), ("xbc", 8), ("pool", 4), ("z1", 4), ("out1", 8),
    ("up1", 2 * FC), ("down1", FC),
    ("small2", 1), ("ik", 1), ("iq", 4), ("dq", 8), ("dk", 2), ("dv", 2), ("gateb", 8),
    ("gqkv", 24), ("z2", 8), ("gatea", 8), ("out2", 8),
    ("up2", 2 * FC), ("down2", FC),
]
FIRST, _u = {}, 0
for _name, _n in RUNS:
    FIRST[_name] = _u
    _u += _n
COUNT = dict(RUNS)
UNITS = _u

COLS = [
    ("b_small0", 1), ("b_mq", 4), ("b_mk", 4), ("b_fq", 4), ("b_fk", 4), ("b_mo", 4), ("ml_norm", 4),
    ("ln1_g0", 8), ("ln1_b0", 8), ("ln2_g0", 8), ("ln2_b0", 8), ("ln1_g1", 8), ("ln1_b1", 8), ("ln2_g1", 8), ("ln2_b1", 8),
    ("dt_bias", 1), ("a_log", 1), ("xbc_conv", 8 * 5), ("d_skip", 4), ("ssm_norm", 4), ("pool_b", 4), ("pool_s", 4),
    ("ffn0", 2 * FC * 4), ("ffn1", 2 * FC * 4), ("ffn2", 2 * FC * 4),
    ("norm1", 8), ("norm2", 8), ("final", 8), ("g_dt_bias", 1), ("g_a_log", 1), ("gqkv_conv", 24 * 4),
    ("gdn_norm", 1), ("ik_norm", 1), ("gate_b", 16),
]
COL, _c = {}, 0
for _name, _n in COLS:
    COL[_name] = _c
    _c += _n
NCOL = _c

K_ID, K_MT, K_MQ, K_LEV, K_CNT, K_SEL = 0, P, 2 * P, 3 * P, (3 + LEVELS) * P, (3 + LEVELS) * P + 64
NCONST = K_SEL + 8 * P


class Counts:

    def __init__(self, marks):
        self.marks, self.n = marks, 0

    def next(self, *key):
        self.n += 1
        if key:
            self.marks[key] = self.n
        return 1

    def mark(self, *key):
        self.marks[key] = self.n

    def find(self, *key):
        return self.marks.get(key, 1)


def build_program(nc, stream, params, brow, poolw, consts, xt, out, marks, last_stage):
    with ExitStack() as ctx:
        def sb(name, shape, dt=F32):
            return ctx.enter_context(nc.sbuf_tensor(name, shape, dt))

        def sem(name):
            return ctx.enter_context(nc.semaphore(name))

        arena = sb("arena", [P, 80, SEQ])
        ring = sb("ring", [P, RING, 8 * P])
        par = sb("par", [P, NCOL])
        con = sb("con", [P, NCONST])
        idb = sb("idb", [P, P], BF16)
        mtb = sb("mtb", [P, P], BF16)
        mqb = sb("mqb", [P, P], BF16)
        ones = sb("ones", [P, SEQ])
        inv = {n: sb(f"inv{n}", [P, P]) for n in (128, 512, 1024)}
        small = sb("small", [P, 256])
        pw = sb("pw", [P, TILES, P])
        bank = [ctx.enter_context(nc.psum_tensor(f"bank{b}", [P, SEQ], F32)) for b in range(8)]

        ident = con[:, K_ID:K_ID + P]
        ident8 = con[0:8, K_ID:K_ID + 8]

        def sel(h, n=8):
            return con[0:n, K_SEL + h * P:K_SEL + (h + 1) * P]

        def col(name, j=0, p0=0, p1=P):
            return par[p0:p1, COL[name] + j:COL[name] + j + 1]

        X, U, MIX = arena[:, 0:8, :], arena[:, 8:16, :], arena[:, 16:24, :]

        in_sem = sem("in_sem")
        ring_sem = [sem(f"ring_loaded{s}") for s in range(RING)]
        units_done = sem("units_done")
        tensor_out, scalar_out, vector_out, gpsimd_out = sem("tensor_out"), sem("scalar_out"), sem("vector_out"), sem("gpsimd_out")
        tensor_at, scalar_at, vector_at, gpsimd_at = (Counts(marks.setdefault(n, {})) for n in ("tensor", "scalar", "vector", "gpsimd"))
        SCALAR, VECTOR = (scalar_out, scalar_at), (vector_out, vector_at)
        acc_done, tap_done, conv_done = sem("ffn_acc_done"), sem("ffn_tap_done"), sem("ffn_conv_done")
        gate_done, hid_done = sem("ffn_gate_done"), sem("ffn_hidden_done")
        out_sem = sem("out_sem")
        nloads = 5

        ctx.enter_context(nc.allow_low_precision(reason="0/1 and mask constants"))
        block = ctx.enter_context(nc.Block())
        last_unit = UNITS if last_stage is None else FIRST[last_stage] + COUNT[last_stage]

        def on(stage):
            return FIRST[stage] < last_unit

        @block.sync
        def _(sp):
            sp.dma_start(X, xt).then_inc(in_sem, 16)
            sp.dma_start(par[:], params).then_inc(in_sem, 16)
            sp.dma_start(con[:], consts).then_inc(in_sem, 16)
            sp.dma_start(pw[:], poolw).then_inc(in_sem, 16)
            sp.dma_start(arena[0:1, 78:80, :], brow.rearrange("a (c n) -> a c n", c=2)).then_inc(in_sem, 16)
            for s in range(RING):
                sp.dma_start(ring[:, s, :], stream[s]).then_inc(ring_sem[s], 16)
            rounds = last_unit // RING
            with sp.Fori(1, rounds) as i:
                for s in range(RING):
                    sp.wait_ge(units_done, (i - 1) * RING + s + 1)
                    sp.dma_start(ring[:, s, :], stream[i * RING + s]).then_inc(ring_sem[s], 16)
            for u in range(rounds * RING, last_unit):
                sp.wait_ge(units_done, u - RING + 1)
                sp.dma_start(ring[:, u % RING, :], stream[u]).then_inc(ring_sem[u % RING], 16)

        def stage_end(eng, mine, name):
            mine.mark("stage", name)
            eng.wait_ge(tensor_out, tensor_at.find("stage", name))
            eng.wait_ge(scalar_out, scalar_at.find("stage", name))
            eng.wait_ge(vector_out, vector_at.find("stage", name))
            eng.wait_ge(gpsimd_out, gpsimd_at.find("stage", name))

        mq, mk, mv = arena[:, 24:28, :], arena[:, 28:32, :], arena[:, 32:36, :]
        fq, fk = arena[:, 36:40, :], arena[:, 40:48, :]
        fv = arena[:, 48:56, :].rearrange("p (t a) n -> p t (a n)", a=2).rearrange("p t (h d) -> p t h d", h=FOX_HEADS)
        row = {j: arena[:, j, :] for j in range(56, 66)}
        RSTD = arena[:, 77, :]
        bias_v = arena[0:1, 78:80, :]
        hid, acc, sg = arena[:, 24:24 + FC, :], arena[:, 46:50, :], arena[:, 50:52, :]
        xbc, ys = arena[:, 24:32, :], arena[:, 32:36, :]
        xpad = arena[:, 36:44, :].rearrange("p (t a) n -> p t (a n)", a=2).rearrange("p t (h d) -> p t h d", h=SSM_HEADS)
        pbuf = [arena[:, 44 + 2 * g:46 + 2 * g, :].rearrange("p a n -> p (a n)") for g in range(6)]
        iq, ikp, dq, dk = arena[:, 24:28, :], arena[:, 28:30, :], arena[:, 30:38, :], arena[:, 38:40, :]
        dv = arena[:, 40:42, :].rearrange("p a n -> p (a n)").rearrange("p (t n) -> p t n", t=TILES)
        madd = arena[:, 42:44, :].rearrange("p a n -> p (a n)").bitcast(BF16).rearrange("p (t n) -> p t n", t=TILES)
        score = arena[:, 44:48, :]
        gq, gk, gv, go = arena[:, 24:32, :], arena[:, 32:40, :], arena[:, 40:48, :], arena[:, 48:56, :]
        GW = {n: arena[:, 65 + i, :].rearrange("p (h n) -> p h n", h=4) for i, n in enumerate(
            ["gam", "eg", "kb", "at", "att", "qg", "u", "t", "lt", "xs", "kbe", "kd", "vb", "nw", "vn"])}
        state = arena[:, 56:58, :].rearrange("p g (h n) -> p g h n", h=4)

        def tile(b):
            return bank[b][:, :].rearrange("p (h n) -> p h n", h=4)

        ml_steps = [dict(j=j, sel=sel(h, 4), rows=row[64][0:4, j * P:], bias=small[:, j * 4 + h:j * 4 + h + 1], k=mk[:, h, j * P:(j + 1) * P],
                         q=mq[:, h, j * P:], v=mv[:, j, h * P:(h + 1) * P], num=0, den=1, first=j == 0, last=j == TILES - 1, out=h)
                    for h in range(ML_HEADS) for j in range(TILES)]
        ssm_steps = [dict(j=j, sel=sel(h), rows=row[60 + j][0:8, j * P:], bias=small[:, 32 + j * 8 + h:33 + j * 8 + h], k=xbc[:, 4 + h // 4, j * P:(j + 1) * P],
                          q=xbc[:, 6 + h // 4, j * P:], v=xpad[:, j, h, :], num=h // 2 % 2, den=None, first=j == 0 and h % 2 == 0,
                          last=j == TILES - 1 and h % 2 == 1, out=h // 2)
                     for h in range(SSM_HEADS) for j in range(TILES)]
        fox_steps = [dict(w=(i + 1) * P, q=fq[:, h // 2, i * P:(i + 1) * P], k=fk[:, h, 0:(i + 1) * P],
                          more=[(sel(h), row[61][0:8, 0:(i + 1) * P], 0, (i + 1) * P), (idb[:], mqb[:], i * P, (i + 1) * P)],
                          v=[fv[:, j, h, :] for j in range(i + 1)], ob=c % 2, oc=i * P, start=h % 2 == 0, stop=h % 2 == 1,
                          claim=i == 0 and h % 2 == 0, last=i == TILES - 1 and h % 2 == 1, o=c, dst=4 + c)
                     for c in range(4) for i in range(TILES) for h in (2 * c, 2 * c + 1)]
        dsa_steps = [dict(w=(i + 1) * P, q=dq[:, h, i * P:(i + 1) * P], k=dk[:, h // 4, 0:(i + 1) * P],
                          more=[(idb[:], madd[:, i, 0:(i + 1) * P] if i else mqb[:], 0, (i + 1) * P)],
                          v=[dv[:, j, (h // 4) * P:(h // 4 + 1) * P] for j in range(i + 1)], ob=h % 2, oc=i * P, start=True, stop=True,
                          claim=i == 0, last=i == TILES - 1, o=h, dst=h)
                     for h in range(DSA_HEADS) for i in range(TILES)]
        for steps in (fox_steps, dsa_steps):
            for n, st in enumerate(steps):
                st["ps"], st["ts"] = 66 + n % 4, 70 + n % 3

        @block.tensor
        def _(pe):
            reader = {}

            def claim(b):
                if b in reader:
                    (semaphore, at), key = reader[b]
                    pe.wait_ge(semaphore, at.find(*key))

            def unit_arrived(u):
                pe.wait_ge(ring_sem[u % RING], 16 * (u // RING + 1))

            def run_units(name, rhs, prog):
                for j in range(COUNT[name]):
                    u = FIRST[name] + j
                    claim(u % RING)
                    unit_arrived(u)
                    for k in range(DC):
                        m = nc.tensor.matmul(bank[u % RING][:], ring[:, u % RING, k * P:(k + 1) * P], rhs[:, k, :], start=k == 0, stop=k == DC - 1)
                    m.then_inc(units_done, 1)
                    reader[u % RING] = (prog, ("read", name, j))

            def run_moving(name, n, src, bias_row):
                kk = 8 * P // n
                for tt in range(TILES):
                    claim(tt)
                    if bias_row is not None:
                        nc.tensor.matmul(bank[tt][:, 0:n], ones[0:1, 0:P], bias_row, start=True, stop=False)
                for j in range(COUNT[name]):
                    u = FIRST[name] + j
                    unit_arrived(u)
                    for tt in range(TILES):
                        for q in range(kk):
                            k = j * kk + q
                            m = nc.tensor.matmul(bank[tt][:, 0:n], src[:, k, tt * P:(tt + 1) * P], ring[:, u % RING, q * n:(q + 1) * n],
                                                 start=(k == 0 and bias_row is None), stop=k == DC - 1)
                    m.then_inc(units_done, 1)
                for tt in range(TILES):
                    reader[tt] = (VECTOR, ("read", name, tt))

            def norm(name, chunks, n, xs, sq, mean):
                if mean:
                    claim(6)
                    for k in range(chunks):
                        pe.wait_ge(vector_out, vector_at.find(name, "x", k))
                        m = nc.tensor.matmul(bank[6][:], inv[n][:], xs[:, k, :], start=k == 0, stop=k == chunks - 1)
                    m.then_inc(tensor_out, tensor_at.next(name, "mean"))
                    reader[6] = (VECTOR, (name, "centred"))
                claim(7)
                for k in range(chunks):
                    pe.wait_ge(scalar_out, scalar_at.find(name, "sq", k))
                    m = nc.tensor.matmul(bank[7][:], inv[n][:], sq[:, k, :], start=k == 0, stop=k == chunks - 1)
                m.then_inc(tensor_out, tensor_at.next(name, "ms"))
                reader[7] = (SCALAR, (name, "root"))

            def item_norms(name, items, mat, xs, sqs, mean):
                for k in range(items + 1):
                    if k < items and mean:
                        claim(6)
                        nc_m = nc.tensor.matmul(bank[6][:], mat[:, 0:P], xs(k), start=True, stop=True)
                        nc_m.then_inc(tensor_out, tensor_at.next(name, "mean", k))
                        reader[6] = (VECTOR, (name, "centred", k))
                    if k >= 1:
                        claim(7)
                        pe.wait_ge(scalar_out, scalar_at.find(name, "sq", k - 1))
                        nc_m = nc.tensor.matmul(bank[7][:], mat[:, 0:P], sqs(k - 1), start=True, stop=True)
                        nc_m.then_inc(tensor_out, tensor_at.next(name, "ms", k - 1))
                        reader[7] = (SCALAR, (name, "root", k - 1))

            def attention(name, steps):
                N = len(steps)
                for n in range(N + 3):
                    if n < N:
                        st, b = steps[n], 2 + n % 3
                        claim(b)
                        W = st["w"]
                        nc.tensor.matmul(bank[b][:, 0:W], st["q"], st["k"], start=True, stop=False)
                        for x, (l, r, c0, c1) in enumerate(st["more"]):
                            m = nc.tensor.matmul(bank[b][:, c0:c1], l, r, start=False, stop=x == len(st["more"]) - 1)
                        m.then_inc(tensor_out, tensor_at.next(name, "logits", n))
                        reader[b] = (SCALAR, (name, "exp", n))
                    if 2 <= n < N + 2:
                        k, st = n - 2, steps[n - 2]
                        b = 5 + k % 2
                        claim(b)
                        pe.wait_ge(vector_out, vector_at.find(name, "p", k))
                        for j in range(st["w"] // P):
                            m = nc.tensor.transpose(bank[b][:, j * P:(j + 1) * P], arena[:, st["ps"], j * P:(j + 1) * P], ident)
                        m.then_inc(tensor_out, tensor_at.next(name, "t", k))
                        reader[b] = (SCALAR, (name, "pt", k))
                    if n >= 3:
                        k, st = n - 3, steps[n - 3]
                        b = st["ob"]
                        if st["claim"]:
                            claim(b)
                        pe.wait_ge(scalar_out, scalar_at.find(name, "pt", k))
                        J = st["w"] // P
                        for j in range(J):
                            m = nc.tensor.matmul(bank[b][:, st["oc"]:st["oc"] + P], st["v"][j], arena[:, st["ts"], j * P:(j + 1) * P],
                                                 start=st["start"] and j == 0, stop=st["stop"] and j == J - 1)
                        m.then_inc(tensor_out, tensor_at.next(name, "pv", k))
                        if st["last"]:
                            reader[b] = (SCALAR, (name, "o", st["o"]))

            def decayed(name, steps, extra=None):
                N = len(steps)
                for n in range(N + 2):
                    if n < N:
                        st = steps[n]
                        c0 = st["j"] * P
                        W = SEQ - c0
                        b = 2 + n % 2
                        claim(b)
                        nc.tensor.matmul(bank[b][:, 0:W], st["sel"], st["rows"], start=True, stop=False)
                        m = nc.tensor.matmul(bank[b][:, 0:P], idb[:], mtb[:], start=False, stop=True)
                        m.then_inc(tensor_out, tensor_at.next(name, "e", n))
                        reader[b] = (SCALAR, (name, "w", n))
                        b = 4 + n % 2
                        claim(b)
                        m = nc.tensor.matmul(bank[b][:, 0:W], st["k"], st["q"], start=True, stop=True)
                        m.then_inc(tensor_out, tensor_at.next(name, "s", n))
                        reader[b] = (VECTOR, (name, "p", n))
                        if st["first"] and extra is not None:
                            extra(st)
                    if n >= 2:
                        k, st = n - 2, steps[n - 2]
                        c0 = st["j"] * P
                        if st["first"]:
                            claim(st["num"])
                            if st["den"] is not None:
                                claim(st["den"])
                        pe.wait_ge(vector_out, vector_at.find(name, "p", k))
                        p = arena[:, 69 + k % 3, 0:SEQ - c0]
                        m = nc.tensor.matmul(bank[st["num"]][:, c0:], st["v"], p, start=st["first"], stop=st["last"])
                        if st["den"] is not None:
                            m = nc.tensor.matmul(bank[st["den"]][:, c0:], ones[:, 0:P], p, start=st["first"], stop=st["last"])
                        m.then_inc(tensor_out, tensor_at.next(name, "pv", k))
                        if st["last"]:
                            reader[st["num"]] = (VECTOR, (name, "fin", st["out"]))
                            if st["den"] is not None:
                                reader[st["den"]] = (VECTOR, (name, "fin", st["out"]))

            def ffn(l, src):
                up, down = f"up{l}", f"down{l}"
                u0 = FIRST[up]
                for s in range(RING):
                    claim(s)
                with pe.Fori(0, 2 * FC // RING) as i:
                    for s in range(RING):
                        b = (u0 + s) % RING
                        pe.wait_ge(ring_sem[b], 16 * i + 16 * ((u0 + s) // RING + 1))
                        pe.wait_ge(conv_done, RING * i + l * 2 * FC + s + 1)
                        for k in range(DC):
                            m = nc.tensor.matmul(bank[b][:], ring[:, b, k * P:(k + 1) * P], src[:, k, :], start=k == 0, stop=k == DC - 1)
                        m.then_inc(units_done, 1)
                pe.wait_ge(hid_done, 2 + (l + 1) * FC)
                for b in range(4, 8):
                    claim(b)
                d0 = FIRST[down]

                def unit(u, wait, rhs, start, stop):
                    pe.wait_ge(ring_sem[u % RING], wait)
                    for n in range(DC):
                        m = nc.tensor.matmul(bank[n][:], ring[:, u % RING, n * P:(n + 1) * P], rhs, start=start, stop=stop)
                    m.then_inc(units_done, 1)

                unit(d0, 16 * (d0 // RING + 1), hid[:, 0, :], True, False)
                with pe.Fori(0, (FC - 2) // RING) as i:
                    for s in range(RING):
                        u = d0 + 1 + s
                        unit(u, 16 * i + 16 * (u // RING + 1), hid[:, bass.ds(RING * i + 1 + s, 1), :].rearrange("p a n -> p (a n)"), False, False)
                u = d0 + FC - 1
                unit(u, 16 * (u // RING + 1), hid[:, FC - 1, :], False, True)
                for b in range(8):
                    reader[b] = (VECTOR, ("read", down, b))

            def columns(name, parts, n):
                claim(4)
                pe.wait_ge(vector_out, vector_at.find(name, "rows"))
                pe.wait_ge(scalar_out, scalar_at.find(name, "rows"))
                for c0, src in parts:
                    m = nc.tensor.matmul(bank[4][:, c0:c0 + n], src, con[0:n, K_ID:K_ID + n], start=True, stop=True)
                m.then_inc(tensor_out, tensor_at.next(name, "cols"))
                reader[4] = (VECTOR, (name, "cols"))

            pe.wait_ge(in_sem, 16 * nloads)
            pe.wait_ge(gpsimd_out, gpsimd_at.find("setup"))
            pe.wait_ge(vector_out, vector_at.find("setup"))
            run_units("small0", X, SCALAR)
            run_units("mq", X, VECTOR)
            run_units("mk", X, SCALAR)
            run_moving("mv", HALF, X, bias_v[:, 0, :])
            run_units("fq", X, VECTOR)
            run_units("fk", X, SCALAR)
            run_moving("fv", HALF, X, bias_v[:, 1, :])
            columns("gate0", [(tt * 4, row[62][0:4, tt * P:(tt + 1) * P]) for tt in range(TILES)], 4)
            stage_end(pe, tensor_at, "in0")

            def minus_m(st):
                claim(6)
                m = nc.tensor.matmul(bank[6][:], st["sel"], row[65][0:4, :], start=True, stop=True)
                m.then_inc(tensor_out, tensor_at.next("ml", "m", st["out"]))
                reader[6] = (SCALAR, ("ml", "em", st["out"]))

            decayed("ml", ml_steps, minus_m)
            item_norms("hn", 4, inv[128], lambda k: MIX[:, k, :], lambda k: arena[:, 72 + k % 2, :], True)
            stage_end(pe, tensor_at, "ml")
            attention("fox", fox_steps)
            run_units("mo", X, SCALAR)
            stage_end(pe, tensor_at, "mix0")
            run_units("out0", MIX, VECTOR)
            norm("ln1_0", DC, 1024, X, MIX, True)
            stage_end(pe, tensor_at, "ln1_0")
            if on("up0"):
                ffn(0, X)
                norm("ln2_0", DC, 1024, X, MIX, True)
                stage_end(pe, tensor_at, "ln2_0")
            if on("small1"):
                run_units("small1", X, SCALAR)
                run_units("xbc", X, VECTOR)
                run_units("pool", X, SCALAR)
                columns("gate1", [(tt * 8, row[58][0:8, tt * P:(tt + 1) * P]) for tt in range(TILES)]
                        + [(32 + tt * 8, row[60 + tt][0:8, tt * P:(tt + 1) * P]) for tt in range(TILES)], 8)
                for c in range(4):
                    claim(4 + c % 2)
                    pe.wait_ge(scalar_out, scalar_at.find("xbc", c))
                    for tt in range(TILES):
                        m = nc.tensor.transpose(bank[4 + c % 2][:, tt * P:(tt + 1) * P], xbc[:, c, tt * P:(tt + 1) * P], ident)
                    m.then_inc(tensor_out, tensor_at.next("xt", c))
                    reader[4 + c % 2] = (VECTOR, ("xp", c))
                for g in range(4):
                    claim(6)
                    pe.wait_ge(vector_out, vector_at.find("pooled", g))
                    m = nc.tensor.matmul(bank[6][:], pw[:, g, :], arena[:, 66 + g, :], start=True, stop=True)
                    m.then_inc(tensor_out, tensor_at.next("poolmm", g))
                    reader[6] = (VECTOR, ("poolout", g))
                stage_end(pe, tensor_at, "in1")
                decayed("ssd", ssm_steps)
                run_units("z1", X, SCALAR)
                norm("ssmn", 4, 512, ys, MIX, False)
                stage_end(pe, tensor_at, "mix1")
                run_units("out1", MIX, VECTOR)
                norm("ln1_1", DC, 1024, X, MIX, True)
                stage_end(pe, tensor_at, "ln1_1")
            if on("up1"):
                ffn(1, X)
                norm("ln2_1", DC, 1024, X, MIX, True)
                stage_end(pe, tensor_at, "ln2_1")
            if on("small2"):
                norm("rms1", DC, 1024, X, MIX, False)
                stage_end(pe, tensor_at, "rms1")
                run_units("small2", U, SCALAR)
                run_units("ik", U, VECTOR)
                run_units("iq", U, SCALAR)
                columns("gate2", [(c * 40 + 8 * x, row[r][0:8, c * P:(c + 1) * P]) for x, r in enumerate((62, 64, 63, 59, 60)) for c in range(TILES)], 8)
                item_norms("ikn", 1, inv[128], lambda k: row[65], lambda k: arena[:, 66, :], True)
                run_units("dq", U, SCALAR)
                run_units("dk", U, SCALAR)
                run_moving("dv", 256, U, None)
                pe.wait_ge(vector_out, vector_at.find("ikn", "out"))
                n = 0
                for i in range(1, TILES):
                    for h in range(IDX_HEADS):
                        claim(4 + n % 4)
                        m = nc.tensor.matmul(bank[4 + n % 4][:, 0:(i + 1) * P], iq[:, h // 2, i * P:(i + 1) * P], ikp[:, h % 2, 0:(i + 1) * P], start=True, stop=True)
                        m.then_inc(tensor_out, tensor_at.next("idx", n))
                        reader[4 + n % 4] = (SCALAR, ("relu", n))
                        n += 1
                stage_end(pe, tensor_at, "topk")
                attention("dsa", dsa_steps)
                run_units("gateb", U, SCALAR)
                stage_end(pe, tensor_at, "dsa")
            if on("gqkv"):
                run_units("gqkv", U, VECTOR)
                item_norms("l2", 16, ones, lambda k: arena[:, 24 + k, :], lambda k: arena[:, 48 + k % 2, :], False)
                stage_end(pe, tensor_at, "gqkv")

                def four(b, l, r, start=True, stop=True):
                    for hh in range(4):
                        m = nc.tensor.matmul(tile(b)[:, hh, :], l(hh), r(hh), start=start, stop=stop)
                    return m

                for c in range(TILES):
                    cs = slice(c * P, (c + 1) * P)
                    for g in range(2):
                        t = (c, g)
                        G = GW
                        claim(0)
                        for hh in range(4):
                            nc.tensor.matmul(tile(0)[:, hh, :], sel(4 * g + hh), row[62][0:8, cs], start=True, stop=False)
                            m = nc.tensor.matmul(tile(0)[:, hh, :], idb[:], mtb[:], start=False, stop=True)
                        m.then_inc(tensor_out, tensor_at.next("gb", t))
                        reader[0] = (SCALAR, ("gam", t))
                        claim(1)
                        four(1, lambda hh: sel(4 * g + hh), lambda hh: row[62][0:8, cs]).then_inc(tensor_out, tensor_at.next("ge", t))
                        reader[1] = (SCALAR, ("eg", t))
                        claim(2)
                        four(2, lambda hh: sel(4 * g + hh), lambda hh: row[59][0:8, cs]).then_inc(tensor_out, tensor_at.next("bb", t))
                        reader[2] = (VECTOR, ("kb", t))
                        claim(3)
                        four(3, lambda hh: gk[:, 4 * g + hh, cs], lambda hh: gq[:, 4 * g + hh, cs]).then_inc(tensor_out, tensor_at.next("kq", t))
                        reader[3] = (VECTOR, ("att", t))
                        claim(4)
                        for hh in range(4):
                            m = nc.tensor.transpose(tile(4)[:, hh, :], gk[:, 4 * g + hh, cs], ident)
                        m.then_inc(tensor_out, tensor_at.next("kt", t))
                        reader[4] = (SCALAR, ("kd", t))
                        claim(5)
                        for hh in range(4):
                            m = nc.tensor.transpose(tile(5)[:, hh, :], gv[:, 4 * g + hh, cs], ident)
                        m.then_inc(tensor_out, tensor_at.next("vt", t))
                        reader[5] = (SCALAR, ("vb", t))
                        claim(6)
                        pe.wait_ge(vector_out, vector_at.find("kb", t))
                        four(6, lambda hh: gk[:, 4 * g + hh, cs], lambda hh: G["kb"][:, hh, :]).then_inc(tensor_out, tensor_at.next("kk", t))
                        reader[6] = (VECTOR, ("at", t))
                        claim(7)
                        pe.wait_ge(vector_out, vector_at.find("lt", t, 0))
                        for hh in range(4):
                            m = nc.tensor.transpose(tile(7)[:, hh, :], G["lt"][:, hh, :], ident)
                        m.then_inc(tensor_out, tensor_at.next("l0", t))
                        reader[7] = (VECTOR, ("t", t, 0))
                        for r in range(1, LEVELS):
                            claim(0)
                            pe.wait_ge(vector_out, vector_at.find("lt", t, r))
                            pe.wait_ge(vector_out, vector_at.find("t", t, r - 1))
                            four(0, lambda hh: G["lt"][:, hh, :], lambda hh: G["t"][:, hh, :]).then_inc(tensor_out, tensor_at.next("x", t, r))
                            reader[0] = (SCALAR, ("xs", t, r))
                            pe.wait_ge(scalar_out, scalar_at.find("xs", t, r))
                            claim(1)
                            claim(2)
                            pe.wait_ge(vector_out, vector_at.find("u", t, r - 1))
                            m = four(1, lambda hh: G["xs"][:, hh, :], lambda hh: G["u"][:, hh, :])
                            if r < LEVELS - 1:
                                m = four(2, lambda hh: G["u"][:, hh, :], lambda hh: G["xs"][:, hh, :])
                            m.then_inc(tensor_out, tensor_at.next("y", t, r))
                            reader[1] = (VECTOR, ("u", t, r))
                            if r < LEVELS - 1:
                                reader[2] = (VECTOR, ("t", t, r))
                        claim(3)
                        pe.wait_ge(scalar_out, scalar_at.find("kd", t))
                        pe.wait_ge(vector_out, vector_at.find("u", t, LEVELS - 1))
                        four(3, lambda hh: G["kbe"][:, hh, :], lambda hh: G["u"][:, hh, :]).then_inc(tensor_out, tensor_at.next("w", t))
                        reader[3] = (SCALAR, ("nw", t))
                        claim(4)
                        pe.wait_ge(scalar_out, scalar_at.find("nw", t))
                        for hh in range(4):
                            m = nc.tensor.matmul(tile(4)[:, hh, :], G["u"][:, hh, :], G["vb"][:, hh, :], start=True, stop=c == 0)
                            if c:
                                m = nc.tensor.matmul(tile(4)[:, hh, :], G["nw"][:, hh, :], state[:, g, hh, :], start=False, stop=True)
                        m.then_inc(tensor_out, tensor_at.next("vn", t))
                        reader[4] = (SCALAR, ("vn", t))
                        claim(5)
                        claim(6)
                        pe.wait_ge(scalar_out, scalar_at.find("vn", t))
                        pe.wait_ge(vector_out, vector_at.find("qg", t))
                        for hh in range(4):
                            m = nc.tensor.matmul(tile(5)[:, hh, :], G["vn"][:, hh, :], G["att"][:, hh, :], start=True, stop=c == 0)
                            if c:
                                m = nc.tensor.matmul(tile(5)[:, hh, :], state[:, g, hh, :], G["qg"][:, hh, :], start=False, stop=True)
                        m.then_inc(tensor_out, tensor_at.next("o", t))
                        reader[5] = (SCALAR, ("o", t))
                        four(6, lambda hh: G["kd"][:, hh, :], lambda hh: G["vn"][:, hh, :]).then_inc(tensor_out, tensor_at.next("s", t))
                        reader[6] = (VECTOR, ("s", t))
                stage_end(pe, tensor_at, "gdn")
                item_norms("gn", 8, inv[128], lambda k: go[:, k, :], lambda k: arena[:, 56 + k % 2, :], False)
                run_units("z2", U, SCALAR)
                run_units("gatea", U, SCALAR)
                stage_end(pe, tensor_at, "mix2")
                run_units("out2", MIX, VECTOR)
                norm("rms2", DC, 1024, X, gq, False)
                stage_end(pe, tensor_at, "rms2")
            if on("up2"):
                ffn(2, U)
                norm("rmsf", DC, 1024, X, MIX, False)

        @block.scalar
        def _(act):
            A = nc.scalar.activation

            def unit_done(name, j):
                act.wait_ge(units_done, FIRST[name] + j + 1)

            def evac(name, func, dst, bias=0.0, scale=1.0, wait=None):
                for j in range(COUNT[name]):
                    unit_done(name, j)
                    if wait is not None:
                        wait(j)
                    b = bias(j) if callable(bias) else bias
                    A(dst(j), bank[(FIRST[name] + j) % RING][:], func, bias=b, scale=scale).then_inc(scalar_out, scalar_at.next("read", name, j))

            def root(b, dst, eps, *key):
                e = small[:, 250:251] if eps == LN_EPS else small[:, 251:252]
                A(dst, bank[b][:], ACT.Sqrt, bias=e).then_inc(scalar_out, scalar_at.next(*key))

            def norm(name, chunks, xs, sq, mean, eps, affine=None):
                for k in range(chunks):
                    act.wait_ge(vector_out, vector_at.find(name, "xc" if mean else "x", k))
                    A(sq[:, k, :], xs[:, k, :], ACT.Square).then_inc(scalar_out, scalar_at.next(name, "sq", k))
                act.wait_ge(tensor_out, tensor_at.find(name, "ms"))
                root(7, RSTD, eps, name, "root")
                if affine is not None:
                    for k in range(chunks):
                        act.wait_ge(vector_out, vector_at.find(name, "scaled", k))
                        A(X[:, k, :], U[:, k, :], ACT.Identity, bias=col(affine[1], k), scale=col(affine[0], k)).then_inc(scalar_out, scalar_at.next(name, "out", k))

            def item_norms(name, items, xs, sqs, mean, eps, tmp):
                for k in range(items + 1):
                    if k < items:
                        if mean:
                            act.wait_ge(vector_out, vector_at.find(name, "xc", k))
                        if k >= 2:
                            act.wait_ge(tensor_out, tensor_at.find(name, "ms", k - 2))
                        A(sqs(k), xs(k), ACT.Square).then_inc(scalar_out, scalar_at.next(name, "sq", k))
                    if k >= 1:
                        act.wait_ge(tensor_out, tensor_at.find(name, "ms", k - 1))
                        if k >= 3:
                            act.wait_ge(vector_out, vector_at.find(name, "out", k - 3))
                        root(7, tmp(k - 1), eps, name, "root", k - 1)

            def attention(name, steps):
                N = len(steps)
                for n in range(N + 3):
                    if n < N:
                        st, W = steps[n], steps[n]["w"]
                        act.wait_ge(vector_out, vector_at.find(name, "max", n))
                        if n >= 4:
                            act.wait_ge(tensor_out, tensor_at.find(name, "t", n - 4))
                        A(arena[:, st["ps"], 0:W], bank[2 + n % 3][:, 0:W], ACT.Exp, bias=small[:, 200 + n % 4:201 + n % 4],
                                     accum_out=small[:, 204 + n % 4:205 + n % 4]).then_inc(scalar_out, scalar_at.next(name, "exp", n))
                    if 2 <= n < N + 2:
                        k, st = n - 2, steps[n - 2]
                        act.wait_ge(tensor_out, tensor_at.find(name, "t", k))
                        if k >= 3:
                            act.wait_ge(tensor_out, tensor_at.find(name, "pv", k - 3))
                        A(arena[:, st["ts"], 0:st["w"]], bank[5 + k % 2][:, 0:st["w"]], ACT.Copy).then_inc(scalar_out, scalar_at.next(name, "pt", k))
                    if n >= 3 and steps[n - 3]["last"]:
                        st = steps[n - 3]
                        act.wait_ge(tensor_out, tensor_at.find(name, "pv", n - 3))
                        A(MIX[:, st["dst"], :], bank[st["ob"]][:], ACT.Copy).then_inc(scalar_out, scalar_at.next(name, "o", st["o"]))

            def decayed(name, steps, extra=None):
                for n, st in enumerate(steps):
                    W = SEQ - st["j"] * P
                    act.wait_ge(tensor_out, tensor_at.find(name, "e", n))
                    if n >= 3:
                        act.wait_ge(vector_out, vector_at.find(name, "p", n - 3))
                    A(arena[:, 66 + n % 3, 0:W], bank[2 + n % 2][:, 0:W], ACT.Exp, bias=st["bias"]).then_inc(scalar_out, scalar_at.next(name, "w", n))
                    if st["first"] and extra is not None:
                        extra(st)

            def ffn(l):
                u0, c0 = FIRST[f"up{l}"], COL[f"ffn{l}"]
                with act.Fori(0, 2 * FC // RING) as i:
                    for s in range(RING):
                        b = (u0 + s) % RING
                        act.wait_ge(units_done, RING * i + u0 + s + 1)
                        act.wait_ge(hid_done, 2 * i + 1 + l * FC + s // 2)
                        A(acc[:, s, :], bank[b][:], ACT.Identity, bias=par[:, bass.ds(4 * RING * i + (c0 + 4 * s + 3), 1)],
                          scale=par[:, bass.ds(4 * RING * i + (c0 + 4 * s + 2), 1)]).then_inc(acc_done, 1)
                        if s % 2:
                            act.wait_ge(conv_done, RING * i + (4 + 2 * l * FC + s))
                            A(sg[:, s // 2, :], acc[:, s - 1, :], ACT.Silu).then_inc(gate_done, 1)

            def softplus_tail(name):
                act.wait_ge(vector_out, vector_at.find(name, "abs"))
                A(row[57], row[57], ACT.Exp).then_inc(scalar_out, scalar_at.next())
                act.wait_ge(scalar_out, scalar_at.n)
                A(row[57], row[57], ACT.Ln, bias=1.0).then_inc(scalar_out, scalar_at.next(name, "ln"))

            act.wait_ge(in_sem, 16 * nloads)
            act.wait_ge(gpsimd_out, gpsimd_at.find("setup"))
            evac("small0", ACT.Identity, lambda j: row[56], bias=lambda j: col("b_small0"))
            softplus_tail("gate0")
            scalar_at.mark("gate0", "rows")
            for j in range(4):
                unit_done("mk", j)
                A(mk[:, j, :], bank[(FIRST["mk"] + j) % RING][:], ACT.Identity, bias=col("b_mk", j)).then_inc(scalar_out, scalar_at.next("read", "mk", j))
            for j in range(4):
                unit_done("fk", j)
                for e in range(2):
                    p0 = 64 * e
                    A(fk[p0:p0 + 64, 2 * j + e, :], bank[(FIRST["fk"] + j) % RING][p0:p0 + 64, :], ACT.Identity, bias=col("b_fk", j, p0, p0 + 64)).then_inc(scalar_out, scalar_at.next("read", "fk", j))
            stage_end(act, scalar_at, "in0")

            def exp_minus_m(st):
                h = st["out"]
                act.wait_ge(tensor_out, tensor_at.find("ml", "m", h))
                if h >= 2:
                    act.wait_ge(vector_out, vector_at.find("ml", "fin", h - 2))
                A(arena[:, 74 + h % 2, :], bank[6][:], ACT.Exp).then_inc(scalar_out, scalar_at.next("ml", "em", h))

            decayed("ml", ml_steps, exp_minus_m)
            item_norms("hn", 4, lambda k: MIX[:, k, :], lambda k: arena[:, 72 + k % 2, :], True, LN_EPS, lambda k: arena[:, 70 + k % 2, :])
            stage_end(act, scalar_at, "ml")
            attention("fox", fox_steps)
            evac("mo", ACT.Sigmoid, lambda j: arena[:, 66 + j, :], bias=lambda j: col("b_mo", j),
                 wait=lambda j: act.wait_ge(tensor_out, tensor_at.find("fox", "pv", len(fox_steps) - 1)) if j == 0 else None)
            stage_end(act, scalar_at, "mix0")
            norm("ln1_0", DC, U, MIX, True, LN_EPS, ("ln1_g0", "ln1_b0"))
            stage_end(act, scalar_at, "ln1_0")
            if on("up0"):
                ffn(0)
                norm("ln2_0", DC, U, MIX, True, LN_EPS, ("ln2_g0", "ln2_b0"))
                stage_end(act, scalar_at, "ln2_0")
            if on("small1"):
                A(small[0:8, 208:209], par[0:8, COL["a_log"]:COL["a_log"] + 1], ACT.Exp).then_inc(scalar_out, scalar_at.next("ea1"))
                evac("small1", ACT.Identity, lambda j: row[56], bias=lambda j: col("dt_bias"))
                softplus_tail("gate1")
                scalar_at.mark("gate1", "rows")
                for j in range(8 + 1):
                    if j < 8:
                        unit_done("xbc", j)
                        A(xbc[:, j, :], bank[(FIRST["xbc"] + j) % RING][:], ACT.Identity, bias=col("xbc_conv", 5 * j + 4), scale=col("xbc_conv", 5 * j + 3)).then_inc(scalar_out, scalar_at.next("xa", j))
                    if j >= 1:
                        act.wait_ge(vector_out, vector_at.find("read", "xbc", j - 1))
                        A(xbc[:, j - 1, :], xbc[:, j - 1, :], ACT.Silu).then_inc(scalar_out, scalar_at.next("xbc", j - 1))
                act.wait_ge(gpsimd_out, gpsimd_at.find("pads1"))
                evac("pool", ACT.Copy, lambda j: pbuf[j][:, 16:16 + SEQ])
                stage_end(act, scalar_at, "in1")
                decayed("ssd", ssm_steps)
                evac("z1", ACT.Silu, lambda j: arena[:, 72 + j, :])
                norm("ssmn", 4, ys, MIX, False, LN_EPS)
                stage_end(act, scalar_at, "mix1")
                norm("ln1_1", DC, U, MIX, True, LN_EPS, ("ln1_g1", "ln1_b1"))
                stage_end(act, scalar_at, "ln1_1")
            if on("up1"):
                ffn(1)
                norm("ln2_1", DC, U, MIX, True, LN_EPS, ("ln2_g1", "ln2_b1"))
                stage_end(act, scalar_at, "ln2_1")
            if on("small2"):
                norm("rms1", DC, X, MIX, False, RMS_EPS)
                stage_end(act, scalar_at, "rms1")
                A(small[0:8, 208:209], par[0:8, COL["g_a_log"]:COL["g_a_log"] + 1], ACT.Exp).then_inc(scalar_out, scalar_at.next("ea2"))
                unit_done("small2", 0)
                b = bank[FIRST["small2"] % RING]
                A(row[56], b[:], ACT.Identity, bias=col("g_dt_bias")).then_inc(scalar_out, scalar_at.next("pre2"))
                A(row[60][0:8, :], b[64:72, :], ACT.Copy, scale=(IDX_HEADS ** -0.5) * (64 ** -0.5)).then_inc(scalar_out, scalar_at.next())
                A(row[59][0:8, :], b[32:40, :], ACT.Sigmoid).then_inc(scalar_out, scalar_at.next("read", "small2", 0))
                softplus_tail("gate2")
                act.wait_ge(vector_out, vector_at.find("dG"))
                A(row[63][0:8, :], row[63][0:8, :], ACT.Exp).then_inc(scalar_out, scalar_at.next())
                A(row[64][0:8, :], row[62][0:8, :], ACT.Exp).then_inc(scalar_out, scalar_at.next("eG"))
                scalar_at.mark("gate2", "rows")
                evac("iq", ACT.Copy, lambda j: iq[:, j, :])
                act.wait_ge(vector_out, vector_at.find("ikn", "x", 0))
                item_norms("ikn", 1, lambda k: row[65], lambda k: arena[:, 66, :], True, RMS_EPS, lambda k: RSTD)
                evac("dq", ACT.Copy, lambda j: dq[:, j, :], scale=P ** -0.5)
                evac("dk", ACT.Copy, lambda j: dk[:, j, :])
                n = 0
                for i in range(1, TILES):
                    for h in range(IDX_HEADS):
                        act.wait_ge(tensor_out, tensor_at.find("idx", n))
                        if n >= 4:
                            act.wait_ge(vector_out, vector_at.find("sc", n - 4))
                        A(arena[:, 67 + n % 4, 0:(i + 1) * P], bank[4 + n % 4][:, 0:(i + 1) * P], ACT.Relu).then_inc(scalar_out, scalar_at.next("relu", n))
                        n += 1
                stage_end(act, scalar_at, "topk")
                attention("dsa", dsa_steps)
                evac("gateb", ACT.Sigmoid, lambda j: arena[:, 66 + j % 4, :], bias=lambda j: col("gate_b", 8 + j),
                     wait=lambda j: act.wait_ge(vector_out, vector_at.find("gateb", j - 4)) if j >= 4 else act.wait_ge(tensor_out, tensor_at.find("dsa", "pv", len(dsa_steps) - 1)))
                stage_end(act, scalar_at, "dsa")
            if on("gqkv"):
                for j in range(24 + 1):
                    if j < 24:
                        unit_done("gqkv", j)
                        A(arena[:, 24 + j, :], bank[(FIRST["gqkv"] + j) % RING][:], ACT.Copy, scale=col("gqkv_conv", 4 * j + 3)).then_inc(scalar_out, scalar_at.next("ga", j))
                    if j >= 1:
                        act.wait_ge(vector_out, vector_at.find("read", "gqkv", j - 1))
                        A(arena[:, 23 + j, :], arena[:, 23 + j, :], ACT.Silu).then_inc(scalar_out, scalar_at.next("gqkv", j - 1))
                act.wait_ge(scalar_out, scalar_at.n)
                item_norms("l2", 16, lambda k: arena[:, 24 + k, :], lambda k: arena[:, 48 + k % 2, :], False, RMS_EPS, lambda k: arena[:, 50 + k % 2, :])
                stage_end(act, scalar_at, "gqkv")
                for c in range(TILES):
                    for g in range(2):
                        t, G = (c, g), GW

                        def cc(x, hh):
                            return small[:, c * 40 + 8 * x + 4 * g + hh:c * 40 + 8 * x + 4 * g + hh + 1]

                        act.wait_ge(tensor_out, tensor_at.find("gb", t))
                        if t != (0, 0):
                            act.wait_ge(vector_out, vector_at.find("s", (c, 0) if g else (c - 1, 1)))
                        for hh in range(4):
                            ng = small[:, 160 + c * 8 + 4 * g + hh:161 + c * 8 + 4 * g + hh]
                            A(G["gam"][:, hh, :], tile(0)[:, hh, :], ACT.Exp, bias=ng).then_inc(scalar_out, scalar_at.next("gam", t))
                        act.wait_ge(tensor_out, tensor_at.find("ge", t))
                        A(G["eg"], tile(1), ACT.Exp).then_inc(scalar_out, scalar_at.next("eg", t))
                        act.wait_ge(tensor_out, tensor_at.find("kt", t))
                        for hh in range(4):
                            A(G["kbe"][:, hh, :], tile(4)[:, hh, :], ACT.Copy, scale=cc(1, hh)).then_inc(scalar_out, scalar_at.next())
                            A(G["kd"][:, hh, :], tile(4)[:, hh, :], ACT.Copy, scale=cc(2, hh)).then_inc(scalar_out, scalar_at.next("kd", t))
                        act.wait_ge(tensor_out, tensor_at.find("vt", t))
                        for hh in range(4):
                            A(G["vb"][:, hh, :], tile(5)[:, hh, :], ACT.Copy, scale=cc(3, hh)).then_inc(scalar_out, scalar_at.next("vb", t))
                        for r in range(1, LEVELS):
                            act.wait_ge(tensor_out, tensor_at.find("x", t, r))
                            A(G["xs"], tile(0), ACT.Copy).then_inc(scalar_out, scalar_at.next("xs", t, r))
                        act.wait_ge(tensor_out, tensor_at.find("w", t))
                        A(G["nw"], tile(3), ACT.Copy, scale=-1.0).then_inc(scalar_out, scalar_at.next("nw", t))
                        act.wait_ge(tensor_out, tensor_at.find("vn", t))
                        A(G["vn"], tile(4), ACT.Copy).then_inc(scalar_out, scalar_at.next("vn", t))
                        act.wait_ge(tensor_out, tensor_at.find("o", t))
                        A(go[:, 4 * g:4 * g + 4, c * P:(c + 1) * P], tile(5), ACT.Copy).then_inc(scalar_out, scalar_at.next("o", t))
                stage_end(act, scalar_at, "gdn")
                item_norms("gn", 8, lambda k: go[:, k, :], lambda k: arena[:, 56 + k % 2, :], False, RMS_EPS, lambda k: arena[:, 58 + k % 2, :])
                evac("z2", ACT.Silu, lambda j: arena[:, 65 + j, :])
                evac("gatea", ACT.Sigmoid, lambda j: arena[:, 65 + j, :], bias=lambda j: col("gate_b", j), wait=lambda j: act.wait_ge(vector_out, vector_at.find("z2", j)))
                stage_end(act, scalar_at, "mix2")
                norm("rms2", DC, X, gq, False, RMS_EPS)
                stage_end(act, scalar_at, "rms2")
            if on("up2"):
                ffn(2)
                norm("rmsf", DC, X, MIX, False, RMS_EPS)
            src = U if on("up2") else X
            for k in range(DC):
                if on("up2"):
                    act.wait_ge(vector_out, vector_at.find("rmsf", "out", k))
                act.dma_start(out[:, k, :], src[:, k, :]).then_inc(out_sem, 16)
            act.wait_ge(out_sem, 16 * DC)

        @block.gpsimd
        def _(pool):
            for n in (128, 512, 1024):
                nc.gpsimd.memset(inv[n][:], 1.0 / n).then_inc(gpsimd_out, gpsimd_at.next())
            nc.gpsimd.memset(ones[:], 1.0).then_inc(gpsimd_out, gpsimd_at.next())
            nc.gpsimd.memset(small[:, 250:251], LN_EPS).then_inc(gpsimd_out, gpsimd_at.next())
            nc.gpsimd.memset(small[:, 251:252], RMS_EPS).then_inc(gpsimd_out, gpsimd_at.next())
            nc.gpsimd.memset(arena[:, 40:56, :], 0.0).then_inc(gpsimd_out, gpsimd_at.next("setup"))
            gpsimd_at.mark("stage", "in0")
            for st in ("ml", "mix0", "ln1_0"):
                gpsimd_at.mark("stage", st)
            if on("up0"):
                gpsimd_at.mark("stage", "ln2_0")
            if on("small1"):
                pool.wait_ge(tensor_out, tensor_at.find("stage", "ln2_0"))
                pool.wait_ge(scalar_out, scalar_at.find("stage", "ln2_0"))
                pool.wait_ge(vector_out, vector_at.find("stage", "ln2_0"))
                nc.gpsimd.memset(arena[:, 36:56, :], 0.0).then_inc(gpsimd_out, gpsimd_at.next("pads1"))
                for st in ("in1", "mix1", "ln1_1", "ln2_1", "rms1"):
                    gpsimd_at.mark("stage", st)
            if on("small2"):
                pool.wait_ge(tensor_out, tensor_at.find("stage", "rms1"))
                pool.wait_ge(scalar_out, scalar_at.find("stage", "rms1"))
                pool.wait_ge(vector_out, vector_at.find("stage", "rms1"))
                nc.gpsimd.memset(ikp, 0.0).then_inc(gpsimd_out, gpsimd_at.next("pads2"))
                for st in ("topk", "dsa", "gqkv", "gdn", "mix2", "rms2"):
                    gpsimd_at.mark("stage", st)

        @block.vector
        def _(dve):
            V = nc.vector
            STT = nc.vector.scalar_tensor_tensor

            def unit_done(name, j):
                dve.wait_ge(units_done, FIRST[name] + j + 1)

            def norm(name, chunks, xs, mean, gain=None, dst=None):
                if mean:
                    dve.wait_ge(tensor_out, tensor_at.find(name, "mean"))
                    for k in range(chunks):
                        V.tensor_tensor(U[:, k, :], xs[:, k, :], bank[6][:], ALU.subtract).then_inc(vector_out, vector_at.next(name, "xc", k))
                    vector_at.mark(name, "centred")
                dve.wait_ge(scalar_out, scalar_at.find(name, "root"))
                V.reciprocal(RSTD, RSTD).then_inc(vector_out, vector_at.next())
                dve.wait_ge(vector_out, vector_at.n)
                for k in range(chunks):
                    if mean:
                        V.tensor_tensor(U[:, k, :], U[:, k, :], RSTD, ALU.mult).then_inc(vector_out, vector_at.next(name, "scaled", k))
                    else:
                        STT(dst[:, k, :], xs[:, k, :], col(gain, k), RSTD, ALU.mult, ALU.mult).then_inc(vector_out, vector_at.next(name, "out", k))

            def residual(name, nxt, factor, last_unit_only):
                for j in range(DC):
                    if last_unit_only:
                        unit_done(name, COUNT[name] - 1)
                        b = j
                    else:
                        unit_done(name, j)
                        b = (FIRST[name] + j) % RING
                    STT(X[:, j, :], X[:, j, :], factor, bank[b][:], ALU.mult, ALU.add).then_inc(vector_out, vector_at.next("read", name, j))
                    vector_at.mark(nxt, "x", j)

            def conv(name, j, dst, u, taps):
                for n, (shift, w) in enumerate(taps):
                    STT(dst[:, shift:], u[:, 0:SEQ - shift], w, dst[:, shift:], ALU.mult, ALU.add).then_inc(vector_out, vector_at.next())
                    if n < len(taps) - 1:
                        dve.wait_ge(vector_out, vector_at.n)
                vector_at.mark("read", name, j)

            def attention(name, steps):
                N = len(steps)
                for n in range(N + 1):
                    if n < N:
                        dve.wait_ge(tensor_out, tensor_at.find(name, "logits", n))
                        if n >= 4:
                            dve.wait_ge(scalar_out, scalar_at.find(name, "exp", n - 4))
                        V.tensor_reduce(small[:, 200 + n % 4:201 + n % 4], bank[2 + n % 3][:, 0:steps[n]["w"]], AX_X, ALU.max, negate=True).then_inc(vector_out, vector_at.next(name, "max", n))
                    if n >= 1:
                        k, st = n - 1, steps[n - 1]
                        dve.wait_ge(scalar_out, scalar_at.find(name, "exp", k))
                        V.reciprocal(small[:, 204 + k % 4:205 + k % 4], small[:, 204 + k % 4:205 + k % 4]).then_inc(vector_out, vector_at.next())
                        dve.wait_ge(vector_out, vector_at.n)
                        p = arena[:, st["ps"], 0:st["w"]]
                        V.tensor_scalar(p, p, small[:, 204 + k % 4:205 + k % 4], None, ALU.mult).then_inc(vector_out, vector_at.next(name, "p", k))

            def decayed(name, steps, finish):
                N = len(steps)
                for n in range(N + 2):
                    if n < N:
                        W = SEQ - steps[n]["j"] * P
                        dve.wait_ge(scalar_out, scalar_at.find(name, "w", n))
                        dve.wait_ge(tensor_out, tensor_at.find(name, "s", n))
                        if n >= 3:
                            dve.wait_ge(tensor_out, tensor_at.find(name, "pv", n - 3))
                        V.tensor_tensor(arena[:, 69 + n % 3, 0:W], arena[:, 66 + n % 3, 0:W], bank[4 + n % 2][:, 0:W], ALU.mult).then_inc(vector_out, vector_at.next(name, "p", n))
                    if n >= 2 and steps[n - 2]["last"]:
                        dve.wait_ge(tensor_out, tensor_at.find(name, "pv", n - 2))
                        finish(steps[n - 2])

            def ffn(l):
                c0 = COL[f"ffn{l}"]
                b0 = FIRST[f"up{l}"]
                with dve.Fori(0, 2 * FC // RING) as i:
                    for s in range(RING):
                        u = bank[(b0 + s) % RING]
                        dve.wait_ge(acc_done, RING * i + (2 * l * FC + s + 1))
                        STT(acc[:, s, 1:], u[:, 0:SEQ - 1], par[:, bass.ds(4 * RING * i + (c0 + 4 * s + 1), 1)], acc[:, s, 1:], ALU.mult, ALU.add).then_inc(tap_done, 1)
                        dve.wait_ge(tap_done, RING * i + (2 * l * FC + s + 1))
                        STT(acc[:, s, 2:], u[:, 0:SEQ - 2], par[:, bass.ds(4 * RING * i + (c0 + 4 * s), 1)], acc[:, s, 2:], ALU.mult, ALU.add).then_inc(conv_done, 1)
                        if s % 2:
                            dve.wait_ge(conv_done, RING * i + (4 + 2 * l * FC + s + 1))
                            dve.wait_ge(gate_done, 2 * i + (l * FC + s // 2 + 1))
                            V.tensor_tensor(hid[:, bass.ds(2 * i + s // 2, 1), :].rearrange("p a n -> p (a n)"), sg[:, s // 2, :], acc[:, s, :], ALU.mult).then_inc(hid_done, 1)

            def absolute(name, key):
                dve.wait_ge(scalar_out, scalar_at.find(*key))
                STT(row[57], row[56], -1.0, row[56], ALU.mult, ALU.min).then_inc(vector_out, vector_at.next(name, "abs"))

            dve.wait_ge(in_sem, 16 * nloads)
            V.tensor_copy(idb[:], ident).then_inc(vector_out, vector_at.next())
            V.tensor_copy(mtb[:], con[:, K_MT:K_MT + P]).then_inc(vector_out, vector_at.next())
            V.tensor_copy(mqb[:], con[:, K_MQ:K_MQ + P]).then_inc(vector_out, vector_at.next("setup"))
            for n in range(RING):
                V.memset(small[:, 210 + n:211 + n], 0.0).then_inc(conv_done, 1)
            for n in range(2):
                V.memset(small[:, 214 + n:215 + n], 0.0).then_inc(hid_done, 1)
            dve.wait_ge(gpsimd_out, gpsimd_at.find("setup"))

            absolute("gate0", ("read", "small0", 0))
            dve.wait_ge(scalar_out, scalar_at.find("gate0", "ln"))
            STT(row[58], row[56], 0.0, row[57], ALU.min, ALU.subtract).then_inc(vector_out, vector_at.next())
            dve.wait_ge(vector_out, vector_at.n)
            V.tensor_tensor_scan(row[59], ones[:], row[58], 0.0, ALU.mult, ALU.add).then_inc(vector_out, vector_at.next())
            dve.wait_ge(vector_out, vector_at.n)
            V.tensor_scalar(row[61][0:8, :], row[59][64:72, :], -1.0, None, ALU.mult).then_inc(vector_out, vector_at.next())
            V.tensor_copy(row[60][0:4, :], row[59][32:36, :]).then_inc(vector_out, vector_at.next())
            dve.wait_ge(vector_out, vector_at.n)
            V.tensor_tensor(row[62][0:4, :], row[56][0:4, :], row[60][0:4, :], ALU.subtract).then_inc(vector_out, vector_at.next())
            dve.wait_ge(vector_out, vector_at.n)
            V.tensor_tensor_scan(row[63][0:4, :], row[62][0:4, :], row[62][0:4, :], 0.0, ALU.max, ALU.max).then_inc(vector_out, vector_at.next())
            dve.wait_ge(vector_out, vector_at.n)
            V.tensor_scalar(row[64][0:4, :], row[63][0:4, :], -1.0, None, ALU.mult).then_inc(vector_out, vector_at.next())
            STT(row[65][0:4, :], row[60][0:4, :], -1.0, row[63][0:4, :], ALU.mult, ALU.subtract).then_inc(vector_out, vector_at.next("gate0", "rows"))
            for j in range(4):
                unit_done("mq", j)
                V.tensor_scalar(mq[:, j, :], bank[(FIRST["mq"] + j) % RING][:], col("b_mq", j), P ** -0.5, ALU.add, ALU.mult).then_inc(vector_out, vector_at.next("read", "mq", j))
            for tt in range(TILES):
                unit_done("mv", COUNT["mv"] - 1)
                V.tensor_copy(mv[:, tt, :], bank[tt][:]).then_inc(vector_out, vector_at.next("read", "mv", tt))
            for j in range(4):
                unit_done("fq", j)
                V.tensor_scalar(fq[:, j, :], bank[(FIRST["fq"] + j) % RING][:], col("b_fq", j), 64 ** -0.5, ALU.add, ALU.mult).then_inc(vector_out, vector_at.next("read", "fq", j))
            for tt in range(TILES):
                unit_done("fv", COUNT["fv"] - 1)
                for e in range(2):
                    dst = fv[:, tt, :, :].rearrange("p (c e) d -> p c e d", e=2)[:, :, e, 64 * e:64 * e + 64]
                    src = bank[tt][:].rearrange("p (c e d) -> p c e d", e=2, d=64)[:, :, e, :]
                    V.tensor_copy(dst, src).then_inc(vector_out, vector_at.next("read", "fv", tt))
            dve.wait_ge(tensor_out, tensor_at.find("gate0", "cols"))
            V.tensor_copy(small[:, 0:16], bank[4][:, 0:16]).then_inc(vector_out, vector_at.next("gate0", "cols"))
            stage_end(dve, vector_at, "in0")

            def ml_finish(st):
                h, b = st["out"], 76
                dve.wait_ge(scalar_out, scalar_at.find("ml", "em", h))
                STT(arena[:, b, :], bank[1][:], -1.0, arena[:, 74 + h % 2, :], ALU.mult, ALU.max).then_inc(vector_out, vector_at.next())
                dve.wait_ge(vector_out, vector_at.n)
                V.tensor_tensor(arena[:, b, :], bank[1][:], arena[:, b, :], ALU.max).then_inc(vector_out, vector_at.next())
                dve.wait_ge(vector_out, vector_at.n)
                V.reciprocal(arena[:, b, :], arena[:, b, :]).then_inc(vector_out, vector_at.next())
                dve.wait_ge(vector_out, vector_at.n)
                V.tensor_tensor(MIX[:, h, :], bank[0][:], arena[:, b, :], ALU.mult).then_inc(vector_out, vector_at.next("ml", "fin", h))
                vector_at.mark("hn", "x", h)

            decayed("ml", ml_steps, ml_finish)
            dve.wait_ge(vector_out, vector_at.n)

            def item_norms(name, items, xs, mean, write, tmp):
                for k in range(items + 1):
                    if k < items and mean:
                        dve.wait_ge(tensor_out, tensor_at.find(name, "mean", k))
                        V.tensor_tensor(xs(k), xs(k), bank[6][:], ALU.subtract).then_inc(vector_out, vector_at.next(name, "xc", k))
                        vector_at.mark(name, "centred", k)
                    if k >= 1:
                        dve.wait_ge(scalar_out, scalar_at.find(name, "root", k - 1))
                        V.reciprocal(tmp(k - 1), tmp(k - 1)).then_inc(vector_out, vector_at.next())
                        dve.wait_ge(vector_out, vector_at.n)
                        write(k - 1, tmp(k - 1))
                        vector_at.mark(name, "out", k - 1)

            item_norms("hn", 4, lambda k: MIX[:, k, :], True,
                       lambda k, r: STT(MIX[:, k, :], MIX[:, k, :], col("ml_norm", k), r, ALU.mult, ALU.mult).then_inc(vector_out, vector_at.next("hn", "out", k)),
                       lambda k: arena[:, 70 + k % 2, :])
            stage_end(dve, vector_at, "ml")
            attention("fox", fox_steps)
            for j in range(4):
                dve.wait_ge(scalar_out, scalar_at.find("read", "mo", j))
                V.tensor_tensor(MIX[:, j, :], MIX[:, j, :], arena[:, 66 + j, :], ALU.mult).then_inc(vector_out, vector_at.next("mo", j))
            stage_end(dve, vector_at, "mix0")
            residual("out0", "ln1_0", ALPHA, False)
            norm("ln1_0", DC, X, True)
            stage_end(dve, vector_at, "ln1_0")
            if on("up0"):
                ffn(0)
                residual("down0", "ln2_0", ALPHA, True)
                norm("ln2_0", DC, X, True)
                stage_end(dve, vector_at, "ln2_0")
            if on("small1"):
                absolute("gate1", ("read", "small1", 0))
                dve.wait_ge(scalar_out, scalar_at.find("gate1", "ln"))
                STT(row[58], row[56], 0.0, row[57], ALU.max, ALU.add).then_inc(vector_out, vector_at.next())
                dve.wait_ge(vector_out, vector_at.n)
                dve.wait_ge(scalar_out, scalar_at.find("ea1"))
                V.tensor_scalar(row[59][0:8, :], row[58][0:8, :], small[0:8, 208:209], -1.0, ALU.mult, ALU.mult).then_inc(vector_out, vector_at.next())
                dve.wait_ge(vector_out, vector_at.n)
                for j in range(TILES):
                    V.tensor_tensor_scan(row[60 + j][0:8, j * P:], ones[0:8, j * P:], row[59][0:8, j * P:], 0.0, ALU.mult, ALU.add).then_inc(vector_out, vector_at.next())
                vector_at.mark("gate1", "rows")
                for j in range(8):
                    dve.wait_ge(scalar_out, scalar_at.find("xa", j))
                    conv("xbc", j, xbc[:, j, :], bank[(FIRST["xbc"] + j) % RING], [(s, col("xbc_conv", 5 * j + 3 - s)) for s in (1, 2, 3)])
                dve.wait_ge(tensor_out, tensor_at.find("gate1", "cols"))
                V.tensor_copy(small[:, 0:32], bank[4][:, 0:32]).then_inc(vector_out, vector_at.next())
                V.tensor_scalar(small[:, 32:64], bank[4][:, 32:64], -1.0, None, ALU.mult).then_inc(vector_out, vector_at.next("gate1", "cols"))
                dve.wait_ge(vector_out, vector_at.n)
                dve.wait_ge(gpsimd_out, gpsimd_at.find("pads1"))
                for c in range(4):
                    dve.wait_ge(tensor_out, tensor_at.find("xt", c))
                    for tt in range(TILES):
                        for e in range(2):
                            h = 2 * c + e
                            V.tensor_scalar(xpad[:, tt, h, 64 * e:64 * e + 64], bank[4 + c % 2][:, tt * P + 64 * e:tt * P + 64 * e + 64],
                                                       small[:, tt * 8 + h:tt * 8 + h + 1], None, ALU.mult).then_inc(vector_out, vector_at.next("xp", c))
                for g, w in enumerate(POOL_WINDOWS):
                    dve.wait_ge(scalar_out, scalar_at.find("read", "pool", g))
                    u, cur, s, n = pbuf[g], pbuf[g], 1, 0
                    while s < w:
                        dst = pbuf[4 + n % 2]
                        V.tensor_tensor(dst[:, 16:16 + SEQ], cur[:, 16:16 + SEQ], cur[:, 16 - s:16 - s + SEQ], ALU.add).then_inc(vector_out, vector_at.next())
                        dve.wait_ge(vector_out, vector_at.n)
                        cur, s, n = dst, 2 * s, n + 1
                    pooled = arena[:, 66 + g, :]
                    STT(pooled, cur[:, 16:16 + SEQ], 1.0 / w, u[:, 16:16 + SEQ], ALU.mult, ALU.subtract).then_inc(vector_out, vector_at.next())
                    V.tensor_tensor(small[:, 64:80], cur[:, 16:32], con[:, K_CNT + 16 * g:K_CNT + 16 * g + 16], ALU.mult).then_inc(vector_out, vector_at.next())
                    dve.wait_ge(vector_out, vector_at.n)
                    V.tensor_tensor(pooled[:, 0:16], small[:, 64:80], u[:, 16:32], ALU.subtract).then_inc(vector_out, vector_at.next("pooled", g))
                for g in range(4):
                    dve.wait_ge(tensor_out, tensor_at.find("poolmm", g))
                    V.tensor_scalar(MIX[:, 4 + g, :], bank[6][:], col("pool_b", g), col("pool_s", g), ALU.add, ALU.mult).then_inc(vector_out, vector_at.next("poolout", g))
                stage_end(dve, vector_at, "in1")

                def ssm_finish(st):
                    c = st["out"]
                    STT(ys[:, c, :], xbc[:, c, :], col("d_skip", c), bank[st["num"]][:], ALU.mult, ALU.add).then_inc(vector_out, vector_at.next("ssd", "fin", c))

                decayed("ssd", ssm_steps, ssm_finish)
                for j in range(4):
                    dve.wait_ge(scalar_out, scalar_at.find("read", "z1", j))
                    dve.wait_ge(vector_out, vector_at.n)
                    V.tensor_tensor(ys[:, j, :], ys[:, j, :], arena[:, 72 + j, :], ALU.mult).then_inc(vector_out, vector_at.next("ssmn", "x", j))
                norm("ssmn", 4, ys, False, "ssm_norm", MIX)
                stage_end(dve, vector_at, "mix1")
                residual("out1", "ln1_1", ALPHA, False)
                norm("ln1_1", DC, X, True)
                stage_end(dve, vector_at, "ln1_1")
            if on("up1"):
                ffn(1)
                residual("down1", "ln2_1", ALPHA, True)
                norm("ln2_1", DC, X, True)
                stage_end(dve, vector_at, "ln2_1")
            if on("small2"):
                for k in range(DC):
                    vector_at.mark("rms1", "x", k)
                norm("rms1", DC, X, False, "norm1", U)
                stage_end(dve, vector_at, "rms1")
                absolute("gate2", ("pre2",))
                dve.wait_ge(scalar_out, scalar_at.find("gate2", "ln"))
                STT(row[58], row[56], 0.0, row[57], ALU.max, ALU.add).then_inc(vector_out, vector_at.next())
                dve.wait_ge(vector_out, vector_at.n)
                dve.wait_ge(scalar_out, scalar_at.find("ea2"))
                V.tensor_scalar(row[61][0:8, :], row[58][0:8, :], small[0:8, 208:209], -1.0, ALU.mult, ALU.mult).then_inc(vector_out, vector_at.next())
                dve.wait_ge(vector_out, vector_at.n)
                for c in range(TILES):
                    V.tensor_tensor_scan(row[62][0:8, c * P:(c + 1) * P], ones[0:8, 0:P], row[61][0:8, c * P:(c + 1) * P], 0.0, ALU.mult, ALU.add).then_inc(vector_out, vector_at.next())
                    dve.wait_ge(vector_out, vector_at.n)
                    V.tensor_scalar(row[63][0:8, c * P:(c + 1) * P], row[62][0:8, c * P:(c + 1) * P], -1.0, row[62][0:8, (c + 1) * P - 1:(c + 1) * P], ALU.mult, ALU.add).then_inc(vector_out, vector_at.next())
                vector_at.mark("dG")
                dve.wait_ge(scalar_out, scalar_at.find("eG"))
                V.tensor_tensor(row[64][0:8, :], row[64][0:8, :], row[59][0:8, :], ALU.mult).then_inc(vector_out, vector_at.next("gate2", "rows"))
                unit_done("ik", 0)
                V.tensor_copy(row[65], bank[FIRST["ik"] % RING][:]).then_inc(vector_out, vector_at.next("read", "ik", 0))
                vector_at.mark("ikn", "x", 0)
                dve.wait_ge(tensor_out, tensor_at.find("gate2", "cols"))
                V.tensor_copy(small[:, 0:160], bank[4][:, 0:160]).then_inc(vector_out, vector_at.next())
                src = bank[4][:, 0:160].rearrange("p (c x) -> p c x", c=TILES)[:, :, 0:8]
                V.tensor_scalar(small[:, 160:192].rearrange("p (c x) -> p c x", c=TILES), src, -1.0, None, ALU.mult).then_inc(vector_out, vector_at.next("gate2", "cols"))
                dve.wait_ge(vector_out, vector_at.n)
                dve.wait_ge(gpsimd_out, gpsimd_at.find("pads2"))

                def ik_write(k, r):
                    for e in range(2):
                        p0 = 64 * e
                        STT(ikp[p0:p0 + 64, e, :], row[65][p0:p0 + 64, :], col("ik_norm", 0, p0, p0 + 64), r[p0:p0 + 64, :], ALU.mult, ALU.mult).then_inc(vector_out, vector_at.next("ikn", "out"))

                dve.wait_ge(vector_out, vector_at.n)
                item_norms("ikn", 1, lambda k: row[65], True, ik_write, lambda k: RSTD)
                for tt in range(TILES):
                    unit_done("dv", 1)
                    V.tensor_copy(dv[:, tt, :], bank[tt][:, 0:256]).then_inc(vector_out, vector_at.next("read", "dv", tt))
                n = 0
                for i in range(1, TILES):
                    sc = score[:, i, 0:(i + 1) * P]
                    for h in range(IDX_HEADS):
                        dve.wait_ge(scalar_out, scalar_at.find("relu", n))
                        r = arena[:, 67 + n % 4, 0:(i + 1) * P]
                        w = small[:, i * 40 + 32 + h:i * 40 + 33 + h]
                        if h == 0:
                            V.tensor_scalar(sc, r, w, None, ALU.mult).then_inc(vector_out, vector_at.next("sc", n))
                            dve.wait_ge(vector_out, vector_at.n)
                        else:
                            STT(sc, r, w, sc, ALU.mult, ALU.add).then_inc(vector_out, vector_at.next("sc", n))
                            dve.wait_ge(vector_out, vector_at.n)
                        n += 1
                    V.tensor_tensor(score[:, i, i * P:(i + 1) * P], score[:, i, i * P:(i + 1) * P], con[:, K_MQ:K_MQ + P], ALU.add).then_inc(vector_out, vector_at.next())
                    dve.wait_ge(vector_out, vector_at.n)
                for rnd in range(TOPK // 8):
                    for i in range(1, TILES):
                        V.max(small[:, 216 + 8 * i:224 + 8 * i], score[:, i, 0:(i + 1) * P]).then_inc(vector_out, vector_at.next("top", rnd, i))
                    for i in range(1, TILES):
                        dve.wait_ge(vector_out, vector_at.find("top", rnd, i))
                        sc = score[:, i, 0:(i + 1) * P]
                        V.match_replace(sc, small[:, 216 + 8 * i:224 + 8 * i], sc, TAKEN).then_inc(vector_out, vector_at.next())
                    dve.wait_ge(vector_out, vector_at.n)
                for i in range(1, TILES):
                    V.tensor_scalar(madd[:, i, 0:(i + 1) * P], score[:, i, 0:(i + 1) * P], -2e38, NEG, ALU.is_ge, ALU.mult).then_inc(vector_out, vector_at.next())
                stage_end(dve, vector_at, "topk")
                attention("dsa", dsa_steps)
                for j in range(DC):
                    dve.wait_ge(scalar_out, scalar_at.find("read", "gateb", j))
                    V.tensor_tensor(MIX[:, j, :], MIX[:, j, :], arena[:, 66 + j % 4, :], ALU.mult).then_inc(vector_out, vector_at.next("gateb", j))
                stage_end(dve, vector_at, "dsa")
            if on("gqkv"):
                for j in range(24):
                    dve.wait_ge(scalar_out, scalar_at.find("ga", j))
                    conv("gqkv", j, arena[:, 24 + j, :], bank[(FIRST["gqkv"] + j) % RING], [(s, col("gqkv_conv", 4 * j + 3 - s)) for s in (1, 2, 3)])

                def l2_write(k, r):
                    x = arena[:, 24 + k, :]
                    STT(x, x, P ** -0.5 if k < 8 else 1.0, r, ALU.mult, ALU.mult).then_inc(vector_out, vector_at.next())

                item_norms("l2", 16, None, False, l2_write, lambda k: arena[:, 50 + k % 2, :])
                stage_end(dve, vector_at, "gqkv")
                for c in range(TILES):
                    cs = slice(c * P, (c + 1) * P)
                    for g in range(2):
                        t, G = (c, g), GW

                        def every(ap):
                            return ap.rearrange("p (a n) -> p a n", a=1).to_broadcast([P, 4, P])

                        def lev(r):
                            return every(con[:, K_LEV + r * P:K_LEV + (r + 1) * P])

                        dve.wait_ge(tensor_out, tensor_at.find("bb", t))
                        V.tensor_tensor(G["kb"], gk[:, 4 * g:4 * g + 4, cs], tile(2), ALU.mult).then_inc(vector_out, vector_at.next("kb", t))
                        dve.wait_ge(tensor_out, tensor_at.find("kk", t))
                        dve.wait_ge(scalar_out, scalar_at.find("gam", t))
                        V.tensor_tensor(G["at"], tile(6), G["gam"], ALU.mult).then_inc(vector_out, vector_at.next("at", t))
                        dve.wait_ge(vector_out, vector_at.n)
                        V.tensor_tensor(G["lt"], G["at"], lev(0), ALU.mult).then_inc(vector_out, vector_at.next("lt", t, 0))
                        dve.wait_ge(vector_out, vector_at.n)
                        V.tensor_tensor(G["u"], every(ident), G["lt"], ALU.subtract).then_inc(vector_out, vector_at.next("u", t, 0))
                        dve.wait_ge(tensor_out, tensor_at.find("kq", t))
                        V.tensor_tensor(G["att"], tile(3), G["gam"], ALU.mult).then_inc(vector_out, vector_at.next("att", t))
                        dve.wait_ge(scalar_out, scalar_at.find("eg", t))
                        V.tensor_tensor(G["qg"], gq[:, 4 * g:4 * g + 4, cs], G["eg"], ALU.mult).then_inc(vector_out, vector_at.next("qg", t))
                        dve.wait_ge(tensor_out, tensor_at.find("l0", t))
                        V.tensor_tensor(G["t"], every(ident), tile(7), ALU.subtract).then_inc(vector_out, vector_at.next("t", t, 0))
                        for r in range(1, LEVELS):
                            if r > 1:
                                dve.wait_ge(tensor_out, tensor_at.find("x", t, r - 1))
                            dve.wait_ge(vector_out, vector_at.n)
                            V.tensor_tensor(G["lt"], G["at"], lev(r), ALU.mult).then_inc(vector_out, vector_at.next("lt", t, r))
                            dve.wait_ge(tensor_out, tensor_at.find("y", t, r))
                            dve.wait_ge(vector_out, vector_at.n)
                            if r < LEVELS - 1:
                                V.tensor_tensor(G["t"], G["t"], tile(2), ALU.subtract).then_inc(vector_out, vector_at.next("t", t, r))
                            V.tensor_tensor(G["u"], G["u"], tile(1), ALU.subtract).then_inc(vector_out, vector_at.next("u", t, r))
                        dve.wait_ge(tensor_out, tensor_at.find("s", t))
                        for hh in range(4):
                            if c:
                                STT(state[:, g, hh, :], state[:, g, hh, :], G["eg"][:, hh, P - 1:P], tile(6)[:, hh, :], ALU.mult, ALU.add).then_inc(vector_out, vector_at.next("s", t))
                            else:
                                V.tensor_copy(state[:, g, hh, :], tile(6)[:, hh, :]).then_inc(vector_out, vector_at.next("s", t))
                stage_end(dve, vector_at, "gdn")
                item_norms("gn", 8, None, False,
                           lambda k, r: STT(go[:, k, :], go[:, k, :], col("gdn_norm"), r, ALU.mult, ALU.mult).then_inc(vector_out, vector_at.next("gn", "out", k)),
                           lambda k: arena[:, 58 + k % 2, :])
                for j in range(DC):
                    dve.wait_ge(scalar_out, scalar_at.find("read", "z2", j))
                    dve.wait_ge(vector_out, vector_at.find("gn", "out", j))
                    V.tensor_tensor(go[:, j, :], go[:, j, :], arena[:, 65 + j, :], ALU.mult).then_inc(vector_out, vector_at.next("z2", j))
                for j in range(DC):
                    dve.wait_ge(scalar_out, scalar_at.find("read", "gatea", j))
                    dve.wait_ge(vector_out, vector_at.find("z2", j))
                    V.tensor_tensor(go[:, j, :], go[:, j, :], arena[:, 65 + j, :], ALU.mult).then_inc(vector_out, vector_at.next())
                    dve.wait_ge(vector_out, vector_at.n)
                    V.tensor_tensor(MIX[:, j, :], MIX[:, j, :], go[:, j, :], ALU.add).then_inc(vector_out, vector_at.next())
                stage_end(dve, vector_at, "mix2")
                residual("out2", "rms2", 1.0, False)
                norm("rms2", DC, X, False, "norm2", U)
                stage_end(dve, vector_at, "rms2")
            if on("up2"):
                ffn(2)
                residual("down2", "rmsf", 1.0, True)
                norm("rmsf", DC, X, False, "final", U)


LAST_STAGE = None


def lay_out(inp):
    f = {k: np.asarray(v) for k, v in inp.items()}
    units = []

    def stationary(w, padded=None):
        k, n = w.shape
        for j in range(n // P):
            units.append(w[:, j * P:(j + 1) * P].reshape(DC, P, P).transpose(1, 0, 2).reshape(P, 8 * P))

    def moving(w, q):
        n = w.shape[1]
        w = w.reshape(DC, P, n)
        for j in range(DC // q):
            units.append(w[j * q:(j + 1) * q].transpose(1, 0, 2).reshape(P, 8 * P))

    def rows(parts, shape):
        w = np.zeros(shape + (P,), np.float32)
        for x, part in enumerate(parts):
            w[..., 32 * x:32 * x + part.shape[-1]] = part
        return w

    def up(w, gate_first):
        a, b = (w[:, :D_FF], w[:, D_FF:]) if gate_first else (w[:, D_FF:], w[:, :D_FF])
        for j in range(FC):
            stationary(a[:, j * P:(j + 1) * P])
            stationary(b[:, j * P:(j + 1) * P])

    def down(w):
        for j in range(FC):
            units.append(w[j * P:(j + 1) * P, :])

    we, be = f["ev_w_in"][0], f["ev_b_in"][0]
    H = HALF
    o = [0, H, 2 * H, 3 * H, 4 * H, 4 * H + 4, 4 * H + 8, 5 * H + 8, 6 * H + 8, 7 * H + 8, 7 * H + 16]
    e = [we[:, o[i]:o[i + 1]] for i in range(10)]
    eb = [be[o[i]:o[i + 1]] for i in range(10)]
    stationary(rows([e[4], e[5], e[9]], (DM,)))
    stationary(e[0]); stationary(e[1]); moving(e[2], 2)
    stationary(e[6]); stationary(e[7]); moving(e[8], 2)
    stationary(e[3])
    stationary(f["ev_w_out"][0])
    up(f["ffn_w_up"][0], False); down(f["ffn_w_down"][0])
    wo = f["od_w_in"][0]
    stationary(rows([wo[:, 1536:1544]], (DM,)))
    stationary(wo[:, 512:1536]); stationary(wo[:, 1544:2056]); stationary(wo[:, 0:512])
    stationary(f["od_w_out"][0])
    up(f["ffn_w_up"][1], False); down(f["ffn_w_down"][1])
    w2 = f["w_in_2"][0]
    cut = lambda a, b: w2[:, a:b]
    stationary(rows([cut(4096, 4104), cut(4104, 4112), cut(6224, 6232)], (DM,)))
    stationary(np.concatenate([cut(6160, 6224)] * 2, 1))
    stationary(cut(5648, 6160)); stationary(cut(4112, 5136)); stationary(cut(5136, 5392)); moving(cut(5392, 5648), 4)
    stationary(cut(7256, 8280))
    stationary(cut(0, 3072)); stationary(cut(3072, 4096)); stationary(cut(6232, 7256))
    stationary(f["w_out_2"][0])
    up(f["ffn_w_up_2"][0], True); down(f["ffn_w_down_2"][0])
    stream = np.ascontiguousarray(np.stack(units))
    assert len(units) == UNITS

    cols = {n: [] for n, _ in COLS}

    def put(name, v):
        cols[name] += list(np.asarray(v).reshape(-1, P))

    put("b_small0", rows([eb[4], eb[5], eb[9]], ()))
    for n, x in (("b_mq", 0), ("b_mk", 1), ("b_fq", 6), ("b_fk", 7), ("b_mo", 3)):
        put(n, eb[x])
    put("ml_norm", f["ev_ml_norm"][0])
    for l in range(2):
        for n in ("ln1_g", "ln1_b", "ln2_g", "ln2_b"):
            put(f"{n}{l}", f[n][l])
    put("dt_bias", rows([f["od_dt_bias"][0]], ()))
    put("a_log", rows([f["od_a_log"][0]], ()))
    cw = f["od_conv_w"][0]
    put("xbc_conv", np.concatenate([cw, f["od_conv_b"]], 0).reshape(5, 8, P).transpose(1, 0, 2))
    put("d_skip", np.repeat(f["od_d_skip"][0], 64))
    put("ssm_norm", f["od_ssm_norm"][0]); put("pool_b", f["od_pool_b"][0]); put("pool_s", f["od_pool_scale"][0])

    def ffn_cols(name, w, b, gate_first):
        x = np.concatenate([w, b[None]], 0).reshape(4, 2, FC, P).transpose(2, 1, 0, 3)
        put(name, x if gate_first else x[:, ::-1])

    ffn_cols("ffn0", f["ffn_conv_w"][0], f["ffn_conv_b"][0], False)
    ffn_cols("ffn1", f["ffn_conv_w"][1], f["ffn_conv_b"][1], False)
    ffn_cols("ffn2", f["ffn_conv_w_2"][0], f["ffn_conv_b_2"][0], True)
    put("norm1", f["norm1_g_2"][0]); put("norm2", f["norm2_g_2"][0]); put("final", f["final_g_2"])
    put("g_dt_bias", rows([f["gdn_dt_bias_2"][0]], ())); put("g_a_log", rows([f["gdn_a_log_2"][0]], ()))
    put("gqkv_conv", f["gdn_conv_w_2"][0].reshape(4, 24, P).transpose(1, 0, 2))
    put("gdn_norm", f["gdn_norm_g_2"][0]); put("ik_norm", np.concatenate([f["idx_k_norm_g_2"][0]] * 2)); put("gate_b", f["branch_gate_b_2"][0])
    for n, c in COLS:
        assert len(cols[n]) == c, (n, len(cols[n]))
    params = np.ascontiguousarray(np.stack([v for n, _ in COLS for v in cols[n]], 1))

    con = np.zeros((P, NCONST), np.float32)
    i = np.arange(P)
    con[:, K_ID:K_ID + P] = np.eye(P)
    con[:, K_MT:K_MT + P] = np.where(i[None, :] >= i[:, None], 0.0, NEG)
    con[:, K_MQ:K_MQ + P] = np.where(i[None, :] <= i[:, None], 0.0, NEG)
    for r in range(LEVELS):
        b = 1 << r
        same = (i[:, None] // (2 * b) == i[None, :] // (2 * b)) & (i[:, None] // b % 2 == 0) & (i[None, :] // b % 2 == 1)
        con[:, K_LEV + r * P:K_LEV + (r + 1) * P] = same
    for g, w in enumerate(POOL_WINDOWS):
        con[:, K_CNT + 16 * g:K_CNT + 16 * g + 16] = 1.0 / np.minimum(np.arange(16) + 1, w)
    for h in range(8):
        con[h, K_SEL + h * P:K_SEL + (h + 1) * P] = 1.0

    xt = np.ascontiguousarray(f["x"][0].T.reshape(DC, P, SEQ).transpose(1, 0, 2))
    brow = np.ascontiguousarray(np.concatenate([eb[2], eb[8]])[None])
    poolw = np.ascontiguousarray(f["od_pool_w"][0].transpose(1, 0, 2))
    return {"stream": stream, "params": params, "brow": brow, "poolw": poolw, "consts": con, "xt": xt}


def kernel(**inputs):
    import concourse.bacc as _bacc
    from concourse.bass_utils import run_bass_kernel_spmd as _run

    arrays = lay_out(inputs)
    marks = {}
    for _ in range(2):
        nc = _bacc.Bacc("TRN2", target_bir_lowering=False, num_devices=1)
        args = [nc.dram_tensor(k, v.shape, F32, kind="ExternalInput").ap() for k, v in arrays.items()]
        args.append(nc.dram_tensor("out", (P, DC, SEQ), F32, kind="ExternalOutput").ap())
        build_program(nc, *args, marks, LAST_STAGE)
    r = _run(nc, [arrays], core_ids=[0])
    got = r.results[0]["out"]
    return np.ascontiguousarray(got.transpose(1, 0, 2).reshape(1, DM, SEQ).transpose(0, 2, 1))
```

```python
from contextlib import ExitStack

import numpy as np
import concourse.bass as bass
from concourse import mybir

ALU = mybir.AluOpType
ACT = mybir.ActivationFunctionType
F32 = mybir.dt.float32
BF16 = mybir.dt.bfloat16
F32R = mybir.dt.float32r
AX_X = mybir.AxisListType.X

P = 128
SEQ = 512
TILES = SEQ // P
DM = 1024
DC = DM // P
D_FF = 2816
FC = D_FF // P
HALF = 512
DEPTH = 2
ALPHA = (2.0 * DEPTH) ** 0.25
LN_EPS = 1e-5
RMS_EPS = 1e-6
NEG = -1e30
TAKEN = -3e38
TOPK = min(256, SEQ // 4)
RING = 4
ML_HEADS, FOX_HEADS, SSM_HEADS, GDN_HEADS, DSA_HEADS, IDX_HEADS = 4, 8, 8, 8, 8, 8
POOL_WINDOWS = (2, 4, 8, 16)
LEVELS = 7

RUNS = [
    ("small0", 1), ("mq", 4), ("mk", 4), ("mv", 4), ("fq", 4), ("fk", 4), ("fv", 4), ("mo", 4), ("out0", 8),
    ("up0", 2 * FC), ("down0", FC),
    ("small1", 1), ("xbc", 8), ("pool", 4), ("z1", 4), ("out1", 8),
    ("up1", 2 * FC), ("down1", FC),
    ("small2", 1), ("ik", 1), ("iq", 4), ("dq", 8), ("dk", 2), ("dv", 2), ("gateb", 8),
    ("gqkv", 24), ("z2", 8), ("gatea", 8), ("out2", 8),
    ("up2", 2 * FC), ("down2", FC),
]
FIRST, _u = {}, 0
for _name, _n in RUNS:
    FIRST[_name] = _u
    _u += _n
COUNT = dict(RUNS)
UNITS = _u

COLS = [
    ("b_small0", 1), ("b_mq", 4), ("b_mk", 4), ("b_fq", 4), ("b_fk", 4), ("b_mo", 4), ("ml_norm", 4),
    ("ln1_g0", 8), ("ln1_b0", 8), ("ln2_g0", 8), ("ln2_b0", 8), ("ln1_g1", 8), ("ln1_b1", 8), ("ln2_g1", 8), ("ln2_b1", 8),
    ("dt_bias", 1), ("a_log", 1), ("xbc_conv", 8 * 5), ("d_skip", 4), ("ssm_norm", 4), ("pool_b", 4), ("pool_s", 4),
    ("ffn0", 2 * FC * 4), ("ffn1", 2 * FC * 4), ("ffn2", 2 * FC * 4),
    ("norm1", 8), ("norm2", 8), ("final", 8), ("g_dt_bias", 1), ("g_a_log", 1), ("gqkv_conv", 24 * 4),
    ("gdn_norm", 1), ("ik_norm", 1), ("gate_b", 16),
]
COL, _c = {}, 0
for _name, _n in COLS:
    COL[_name] = _c
    _c += _n
NCOL = _c

K_ID, K_MT, K_MQ, K_LEV, K_CNT, K_SEL = 0, P, 2 * P, 3 * P, (3 + LEVELS) * P, (3 + LEVELS) * P + 64
NCONST = K_SEL + 8 * P


class Counts:

    def __init__(self, marks):
        self.marks, self.n = marks, 0

    def next(self, *key):
        self.n += 1
        if key:
            self.marks[key] = self.n
        return 1

    def mark(self, *key):
        self.marks[key] = self.n

    def find(self, *key):
        return self.marks.get(key, 1)


def build_program(nc, stream, params, brow, poolw, consts, xt, out, marks, last_stage):
    with ExitStack() as ctx:
        def sb(name, shape, dt=F32):
            return ctx.enter_context(nc.sbuf_tensor(name, shape, dt))

        def sem(name):
            return ctx.enter_context(nc.semaphore(name))

        arena = sb("arena", [P, 62, SEQ])
        ring = sb("ring", [P, RING, 8 * P])
        whi, wlo = sb("whi", [P, 2, 8 * P], F32R), sb("wlo", [P, 2, 8 * P], F32R)
        with nc.sbuf_tensor("scratch", [P, 16, SEQ], F32) as scratch:
            pass
        xs = sb("xs", [P, 16, SEQ], F32R)
        xhi, xlo = xs[:, 0:8, :], xs[:, 8:16, :]
        par = sb("par", [P, NCOL])
        con = sb("con", [P, NCONST])
        idb = sb("idb", [P, P], BF16)
        mtb = sb("mtb", [P, P], BF16)
        mqb = sb("mqb", [P, P], BF16)
        ones = sb("ones", [P, SEQ])
        inv = {n: sb(f"inv{n}", [P, P]) for n in (128, 512, 1024)}
        small = sb("small", [P, 256])
        pw = sb("pw", [P, TILES, P])
        bank = [ctx.enter_context(nc.psum_tensor(f"bank{b}", [P, SEQ], F32)) for b in range(8)]

        ident = con[:, K_ID:K_ID + P]
        ident8 = con[0:8, K_ID:K_ID + 8]

        def sel(h, n=8):
            return con[0:n, K_SEL + h * P:K_SEL + (h + 1) * P]

        def col(name, j=0, p0=0, p1=P):
            return par[p0:p1, COL[name] + j:COL[name] + j + 1]

        X, U, MIX = arena[:, 0:8, :], arena[:, 8:16, :], arena[:, 16:24, :]

        in_sem = sem("in_sem")
        ring_sem = [sem(f"ring_loaded{s}") for s in range(RING)]
        units_done, whi_done, wlo_done = sem("units_done"), sem("weights_high_done"), sem("weights_low_done")
        tensor_out, scalar_out, vector_out, gpsimd_out = sem("tensor_out"), sem("scalar_out"), sem("vector_out"), sem("gpsimd_out")
        tensor_at, scalar_at, vector_at, gpsimd_at = (Counts(marks.setdefault(n, {})) for n in ("tensor", "scalar", "vector", "gpsimd"))
        SCALAR, VECTOR = (scalar_out, scalar_at), (vector_out, vector_at)
        acc_done, tap_done, conv_done = sem("ffn_acc_done"), sem("ffn_tap_done"), sem("ffn_conv_done")
        gate_done, hid_done = sem("ffn_gate_done"), sem("ffn_hidden_done")
        hhi_done, hlo_done = sem("hidden_high_done"), sem("hidden_low_done")
        out_sem = sem("out_sem")
        nloads = 5

        ctx.enter_context(nc.allow_low_precision(reason="0/1 and mask constants"))
        block = ctx.enter_context(nc.Block())
        last_unit = UNITS if last_stage is None else FIRST[last_stage] + COUNT[last_stage]

        def on(stage):
            return FIRST[stage] < last_unit

        @block.sync
        def _(sp):
            sp.dma_start(X, xt).then_inc(in_sem, 16)
            sp.dma_start(par[:], params).then_inc(in_sem, 16)
            sp.dma_start(con[:], consts).then_inc(in_sem, 16)
            sp.dma_start(pw[:], poolw).then_inc(in_sem, 16)
            sp.dma_start(arena[0:1, 20:22, :], brow.rearrange("a (c n) -> a c n", c=2)).then_inc(in_sem, 16)
            for s in range(RING):
                sp.dma_start(ring[:, s, :], stream[s]).then_inc(ring_sem[s], 16)
            loads = last_unit + 2
            rounds = loads // RING
            with sp.Fori(1, rounds) as i:
                for s in range(RING):
                    sp.wait_ge(wlo_done, (i - 1) * RING + s + 1)
                    sp.dma_start(ring[:, s, :], stream[i * RING + s]).then_inc(ring_sem[s], 16)
            for u in range(rounds * RING, loads):
                sp.wait_ge(wlo_done, u - RING + 1)
                sp.dma_start(ring[:, u % RING, :], stream[u]).then_inc(ring_sem[u % RING], 16)

        def stage_end(eng, mine, name):
            mine.mark("stage", name)
            eng.wait_ge(tensor_out, tensor_at.find("stage", name))
            eng.wait_ge(scalar_out, scalar_at.find("stage", name))
            eng.wait_ge(vector_out, vector_at.find("stage", name))
            eng.wait_ge(gpsimd_out, gpsimd_at.find("stage", name))

        mq, mk, mv = arena[:, 24:28, :], arena[:, 28:32, :], arena[:, 32:36, :]
        fq, fk = arena[:, 36:40, :], arena[:, 40:48, :]
        fv = arena[:, 48:56, :].rearrange("p (t a) n -> p t (a n)", a=2).rearrange("p t (h d) -> p t h d", h=FOX_HEADS)
        row = {j: arena[:, c, :] for j, c in {56: 16, 57: 17, 58: 18, 65: 19, 59: 56, 60: 57, 61: 58, 62: 59, 63: 60, 64: 61}.items()}
        RSTD = arena[:, 55, :]
        gate = arena[:, 8:12, :]
        bias_v = arena[0:1, 20:22, :]
        hid, acc, sg = arena[:, 24:24 + FC, :], arena[:, 46:50, :], arena[:, 50:52, :]
        xbc, ys = arena[:, 24:32, :], arena[:, 32:36, :]
        xpad = arena[:, 36:44, :].rearrange("p (t a) n -> p t (a n)", a=2).rearrange("p t (h d) -> p t h d", h=SSM_HEADS)
        pbuf = [arena[:, 44 + 2 * g:46 + 2 * g, :].rearrange("p a n -> p (a n)") for g in range(6)]
        iq, ikp, dq, dk = arena[:, 24:28, :], arena[:, 28:30, :], arena[:, 30:38, :], arena[:, 38:40, :]
        dv = arena[:, 40:42, :].rearrange("p a n -> p (a n)").rearrange("p (t n) -> p t n", t=TILES)
        madd = arena[:, 42:44, :].rearrange("p a n -> p (a n)").bitcast(BF16).rearrange("p (t n) -> p t n", t=TILES)
        score = arena[:, 44:48, :]
        gq, gk, gv = arena[:, 24:32, :], arena[:, 32:40, :], arena[:, 40:48, :]
        go = gv
        GW = {n: scratch[:, i, :].rearrange("p (h n) -> p h n", h=4) for i, n in enumerate(
            ["gam", "eg", "kb", "at", "att", "qg", "u", "t", "lt", "xs", "kbe", "kd", "vb", "nw", "vn"])}
        state = arena[:, 57:59, :].rearrange("p g (h n) -> p g h n", h=4)

        def tile(b):
            return bank[b][:, :].rearrange("p (h n) -> p h n", h=4)

        ml_steps = [dict(j=j, sel=sel(h, 4), rows=row[64][0:4, j * P:], bias=small[:, j * 4 + h:j * 4 + h + 1], k=mk[:, h, j * P:(j + 1) * P],
                         q=mq[:, h, j * P:], v=mv[:, j, h * P:(h + 1) * P], num=0, den=1, first=j == 0, last=j == TILES - 1, out=h)
                    for h in range(ML_HEADS) for j in range(TILES)]
        ssm_steps = [dict(j=j, sel=sel(h), rows=row[60 + j][0:8, j * P:], bias=small[:, 32 + j * 8 + h:33 + j * 8 + h], k=xbc[:, 4 + h // 4, j * P:(j + 1) * P],
                          q=xbc[:, 6 + h // 4, j * P:], v=xpad[:, j, h, :], num=h // 2 % 2, den=None, first=j == 0 and h % 2 == 0,
                          last=j == TILES - 1 and h % 2 == 1, out=h // 2)
                     for h in range(SSM_HEADS) for j in range(TILES)]
        fox_steps = [dict(w=(i + 1) * P, q=fq[:, h // 2, i * P:(i + 1) * P], k=fk[:, h, 0:(i + 1) * P],
                          more=[(sel(h), row[61][0:8, 0:(i + 1) * P], 0, (i + 1) * P), (idb[:], mqb[:], i * P, (i + 1) * P)],
                          v=[fv[:, j, h, :] for j in range(i + 1)], ob=c % 2, oc=i * P, start=h % 2 == 0, stop=h % 2 == 1,
                          claim=i == 0 and h % 2 == 0, last=i == TILES - 1 and h % 2 == 1, o=c, dst=4 + c)
                     for c in range(4) for i in range(TILES) for h in (2 * c, 2 * c + 1)]
        dsa_steps = [dict(w=(i + 1) * P, q=dq[:, h, i * P:(i + 1) * P], k=dk[:, h // 4, 0:(i + 1) * P],
                          more=[(idb[:], madd[:, i, 0:(i + 1) * P] if i else mqb[:], 0, (i + 1) * P)],
                          v=[dv[:, j, (h // 4) * P:(h // 4 + 1) * P] for j in range(i + 1)], ob=h % 2, oc=i * P, start=True, stop=True,
                          claim=i == 0, last=i == TILES - 1, o=h, dst=h)
                     for h in range(DSA_HEADS) for i in range(TILES)]
        for steps, work in ((fox_steps, scratch[:, 0:7, :]), (dsa_steps, arena[:, 48:55, :])):
            for n, st in enumerate(steps):
                st["ps"], st["ts"] = work[:, n % 4, :], work[:, 4 + n % 3, :]

        @block.tensor
        def _(pe):
            reader = {}

            def claim(b):
                if b in reader:
                    (semaphore, at), key = reader[b]
                    pe.wait_ge(semaphore, at.find(*key))

            def unit_split(u):
                pe.wait_ge(wlo_done, u + 1)

            def products(out, wcols, xs3, first, last):
                (ah, al), (bh, bl) = wcols, xs3
                nc.tensor.matmul(out, ah, bh, start=first, stop=False)
                nc.tensor.matmul(out, ah, bl, start=False, stop=False)
                return nc.tensor.matmul(out, al, bh, start=False, stop=last)

            def run_units(name, prog, operand=None):
                for j in range(COUNT[name]):
                    u = FIRST[name] + j
                    claim(u % RING)
                    unit_split(u)
                    for k in range(DC):
                        if operand is not None and j == 0:
                            pe.wait_ge(vector_out, vector_at.find("xl", operand, k))
                        w = slice(k * P, (k + 1) * P)
                        m = products(bank[u % RING][:], (whi[:, u % 2, w], wlo[:, u % 2, w]), (xhi[:, k, :], xlo[:, k, :]), k == 0, k == DC - 1)
                    m.then_inc(units_done, 1)
                    reader[u % RING] = (prog, ("read", name, j))

            def run_moving(name, n, bias_row):
                kk = 8 * P // n
                for tt in range(TILES):
                    claim(tt)
                    if bias_row is not None:
                        nc.tensor.matmul(bank[tt][:, 0:n], ones[0:1, 0:P], bias_row, start=True, stop=False)
                for j in range(COUNT[name]):
                    u = FIRST[name] + j
                    unit_split(u)
                    for tt in range(TILES):
                        for q in range(kk):
                            k, t, w = j * kk + q, slice(tt * P, (tt + 1) * P), slice(q * n, (q + 1) * n)
                            m = products(bank[tt][:, 0:n], (xhi[:, k, t], xlo[:, k, t]), (whi[:, u % 2, w], wlo[:, u % 2, w]), k == 0 and bias_row is None, k == DC - 1)
                    m.then_inc(units_done, 1)
                for tt in range(TILES):
                    reader[tt] = (VECTOR, ("read", name, tt))

            def norm(name, chunks, n, xs, sq, mean):
                if mean:
                    claim(6)
                    for k in range(chunks):
                        pe.wait_ge(vector_out, vector_at.find(name, "x", k))
                        m = nc.tensor.matmul(bank[6][:], inv[n][:], xs[:, k, :], start=k == 0, stop=k == chunks - 1)
                    m.then_inc(tensor_out, tensor_at.next(name, "mean"))
                    reader[6] = (VECTOR, (name, "centred"))
                claim(7)
                for k in range(chunks):
                    pe.wait_ge(scalar_out, scalar_at.find(name, "sq", k))
                    m = nc.tensor.matmul(bank[7][:], inv[n][:], sq[:, k, :], start=k == 0, stop=k == chunks - 1)
                m.then_inc(tensor_out, tensor_at.next(name, "ms"))
                reader[7] = (SCALAR, (name, "root"))

            def item_norms(name, items, mat, xs, sqs, mean):
                for k in range(items + 1):
                    if k < items and mean:
                        claim(6)
                        nc_m = nc.tensor.matmul(bank[6][:], mat[:, 0:P], xs(k), start=True, stop=True)
                        nc_m.then_inc(tensor_out, tensor_at.next(name, "mean", k))
                        reader[6] = (VECTOR, (name, "centred", k))
                    if k >= 1:
                        claim(7)
                        pe.wait_ge(scalar_out, scalar_at.find(name, "sq", k - 1))
                        nc_m = nc.tensor.matmul(bank[7][:], mat[:, 0:P], sqs(k - 1), start=True, stop=True)
                        nc_m.then_inc(tensor_out, tensor_at.next(name, "ms", k - 1))
                        reader[7] = (SCALAR, (name, "root", k - 1))

            def attention(name, steps):
                N = len(steps)
                for n in range(N + 3):
                    if n < N:
                        st, b = steps[n], 2 + n % 3
                        claim(b)
                        W = st["w"]
                        nc.tensor.matmul(bank[b][:, 0:W], st["q"], st["k"], start=True, stop=False)
                        for x, (l, r, c0, c1) in enumerate(st["more"]):
                            m = nc.tensor.matmul(bank[b][:, c0:c1], l, r, start=False, stop=x == len(st["more"]) - 1)
                        m.then_inc(tensor_out, tensor_at.next(name, "logits", n))
                        reader[b] = (SCALAR, (name, "exp", n))
                    if 2 <= n < N + 2:
                        k, st = n - 2, steps[n - 2]
                        b = 5 + k % 2
                        claim(b)
                        pe.wait_ge(vector_out, vector_at.find(name, "p", k))
                        for j in range(st["w"] // P):
                            m = nc.tensor.transpose(bank[b][:, j * P:(j + 1) * P], st["ps"][:, j * P:(j + 1) * P], ident)
                        m.then_inc(tensor_out, tensor_at.next(name, "t", k))
                        reader[b] = (SCALAR, (name, "pt", k))
                    if n >= 3:
                        k, st = n - 3, steps[n - 3]
                        b = st["ob"]
                        if st["claim"]:
                            claim(b)
                        pe.wait_ge(scalar_out, scalar_at.find(name, "pt", k))
                        J = st["w"] // P
                        for j in range(J):
                            m = nc.tensor.matmul(bank[b][:, st["oc"]:st["oc"] + P], st["v"][j], st["ts"][:, j * P:(j + 1) * P],
                                                 start=st["start"] and j == 0, stop=st["stop"] and j == J - 1)
                        m.then_inc(tensor_out, tensor_at.next(name, "pv", k))
                        if st["last"]:
                            reader[b] = (SCALAR, (name, "o", st["o"]))

            def decayed(name, steps, extra=None):
                N = len(steps)
                for n in range(N + 2):
                    if n < N:
                        st = steps[n]
                        c0 = st["j"] * P
                        W = SEQ - c0
                        b = 2 + n % 2
                        claim(b)
                        nc.tensor.matmul(bank[b][:, 0:W], st["sel"], st["rows"], start=True, stop=False)
                        m = nc.tensor.matmul(bank[b][:, 0:P], idb[:], mtb[:], start=False, stop=True)
                        m.then_inc(tensor_out, tensor_at.next(name, "e", n))
                        reader[b] = (SCALAR, (name, "w", n))
                        b = 4 + n % 2
                        claim(b)
                        m = nc.tensor.matmul(bank[b][:, 0:W], st["k"], st["q"], start=True, stop=True)
                        m.then_inc(tensor_out, tensor_at.next(name, "s", n))
                        reader[b] = (VECTOR, (name, "p", n))
                        if st["first"] and extra is not None:
                            extra(st)
                    if n >= 2:
                        k, st = n - 2, steps[n - 2]
                        c0 = st["j"] * P
                        if st["first"]:
                            claim(st["num"])
                            if st["den"] is not None:
                                claim(st["den"])
                        pe.wait_ge(vector_out, vector_at.find(name, "p", k))
                        p = scratch[:, 3 + k % 3, 0:SEQ - c0]
                        m = nc.tensor.matmul(bank[st["num"]][:, c0:], st["v"], p, start=st["first"], stop=st["last"])
                        if st["den"] is not None:
                            m = nc.tensor.matmul(bank[st["den"]][:, c0:], ones[:, 0:P], p, start=st["first"], stop=st["last"])
                        m.then_inc(tensor_out, tensor_at.next(name, "pv", k))
                        if st["last"]:
                            reader[st["num"]] = (VECTOR, (name, "fin", st["out"]))
                            if st["den"] is not None:
                                reader[st["den"]] = (VECTOR, (name, "fin", st["out"]))

            def ffn(l, operand):
                up, down = f"up{l}", f"down{l}"
                u0, d0 = FIRST[up], FIRST[down]
                for s in range(RING):
                    claim(s)
                pe.wait_ge(vector_out, vector_at.find("xl", operand, DC - 1))
                with pe.Fori(0, 2 * FC // RING) as i:
                    for s in range(RING):
                        b, t = (u0 + s) % RING, (u0 + s) % 2
                        pe.wait_ge(wlo_done, RING * i + (u0 + s + 1))
                        pe.wait_ge(conv_done, RING * i + l * 2 * FC + s + 1)
                        for k in range(DC):
                            w = slice(k * P, (k + 1) * P)
                            m = products(bank[b][:], (whi[:, t, w], wlo[:, t, w]), (xhi[:, k, :], xlo[:, k, :]), k == 0, k == DC - 1)
                        m.then_inc(units_done, 1)
                pe.wait_ge(conv_done, RING + (l + 1) * 2 * FC)
                for b in range(4, 8):
                    claim(b)

                def unit(u, weights, hidden, h, start, stop):
                    pe.wait_ge(wlo_done, weights)
                    pe.wait_ge(hlo_done, hidden)
                    for n in range(DC):
                        w = slice(n * P, (n + 1) * P)
                        m = products(bank[n][:], (whi[:, u % 2, w], wlo[:, u % 2, w]), (xhi[:, h, :], xlo[:, h, :]), start, stop)
                    m.then_inc(units_done, 1)

                unit(d0, d0 + 1, l * FC + 1, 0, True, False)
                with pe.Fori(0, (FC - 2) // RING) as i:
                    for s in range(RING):
                        unit(d0 + 1 + s, RING * i + (d0 + 2 + s), RING * i + (l * FC + 2 + s), (1 + s) % 2, False, False)
                unit(d0 + FC - 1, d0 + FC, (l + 1) * FC, (FC - 1) % 2, False, True)
                for b in range(8):
                    reader[b] = (VECTOR, ("read", down, b))

            def columns(name, parts, n):
                claim(4)
                pe.wait_ge(vector_out, vector_at.find(name, "rows"))
                pe.wait_ge(scalar_out, scalar_at.find(name, "rows"))
                for c0, src in parts:
                    m = nc.tensor.matmul(bank[4][:, c0:c0 + n], src, con[0:n, K_ID:K_ID + n], start=True, stop=True)
                m.then_inc(tensor_out, tensor_at.next(name, "cols"))
                reader[4] = (VECTOR, (name, "cols"))

            pe.wait_ge(in_sem, 16 * nloads)
            pe.wait_ge(gpsimd_out, gpsimd_at.find("setup"))
            pe.wait_ge(vector_out, vector_at.find("setup"))
            run_units("small0", SCALAR, "x")
            run_units("mq", VECTOR)
            run_units("mk", SCALAR)
            run_moving("mv", HALF, bias_v[:, 0, :])
            run_units("fq", VECTOR)
            run_units("fk", SCALAR)
            run_moving("fv", HALF, bias_v[:, 1, :])
            run_units("mo", SCALAR)
            columns("gate0", [(tt * 4, row[62][0:4, tt * P:(tt + 1) * P]) for tt in range(TILES)], 4)
            stage_end(pe, tensor_at, "in0")

            def minus_m(st):
                claim(6)
                m = nc.tensor.matmul(bank[6][:], st["sel"], row[60][0:4, :], start=True, stop=True)
                m.then_inc(tensor_out, tensor_at.next("ml", "m", st["out"]))
                reader[6] = (SCALAR, ("ml", "em", st["out"]))

            decayed("ml", ml_steps, minus_m)
            item_norms("hn", 4, inv[128], lambda k: MIX[:, k, :], lambda k: scratch[:, 6 + k % 2, :], True)
            stage_end(pe, tensor_at, "ml")
            attention("fox", fox_steps)
            stage_end(pe, tensor_at, "mix0")
            run_units("out0", VECTOR, "mix0")
            norm("ln1_0", DC, 1024, X, MIX, True)
            stage_end(pe, tensor_at, "ln1_0")
            if on("up0"):
                ffn(0, "ln1_0")
                norm("ln2_0", DC, 1024, X, MIX, True)
                stage_end(pe, tensor_at, "ln2_0")
            if on("small1"):
                run_units("small1", SCALAR, "ln2_0")
                run_units("xbc", VECTOR)
                run_units("pool", SCALAR)
                run_units("z1", SCALAR)
                columns("gate1", [(tt * 8, row[58][0:8, tt * P:(tt + 1) * P]) for tt in range(TILES)]
                        + [(32 + tt * 8, row[60 + tt][0:8, tt * P:(tt + 1) * P]) for tt in range(TILES)], 8)
                for c in range(4):
                    claim(4 + c % 2)
                    pe.wait_ge(scalar_out, scalar_at.find("xbc", c))
                    for tt in range(TILES):
                        m = nc.tensor.transpose(bank[4 + c % 2][:, tt * P:(tt + 1) * P], xbc[:, c, tt * P:(tt + 1) * P], ident)
                    m.then_inc(tensor_out, tensor_at.next("xt", c))
                    reader[4 + c % 2] = (VECTOR, ("xp", c))
                for g in range(4):
                    claim(6)
                    pe.wait_ge(vector_out, vector_at.find("pooled", g))
                    m = nc.tensor.matmul(bank[6][:], pw[:, g, :], U[:, 4 + g, :], start=True, stop=True)
                    m.then_inc(tensor_out, tensor_at.next("poolmm", g))
                    reader[6] = (VECTOR, ("poolout", g))
                stage_end(pe, tensor_at, "in1")
                decayed("ssd", ssm_steps)
                norm("ssmn", 4, 512, ys, MIX, False)
                stage_end(pe, tensor_at, "mix1")
                run_units("out1", VECTOR, "mix1")
                norm("ln1_1", DC, 1024, X, MIX, True)
                stage_end(pe, tensor_at, "ln1_1")
            if on("up1"):
                ffn(1, "ln1_1")
                norm("ln2_1", DC, 1024, X, MIX, True)
                stage_end(pe, tensor_at, "ln2_1")
            if on("small2"):
                norm("rms1", DC, 1024, X, MIX, False)
                stage_end(pe, tensor_at, "rms1")
                run_units("small2", SCALAR, "rms1")
                run_units("ik", VECTOR)
                run_units("iq", SCALAR)
                columns("gate2", [(c * 40 + 8 * x, row[r][0:8, c * P:(c + 1) * P]) for x, r in enumerate((62, 64, 63, 59, 60)) for c in range(TILES)], 8)
                item_norms("ikn", 1, inv[128], lambda k: row[65], lambda k: arena[:, 52, :], True)
                run_units("dq", SCALAR)
                run_units("dk", SCALAR)
                run_moving("dv", 256, None)
                pe.wait_ge(vector_out, vector_at.find("ikn", "out"))
                n = 0
                for i in range(1, TILES):
                    for h in range(IDX_HEADS):
                        claim(4 + n % 4)
                        m = nc.tensor.matmul(bank[4 + n % 4][:, 0:(i + 1) * P], iq[:, h // 2, i * P:(i + 1) * P], ikp[:, h % 2, 0:(i + 1) * P], start=True, stop=True)
                        m.then_inc(tensor_out, tensor_at.next("idx", n))
                        reader[4 + n % 4] = (SCALAR, ("relu", n))
                        n += 1
                stage_end(pe, tensor_at, "topk")
                attention("dsa", dsa_steps)
                run_units("gateb", SCALAR)
                stage_end(pe, tensor_at, "dsa")
            if on("gqkv"):
                run_units("gqkv", VECTOR)
                item_norms("l2", 16, ones, lambda k: arena[:, 24 + k, :], lambda k: arena[:, 48 + k % 2, :], False)
                stage_end(pe, tensor_at, "gqkv")

                def four(b, l, r, start=True, stop=True):
                    for hh in range(4):
                        m = nc.tensor.matmul(tile(b)[:, hh, :], l(hh), r(hh), start=start, stop=stop)
                    return m

                for c in range(TILES):
                    cs = slice(c * P, (c + 1) * P)
                    for g in range(2):
                        t = (c, g)
                        G = GW
                        claim(0)
                        for hh in range(4):
                            nc.tensor.matmul(tile(0)[:, hh, :], sel(4 * g + hh), row[62][0:8, cs], start=True, stop=False)
                            m = nc.tensor.matmul(tile(0)[:, hh, :], idb[:], mtb[:], start=False, stop=True)
                        m.then_inc(tensor_out, tensor_at.next("gb", t))
                        reader[0] = (SCALAR, ("gam", t))
                        claim(1)
                        four(1, lambda hh: sel(4 * g + hh), lambda hh: row[62][0:8, cs]).then_inc(tensor_out, tensor_at.next("ge", t))
                        reader[1] = (SCALAR, ("eg", t))
                        claim(2)
                        four(2, lambda hh: sel(4 * g + hh), lambda hh: row[59][0:8, cs]).then_inc(tensor_out, tensor_at.next("bb", t))
                        reader[2] = (VECTOR, ("kb", t))
                        claim(3)
                        four(3, lambda hh: gk[:, 4 * g + hh, cs], lambda hh: gq[:, 4 * g + hh, cs]).then_inc(tensor_out, tensor_at.next("kq", t))
                        reader[3] = (VECTOR, ("att", t))
                        claim(4)
                        for hh in range(4):
                            m = nc.tensor.transpose(tile(4)[:, hh, :], gk[:, 4 * g + hh, cs], ident)
                        m.then_inc(tensor_out, tensor_at.next("kt", t))
                        reader[4] = (SCALAR, ("kd", t))
                        claim(5)
                        for hh in range(4):
                            m = nc.tensor.transpose(tile(5)[:, hh, :], gv[:, 4 * g + hh, cs], ident)
                        m.then_inc(tensor_out, tensor_at.next("vt", t))
                        reader[5] = (SCALAR, ("vb", t))
                        claim(6)
                        pe.wait_ge(vector_out, vector_at.find("kb", t))
                        four(6, lambda hh: gk[:, 4 * g + hh, cs], lambda hh: G["kb"][:, hh, :]).then_inc(tensor_out, tensor_at.next("kk", t))
                        reader[6] = (VECTOR, ("at", t))
                        claim(7)
                        pe.wait_ge(vector_out, vector_at.find("lt", t, 0))
                        for hh in range(4):
                            m = nc.tensor.transpose(tile(7)[:, hh, :], G["lt"][:, hh, :], ident)
                        m.then_inc(tensor_out, tensor_at.next("l0", t))
                        reader[7] = (VECTOR, ("t", t, 0))
                        for r in range(1, LEVELS):
                            claim(0)
                            pe.wait_ge(vector_out, vector_at.find("lt", t, r))
                            pe.wait_ge(vector_out, vector_at.find("t", t, r - 1))
                            four(0, lambda hh: G["lt"][:, hh, :], lambda hh: G["t"][:, hh, :]).then_inc(tensor_out, tensor_at.next("x", t, r))
                            reader[0] = (SCALAR, ("xs", t, r))
                            pe.wait_ge(scalar_out, scalar_at.find("xs", t, r))
                            claim(1)
                            claim(2)
                            pe.wait_ge(vector_out, vector_at.find("u", t, r - 1))
                            m = four(1, lambda hh: G["xs"][:, hh, :], lambda hh: G["u"][:, hh, :])
                            if r < LEVELS - 1:
                                m = four(2, lambda hh: G["u"][:, hh, :], lambda hh: G["xs"][:, hh, :])
                            m.then_inc(tensor_out, tensor_at.next("y", t, r))
                            reader[1] = (VECTOR, ("u", t, r))
                            if r < LEVELS - 1:
                                reader[2] = (VECTOR, ("t", t, r))
                        claim(3)
                        pe.wait_ge(scalar_out, scalar_at.find("kd", t))
                        pe.wait_ge(vector_out, vector_at.find("u", t, LEVELS - 1))
                        four(3, lambda hh: G["kbe"][:, hh, :], lambda hh: G["u"][:, hh, :]).then_inc(tensor_out, tensor_at.next("w", t))
                        reader[3] = (SCALAR, ("nw", t))
                        claim(4)
                        pe.wait_ge(scalar_out, scalar_at.find("nw", t))
                        for hh in range(4):
                            m = nc.tensor.matmul(tile(4)[:, hh, :], G["u"][:, hh, :], G["vb"][:, hh, :], start=True, stop=c == 0)
                            if c:
                                m = nc.tensor.matmul(tile(4)[:, hh, :], G["nw"][:, hh, :], state[:, g, hh, :], start=False, stop=True)
                        m.then_inc(tensor_out, tensor_at.next("vn", t))
                        reader[4] = (SCALAR, ("vn", t))
                        claim(5)
                        claim(6)
                        pe.wait_ge(scalar_out, scalar_at.find("vn", t))
                        pe.wait_ge(vector_out, vector_at.find("qg", t))
                        for hh in range(4):
                            m = nc.tensor.matmul(tile(5)[:, hh, :], G["vn"][:, hh, :], G["att"][:, hh, :], start=True, stop=c == 0)
                            if c:
                                m = nc.tensor.matmul(tile(5)[:, hh, :], state[:, g, hh, :], G["qg"][:, hh, :], start=False, stop=True)
                        m.then_inc(tensor_out, tensor_at.next("o", t))
                        reader[5] = (SCALAR, ("o", t))
                        four(6, lambda hh: G["kd"][:, hh, :], lambda hh: G["vn"][:, hh, :]).then_inc(tensor_out, tensor_at.next("s", t))
                        reader[6] = (VECTOR, ("s", t))
                stage_end(pe, tensor_at, "gdn")
                item_norms("gn", 8, inv[128], lambda k: go[:, k, :], lambda k: arena[:, 32 + k % 2, :], False)
                run_units("z2", SCALAR, "again")
                run_units("gatea", SCALAR)
                stage_end(pe, tensor_at, "mix2")
                run_units("out2", VECTOR, "mix2")
                norm("rms2", DC, 1024, X, gq, False)
                stage_end(pe, tensor_at, "rms2")
            if on("up2"):
                ffn(2, "rms2")
                norm("rmsf", DC, 1024, X, MIX, False)

        @block.scalar
        def _(act):
            A = nc.scalar.activation

            split = [0]

            def split_units(end):
                for v in range(split[0], min(end, last_unit + 1) + 1):
                    act.wait_ge(ring_sem[v % RING], 16 * (v // RING + 1))
                    if v >= 2:
                        act.wait_ge(units_done, v - 1)
                    A(whi[:, v % 2, :], ring[:, v % RING, :], ACT.Copy).then_inc(whi_done, 1)
                split[0] = max(split[0], end + 1)

            def passing(name):
                split_units(FIRST[name] + COUNT[name] + 1)

            def unit_done(name, j):
                split_units(FIRST[name] + j + 2)
                act.wait_ge(units_done, FIRST[name] + j + 1)

            def split_operand(name, src, ready=None):
                for k in range(DC):
                    if ready is not None:
                        act.wait_ge(vector_out, vector_at.find(*ready, k))
                    A(xhi[:, k, :], src[:, k, :], ACT.Copy).then_inc(scalar_out, scalar_at.next("xh", name, k))

            def evac(name, func, dst, bias=0.0, scale=1.0, wait=None):
                for j in range(COUNT[name]):
                    unit_done(name, j)
                    if wait is not None:
                        wait(j)
                    b = bias(j) if callable(bias) else bias
                    A(dst(j), bank[(FIRST[name] + j) % RING][:], func, bias=b, scale=scale).then_inc(scalar_out, scalar_at.next("read", name, j))

            def root(b, dst, eps, *key):
                e = small[:, 250:251] if eps == LN_EPS else small[:, 251:252]
                A(dst, bank[b][:], ACT.Sqrt, bias=e).then_inc(scalar_out, scalar_at.next(*key))

            def norm(name, chunks, xs, sq, mean, eps, affine=None):
                for k in range(chunks):
                    act.wait_ge(vector_out, vector_at.find(name, "xc" if mean else "x", k))
                    A(sq[:, k, :], xs[:, k, :], ACT.Square).then_inc(scalar_out, scalar_at.next(name, "sq", k))
                act.wait_ge(tensor_out, tensor_at.find(name, "ms"))
                root(7, RSTD, eps, name, "root")
                if affine is not None:
                    for k in range(chunks):
                        act.wait_ge(vector_out, vector_at.find(name, "scaled", k))
                        A(X[:, k, :], U[:, k, :], ACT.Identity, bias=col(affine[1], k), scale=col(affine[0], k)).then_inc(scalar_out, scalar_at.next(name, "out", k))
                        A(xhi[:, k, :], U[:, k, :], ACT.Identity, bias=col(affine[1], k), scale=col(affine[0], k)).then_inc(scalar_out, scalar_at.next("xh", name, k))

            def item_norms(name, items, xs, sqs, mean, eps, tmp):
                for k in range(items + 1):
                    if k < items:
                        if mean:
                            act.wait_ge(vector_out, vector_at.find(name, "xc", k))
                        if k >= 2:
                            act.wait_ge(tensor_out, tensor_at.find(name, "ms", k - 2))
                        A(sqs(k), xs(k), ACT.Square).then_inc(scalar_out, scalar_at.next(name, "sq", k))
                    if k >= 1:
                        act.wait_ge(tensor_out, tensor_at.find(name, "ms", k - 1))
                        if k >= 3:
                            act.wait_ge(vector_out, vector_at.find(name, "out", k - 3))
                        root(7, tmp(k - 1), eps, name, "root", k - 1)

            def attention(name, steps):
                N = len(steps)
                for n in range(N + 3):
                    if n < N:
                        st, W = steps[n], steps[n]["w"]
                        act.wait_ge(vector_out, vector_at.find(name, "max", n))
                        if n >= 4:
                            act.wait_ge(tensor_out, tensor_at.find(name, "t", n - 4))
                        A(st["ps"][:, 0:W], bank[2 + n % 3][:, 0:W], ACT.Exp, bias=small[:, 200 + n % 4:201 + n % 4],
                                     accum_out=small[:, 204 + n % 4:205 + n % 4]).then_inc(scalar_out, scalar_at.next(name, "exp", n))
                    if 2 <= n < N + 2:
                        k, st = n - 2, steps[n - 2]
                        act.wait_ge(tensor_out, tensor_at.find(name, "t", k))
                        if k >= 3:
                            act.wait_ge(tensor_out, tensor_at.find(name, "pv", k - 3))
                        A(st["ts"][:, 0:st["w"]], bank[5 + k % 2][:, 0:st["w"]], ACT.Copy).then_inc(scalar_out, scalar_at.next(name, "pt", k))
                    if n >= 3 and steps[n - 3]["last"]:
                        st = steps[n - 3]
                        act.wait_ge(tensor_out, tensor_at.find(name, "pv", n - 3))
                        A(MIX[:, st["dst"], :], bank[st["ob"]][:], ACT.Copy).then_inc(scalar_out, scalar_at.next(name, "o", st["o"]))

            def decayed(name, steps, extra=None):
                for n, st in enumerate(steps):
                    W = SEQ - st["j"] * P
                    act.wait_ge(tensor_out, tensor_at.find(name, "e", n))
                    if n >= 3:
                        act.wait_ge(vector_out, vector_at.find(name, "p", n - 3))
                    A(scratch[:, n % 3, 0:W], bank[2 + n % 2][:, 0:W], ACT.Exp, bias=st["bias"]).then_inc(scalar_out, scalar_at.next(name, "w", n))
                    if st["first"] and extra is not None:
                        extra(st)

            def ffn(l):
                u0, d0, c0 = FIRST[f"up{l}"], FIRST[f"down{l}"], COL[f"ffn{l}"]
                split_units(u0 + 1)

                def weights(v, n, done):
                    act.wait_ge(ring_sem[v % RING], n * 16 + 16 * (v // RING + 1))
                    act.wait_ge(units_done, done)
                    A(whi[:, v % 2, :], ring[:, v % RING, :], ACT.Copy).then_inc(whi_done, 1)

                with act.Fori(0, 2 * FC // RING) as i:
                    for s in range(RING):
                        b = (u0 + s) % RING
                        weights(u0 + s + 2, i, RING * i + (u0 + s + 1))
                        act.wait_ge(hid_done, 2 * i + 1 + l * FC + s // 2)
                        A(acc[:, s, :], bank[b][:], ACT.Identity, bias=par[:, bass.ds(4 * RING * i + (c0 + 4 * s + 3), 1)],
                          scale=par[:, bass.ds(4 * RING * i + (c0 + 4 * s + 2), 1)]).then_inc(acc_done, 1)
                        if s % 2:
                            act.wait_ge(conv_done, RING * i + (4 + 2 * l * FC + s))
                            A(sg[:, s // 2, :], acc[:, s - 1, :], ACT.Silu).then_inc(gate_done, 1)
                for k in range(2):
                    act.wait_ge(hid_done, 3 + l * FC + k)
                    A(xhi[:, k, :], hid[:, k, :], ACT.Copy).then_inc(hhi_done, 1)
                weights(d0 + 2, 0, d0 + 1)
                act.wait_ge(hid_done, 2 + (l + 1) * FC)
                with act.Fori(0, (FC - 2) // RING) as i:
                    for s in range(RING):
                        act.wait_ge(units_done, RING * i + (d0 + s + 1))
                        A(xhi[:, s % 2, :], hid[:, bass.ds(RING * i + s + 2, 1), :].rearrange("p a n -> p (a n)"), ACT.Copy).then_inc(hhi_done, 1)
                        weights(d0 + s + 3, i, RING * i + (d0 + s + 2))
                split[0] = d0 + FC + 1
                split_units(d0 + FC + 1)

            def softplus_tail(name):
                act.wait_ge(vector_out, vector_at.find(name, "abs"))
                A(row[57], row[57], ACT.Exp).then_inc(scalar_out, scalar_at.next())
                act.wait_ge(scalar_out, scalar_at.n)
                A(row[57], row[57], ACT.Ln, bias=1.0).then_inc(scalar_out, scalar_at.next(name, "ln"))

            act.wait_ge(in_sem, 16 * nloads)
            act.wait_ge(gpsimd_out, gpsimd_at.find("setup"))
            split_units(1)
            split_operand("x", X)
            evac("small0", ACT.Identity, lambda j: row[56], bias=lambda j: col("b_small0"))
            softplus_tail("gate0")
            scalar_at.mark("gate0", "rows")
            for j in range(4):
                unit_done("mk", j)
                A(mk[:, j, :], bank[(FIRST["mk"] + j) % RING][:], ACT.Identity, bias=col("b_mk", j)).then_inc(scalar_out, scalar_at.next("read", "mk", j))
            for j in range(4):
                unit_done("fk", j)
                for e in range(2):
                    p0 = 64 * e
                    A(fk[p0:p0 + 64, 2 * j + e, :], bank[(FIRST["fk"] + j) % RING][p0:p0 + 64, :], ACT.Identity, bias=col("b_fk", j, p0, p0 + 64)).then_inc(scalar_out, scalar_at.next("read", "fk", j))
            evac("mo", ACT.Sigmoid, lambda j: gate[:, j, :], bias=lambda j: col("b_mo", j))
            stage_end(act, scalar_at, "in0")

            def exp_minus_m(st):
                h = st["out"]
                act.wait_ge(tensor_out, tensor_at.find("ml", "m", h))
                if h >= 2:
                    act.wait_ge(vector_out, vector_at.find("ml", "fin", h - 2))
                A(scratch[:, 8 + h % 2, :], bank[6][:], ACT.Exp).then_inc(scalar_out, scalar_at.next("ml", "em", h))

            decayed("ml", ml_steps, exp_minus_m)
            item_norms("hn", 4, lambda k: MIX[:, k, :], lambda k: scratch[:, 6 + k % 2, :], True, LN_EPS, lambda k: scratch[:, 10 + k % 2, :])
            stage_end(act, scalar_at, "ml")
            attention("fox", fox_steps)
            stage_end(act, scalar_at, "mix0")
            split_operand("mix0", MIX)
            passing("out0")
            norm("ln1_0", DC, U, MIX, True, LN_EPS, ("ln1_g0", "ln1_b0"))
            stage_end(act, scalar_at, "ln1_0")
            if on("up0"):
                ffn(0)
                norm("ln2_0", DC, U, MIX, True, LN_EPS, ("ln2_g0", "ln2_b0"))
                stage_end(act, scalar_at, "ln2_0")
            if on("small1"):
                A(small[0:8, 208:209], par[0:8, COL["a_log"]:COL["a_log"] + 1], ACT.Exp).then_inc(scalar_out, scalar_at.next("ea1"))
                evac("small1", ACT.Identity, lambda j: row[56], bias=lambda j: col("dt_bias"))
                softplus_tail("gate1")
                scalar_at.mark("gate1", "rows")
                for j in range(8 + 1):
                    if j < 8:
                        unit_done("xbc", j)
                        A(xbc[:, j, :], bank[(FIRST["xbc"] + j) % RING][:], ACT.Identity, bias=col("xbc_conv", 5 * j + 4), scale=col("xbc_conv", 5 * j + 3)).then_inc(scalar_out, scalar_at.next("xa", j))
                    if j >= 1:
                        act.wait_ge(vector_out, vector_at.find("read", "xbc", j - 1))
                        A(xbc[:, j - 1, :], xbc[:, j - 1, :], ACT.Silu).then_inc(scalar_out, scalar_at.next("xbc", j - 1))
                act.wait_ge(gpsimd_out, gpsimd_at.find("pads1"))
                evac("pool", ACT.Copy, lambda j: pbuf[j][:, 16:16 + SEQ])
                evac("z1", ACT.Silu, lambda j: gate[:, j, :])
                stage_end(act, scalar_at, "in1")
                decayed("ssd", ssm_steps)
                norm("ssmn", 4, ys, MIX, False, LN_EPS)
                stage_end(act, scalar_at, "mix1")
                split_operand("mix1", MIX)
                passing("out1")
                norm("ln1_1", DC, U, MIX, True, LN_EPS, ("ln1_g1", "ln1_b1"))
                stage_end(act, scalar_at, "ln1_1")
            if on("up1"):
                ffn(1)
                norm("ln2_1", DC, U, MIX, True, LN_EPS, ("ln2_g1", "ln2_b1"))
                stage_end(act, scalar_at, "ln2_1")
            if on("small2"):
                norm("rms1", DC, X, MIX, False, RMS_EPS)
                split_operand("rms1", U, ("rms1", "out"))
                stage_end(act, scalar_at, "rms1")
                A(small[0:8, 208:209], par[0:8, COL["g_a_log"]:COL["g_a_log"] + 1], ACT.Exp).then_inc(scalar_out, scalar_at.next("ea2"))
                unit_done("small2", 0)
                b = bank[FIRST["small2"] % RING]
                A(row[56], b[:], ACT.Identity, bias=col("g_dt_bias")).then_inc(scalar_out, scalar_at.next("pre2"))
                A(row[60][0:8, :], b[64:72, :], ACT.Copy, scale=(IDX_HEADS ** -0.5) * (64 ** -0.5)).then_inc(scalar_out, scalar_at.next())
                A(row[59][0:8, :], b[32:40, :], ACT.Sigmoid).then_inc(scalar_out, scalar_at.next("read", "small2", 0))
                softplus_tail("gate2")
                act.wait_ge(vector_out, vector_at.find("dG"))
                A(row[63][0:8, :], row[63][0:8, :], ACT.Exp).then_inc(scalar_out, scalar_at.next())
                A(row[64][0:8, :], row[62][0:8, :], ACT.Exp).then_inc(scalar_out, scalar_at.next("eG"))
                scalar_at.mark("gate2", "rows")
                evac("iq", ACT.Copy, lambda j: iq[:, j, :])
                act.wait_ge(vector_out, vector_at.find("ikn", "x", 0))
                item_norms("ikn", 1, lambda k: row[65], lambda k: arena[:, 52, :], True, RMS_EPS, lambda k: RSTD)
                evac("dq", ACT.Copy, lambda j: dq[:, j, :], scale=P ** -0.5)
                evac("dk", ACT.Copy, lambda j: dk[:, j, :])
                passing("dv")
                n = 0
                for i in range(1, TILES):
                    for h in range(IDX_HEADS):
                        act.wait_ge(tensor_out, tensor_at.find("idx", n))
                        if n >= 4:
                            act.wait_ge(vector_out, vector_at.find("sc", n - 4))
                        A(arena[:, 48 + n % 4, 0:(i + 1) * P], bank[4 + n % 4][:, 0:(i + 1) * P], ACT.Relu).then_inc(scalar_out, scalar_at.next("relu", n))
                        n += 1
                stage_end(act, scalar_at, "topk")
                attention("dsa", dsa_steps)
                evac("gateb", ACT.Sigmoid, lambda j: arena[:, 48 + j % 4, :], bias=lambda j: col("gate_b", 8 + j),
                     wait=lambda j: act.wait_ge(vector_out, vector_at.find("gateb", j - 4)) if j >= 4 else act.wait_ge(tensor_out, tensor_at.find("dsa", "pv", len(dsa_steps) - 1)))
                stage_end(act, scalar_at, "dsa")
            if on("gqkv"):
                for j in range(24 + 1):
                    if j < 24:
                        unit_done("gqkv", j)
                        A(arena[:, 24 + j, :], bank[(FIRST["gqkv"] + j) % RING][:], ACT.Copy, scale=col("gqkv_conv", 4 * j + 3)).then_inc(scalar_out, scalar_at.next("ga", j))
                    if j >= 1:
                        act.wait_ge(vector_out, vector_at.find("read", "gqkv", j - 1))
                        A(arena[:, 23 + j, :], arena[:, 23 + j, :], ACT.Silu).then_inc(scalar_out, scalar_at.next("gqkv", j - 1))
                act.wait_ge(scalar_out, scalar_at.n)
                item_norms("l2", 16, lambda k: arena[:, 24 + k, :], lambda k: arena[:, 48 + k % 2, :], False, RMS_EPS, lambda k: arena[:, 50 + k % 2, :])
                stage_end(act, scalar_at, "gqkv")
                for c in range(TILES):
                    for g in range(2):
                        t, G = (c, g), GW

                        def cc(x, hh):
                            return small[:, c * 40 + 8 * x + 4 * g + hh:c * 40 + 8 * x + 4 * g + hh + 1]

                        act.wait_ge(tensor_out, tensor_at.find("gb", t))
                        if t != (0, 0):
                            act.wait_ge(vector_out, vector_at.find("s", (c, 0) if g else (c - 1, 1)))
                        for hh in range(4):
                            ng = small[:, 160 + c * 8 + 4 * g + hh:161 + c * 8 + 4 * g + hh]
                            A(G["gam"][:, hh, :], tile(0)[:, hh, :], ACT.Exp, bias=ng).then_inc(scalar_out, scalar_at.next("gam", t))
                        act.wait_ge(tensor_out, tensor_at.find("ge", t))
                        A(G["eg"], tile(1), ACT.Exp).then_inc(scalar_out, scalar_at.next("eg", t))
                        act.wait_ge(tensor_out, tensor_at.find("kt", t))
                        for hh in range(4):
                            A(G["kbe"][:, hh, :], tile(4)[:, hh, :], ACT.Copy, scale=cc(1, hh)).then_inc(scalar_out, scalar_at.next())
                            A(G["kd"][:, hh, :], tile(4)[:, hh, :], ACT.Copy, scale=cc(2, hh)).then_inc(scalar_out, scalar_at.next("kd", t))
                        act.wait_ge(tensor_out, tensor_at.find("vt", t))
                        for hh in range(4):
                            A(G["vb"][:, hh, :], tile(5)[:, hh, :], ACT.Copy, scale=cc(3, hh)).then_inc(scalar_out, scalar_at.next("vb", t))
                        for r in range(1, LEVELS):
                            act.wait_ge(tensor_out, tensor_at.find("x", t, r))
                            A(G["xs"], tile(0), ACT.Copy).then_inc(scalar_out, scalar_at.next("xs", t, r))
                        act.wait_ge(tensor_out, tensor_at.find("w", t))
                        A(G["nw"], tile(3), ACT.Copy, scale=-1.0).then_inc(scalar_out, scalar_at.next("nw", t))
                        act.wait_ge(tensor_out, tensor_at.find("vn", t))
                        A(G["vn"], tile(4), ACT.Copy).then_inc(scalar_out, scalar_at.next("vn", t))
                        act.wait_ge(tensor_out, tensor_at.find("o", t))
                        A(go[:, 4 * g:4 * g + 4, c * P:(c + 1) * P], tile(5), ACT.Copy).then_inc(scalar_out, scalar_at.next("o", t))
                stage_end(act, scalar_at, "gdn")
                split_operand("again", U)
                item_norms("gn", 8, lambda k: go[:, k, :], lambda k: arena[:, 32 + k % 2, :], False, RMS_EPS, lambda k: arena[:, 34 + k % 2, :])
                evac("z2", ACT.Silu, lambda j: arena[:, 24 + j, :])
                evac("gatea", ACT.Sigmoid, lambda j: arena[:, 24 + j, :], bias=lambda j: col("gate_b", j), wait=lambda j: act.wait_ge(vector_out, vector_at.find("z2", j)))
                stage_end(act, scalar_at, "mix2")
                split_operand("mix2", MIX)
                passing("out2")
                norm("rms2", DC, X, gq, False, RMS_EPS)
                split_operand("rms2", U, ("rms2", "out"))
                stage_end(act, scalar_at, "rms2")
            if on("up2"):
                ffn(2)
                norm("rmsf", DC, X, MIX, False, RMS_EPS)
            src = U if on("up2") else X
            for k in range(DC):
                if on("up2"):
                    act.wait_ge(vector_out, vector_at.find("rmsf", "out", k))
                act.dma_start(out[:, k, :], src[:, k, :]).then_inc(out_sem, 16)
            act.wait_ge(out_sem, 16 * DC)

        @block.gpsimd
        def _(pool):
            for n in (128, 512, 1024):
                nc.gpsimd.memset(inv[n][:], 1.0 / n).then_inc(gpsimd_out, gpsimd_at.next())
            nc.gpsimd.memset(ones[:], 1.0).then_inc(gpsimd_out, gpsimd_at.next())
            nc.gpsimd.memset(small[:, 250:251], LN_EPS).then_inc(gpsimd_out, gpsimd_at.next())
            nc.gpsimd.memset(small[:, 251:252], RMS_EPS).then_inc(gpsimd_out, gpsimd_at.next())
            nc.gpsimd.memset(arena[:, 40:56, :], 0.0).then_inc(gpsimd_out, gpsimd_at.next("setup"))
            gpsimd_at.mark("stage", "in0")
            for st in ("ml", "mix0", "ln1_0"):
                gpsimd_at.mark("stage", st)
            if on("up0"):
                gpsimd_at.mark("stage", "ln2_0")
            if on("small1"):
                pool.wait_ge(tensor_out, tensor_at.find("stage", "ln2_0"))
                pool.wait_ge(scalar_out, scalar_at.find("stage", "ln2_0"))
                pool.wait_ge(vector_out, vector_at.find("stage", "ln2_0"))
                nc.gpsimd.memset(arena[:, 36:56, :], 0.0).then_inc(gpsimd_out, gpsimd_at.next("pads1"))
                for st in ("in1", "mix1", "ln1_1", "ln2_1", "rms1"):
                    gpsimd_at.mark("stage", st)
            if on("small2"):
                pool.wait_ge(tensor_out, tensor_at.find("stage", "rms1"))
                pool.wait_ge(scalar_out, scalar_at.find("stage", "rms1"))
                pool.wait_ge(vector_out, vector_at.find("stage", "rms1"))
                nc.gpsimd.memset(ikp, 0.0).then_inc(gpsimd_out, gpsimd_at.next("pads2"))
                for st in ("topk", "dsa", "gqkv", "gdn", "mix2", "rms2"):
                    gpsimd_at.mark("stage", st)

        @block.vector
        def _(dve):
            V = nc.vector
            STT = nc.vector.scalar_tensor_tensor

            split = [0]

            def split_units(end):
                for v in range(split[0], min(end, last_unit + 1) + 1):
                    dve.wait_ge(whi_done, v + 1)
                    V.tensor_tensor(wlo[:, v % 2, :], ring[:, v % RING, :], whi[:, v % 2, :], ALU.subtract).then_inc(wlo_done, 1)
                split[0] = max(split[0], end + 1)

            def passing(name):
                split_units(FIRST[name] + COUNT[name] + 1)

            def unit_done(name, j):
                split_units(FIRST[name] + j + 2)
                dve.wait_ge(units_done, FIRST[name] + j + 1)

            def split_operand(name, src):
                for k in range(DC):
                    dve.wait_ge(scalar_out, scalar_at.find("xh", name, k))
                    V.tensor_tensor(xlo[:, k, :], src[:, k, :], xhi[:, k, :], ALU.subtract).then_inc(vector_out, vector_at.next("xl", name, k))

            def norm(name, chunks, xs, mean, gain=None, dst=None):
                if mean:
                    dve.wait_ge(tensor_out, tensor_at.find(name, "mean"))
                    for k in range(chunks):
                        V.tensor_tensor(U[:, k, :], xs[:, k, :], bank[6][:], ALU.subtract).then_inc(vector_out, vector_at.next(name, "xc", k))
                    vector_at.mark(name, "centred")
                dve.wait_ge(scalar_out, scalar_at.find(name, "root"))
                V.reciprocal(RSTD, RSTD).then_inc(vector_out, vector_at.next())
                dve.wait_ge(vector_out, vector_at.n)
                for k in range(chunks):
                    if mean:
                        V.tensor_tensor(U[:, k, :], U[:, k, :], RSTD, ALU.mult).then_inc(vector_out, vector_at.next(name, "scaled", k))
                    else:
                        STT(dst[:, k, :], xs[:, k, :], col(gain, k), RSTD, ALU.mult, ALU.mult).then_inc(vector_out, vector_at.next(name, "out", k))
                if mean:
                    split_operand(name, X)

            def residual(name, nxt, factor, last_unit_only):
                for j in range(DC):
                    if last_unit_only:
                        unit_done(name, COUNT[name] - 1)
                        b = j
                    else:
                        unit_done(name, j)
                        b = (FIRST[name] + j) % RING
                    STT(X[:, j, :], X[:, j, :], factor, bank[b][:], ALU.mult, ALU.add).then_inc(vector_out, vector_at.next("read", name, j))
                    vector_at.mark(nxt, "x", j)

            def conv(name, j, dst, u, taps):
                for n, (shift, w) in enumerate(taps):
                    STT(dst[:, shift:], u[:, 0:SEQ - shift], w, dst[:, shift:], ALU.mult, ALU.add).then_inc(vector_out, vector_at.next())
                    if n < len(taps) - 1:
                        dve.wait_ge(vector_out, vector_at.n)
                vector_at.mark("read", name, j)

            def attention(name, steps):
                N = len(steps)
                for n in range(N + 1):
                    if n < N:
                        dve.wait_ge(tensor_out, tensor_at.find(name, "logits", n))
                        if n >= 4:
                            dve.wait_ge(scalar_out, scalar_at.find(name, "exp", n - 4))
                        V.tensor_reduce(small[:, 200 + n % 4:201 + n % 4], bank[2 + n % 3][:, 0:steps[n]["w"]], AX_X, ALU.max, negate=True).then_inc(vector_out, vector_at.next(name, "max", n))
                    if n >= 1:
                        k, st = n - 1, steps[n - 1]
                        dve.wait_ge(scalar_out, scalar_at.find(name, "exp", k))
                        V.reciprocal(small[:, 204 + k % 4:205 + k % 4], small[:, 204 + k % 4:205 + k % 4]).then_inc(vector_out, vector_at.next())
                        dve.wait_ge(vector_out, vector_at.n)
                        p = st["ps"][:, 0:st["w"]]
                        V.tensor_scalar(p, p, small[:, 204 + k % 4:205 + k % 4], None, ALU.mult).then_inc(vector_out, vector_at.next(name, "p", k))

            def decayed(name, steps, finish):
                N = len(steps)
                for n in range(N + 2):
                    if n < N:
                        W = SEQ - steps[n]["j"] * P
                        dve.wait_ge(scalar_out, scalar_at.find(name, "w", n))
                        dve.wait_ge(tensor_out, tensor_at.find(name, "s", n))
                        if n >= 3:
                            dve.wait_ge(tensor_out, tensor_at.find(name, "pv", n - 3))
                        V.tensor_tensor(scratch[:, 3 + n % 3, 0:W], scratch[:, n % 3, 0:W], bank[4 + n % 2][:, 0:W], ALU.mult).then_inc(vector_out, vector_at.next(name, "p", n))
                    if n >= 2 and steps[n - 2]["last"]:
                        dve.wait_ge(tensor_out, tensor_at.find(name, "pv", n - 2))
                        finish(steps[n - 2])

            def ffn(l):
                c0 = COL[f"ffn{l}"]
                u0, d0 = FIRST[f"up{l}"], FIRST[f"down{l}"]
                split_units(u0 + 1)

                def weights(v, high):
                    dve.wait_ge(whi_done, high)
                    V.tensor_tensor(wlo[:, v % 2, :], ring[:, v % RING, :], whi[:, v % 2, :], ALU.subtract).then_inc(wlo_done, 1)

                with dve.Fori(0, 2 * FC // RING) as i:
                    for s in range(RING):
                        weights(u0 + s + 2, RING * i + (u0 + s + 3))
                        u = bank[(u0 + s) % RING]
                        dve.wait_ge(acc_done, RING * i + (2 * l * FC + s + 1))
                        STT(acc[:, s, 1:], u[:, 0:SEQ - 1], par[:, bass.ds(4 * RING * i + (c0 + 4 * s + 1), 1)], acc[:, s, 1:], ALU.mult, ALU.add).then_inc(tap_done, 1)
                        dve.wait_ge(tap_done, RING * i + (2 * l * FC + s + 1))
                        STT(acc[:, s, 2:], u[:, 0:SEQ - 2], par[:, bass.ds(4 * RING * i + (c0 + 4 * s), 1)], acc[:, s, 2:], ALU.mult, ALU.add).then_inc(conv_done, 1)
                        if s % 2:
                            dve.wait_ge(conv_done, RING * i + (4 + 2 * l * FC + s + 1))
                            dve.wait_ge(gate_done, 2 * i + (l * FC + s // 2 + 1))
                            V.tensor_tensor(hid[:, bass.ds(2 * i + s // 2, 1), :].rearrange("p a n -> p (a n)"), sg[:, s // 2, :], acc[:, s, :], ALU.mult).then_inc(hid_done, 1)
                for k in range(2):
                    dve.wait_ge(hhi_done, l * FC + k + 1)
                    V.tensor_tensor(xlo[:, k, :], hid[:, k, :], xhi[:, k, :], ALU.subtract).then_inc(hlo_done, 1)
                weights(d0 + 2, d0 + 3)
                with dve.Fori(0, (FC - 2) // RING) as i:
                    for s in range(RING):
                        dve.wait_ge(hhi_done, RING * i + (l * FC + s + 3))
                        V.tensor_tensor(xlo[:, s % 2, :], hid[:, bass.ds(RING * i + s + 2, 1), :].rearrange("p a n -> p (a n)"), xhi[:, s % 2, :], ALU.subtract).then_inc(hlo_done, 1)
                        weights(d0 + s + 3, RING * i + (d0 + s + 4))
                split[0] = d0 + FC + 1
                split_units(d0 + FC + 1)

            def absolute(name, key):
                dve.wait_ge(scalar_out, scalar_at.find(*key))
                STT(row[57], row[56], -1.0, row[56], ALU.mult, ALU.min).then_inc(vector_out, vector_at.next(name, "abs"))

            dve.wait_ge(in_sem, 16 * nloads)
            V.tensor_copy(idb[:], ident).then_inc(vector_out, vector_at.next())
            V.tensor_copy(mtb[:], con[:, K_MT:K_MT + P]).then_inc(vector_out, vector_at.next())
            V.tensor_copy(mqb[:], con[:, K_MQ:K_MQ + P]).then_inc(vector_out, vector_at.next("setup"))
            for n in range(RING):
                V.memset(small[:, 210 + n:211 + n], 0.0).then_inc(conv_done, 1)
            for n in range(2):
                V.memset(small[:, 214 + n:215 + n], 0.0).then_inc(hid_done, 1)
            dve.wait_ge(gpsimd_out, gpsimd_at.find("setup"))

            split_units(1)
            split_operand("x", X)
            absolute("gate0", ("read", "small0", 0))
            dve.wait_ge(scalar_out, scalar_at.find("gate0", "ln"))
            STT(row[58], row[56], 0.0, row[57], ALU.min, ALU.subtract).then_inc(vector_out, vector_at.next())
            dve.wait_ge(vector_out, vector_at.n)
            V.tensor_tensor_scan(row[59], ones[:], row[58], 0.0, ALU.mult, ALU.add).then_inc(vector_out, vector_at.next())
            dve.wait_ge(vector_out, vector_at.n)
            V.tensor_scalar(row[61][0:8, :], row[59][64:72, :], -1.0, None, ALU.mult).then_inc(vector_out, vector_at.next())
            V.tensor_copy(row[60][0:4, :], row[59][32:36, :]).then_inc(vector_out, vector_at.next())
            dve.wait_ge(vector_out, vector_at.n)
            V.tensor_tensor(row[62][0:4, :], row[56][0:4, :], row[60][0:4, :], ALU.subtract).then_inc(vector_out, vector_at.next())
            dve.wait_ge(vector_out, vector_at.n)
            V.tensor_tensor_scan(row[63][0:4, :], row[62][0:4, :], row[62][0:4, :], 0.0, ALU.max, ALU.max).then_inc(vector_out, vector_at.next())
            dve.wait_ge(vector_out, vector_at.n)
            V.tensor_scalar(row[64][0:4, :], row[63][0:4, :], -1.0, None, ALU.mult).then_inc(vector_out, vector_at.next())
            STT(row[60][0:4, :], row[60][0:4, :], -1.0, row[63][0:4, :], ALU.mult, ALU.subtract).then_inc(vector_out, vector_at.next("gate0", "rows"))
            for j in range(4):
                unit_done("mq", j)
                V.tensor_scalar(mq[:, j, :], bank[(FIRST["mq"] + j) % RING][:], col("b_mq", j), P ** -0.5, ALU.add, ALU.mult).then_inc(vector_out, vector_at.next("read", "mq", j))
            for tt in range(TILES):
                unit_done("mv", COUNT["mv"] - 1)
                V.tensor_copy(mv[:, tt, :], bank[tt][:]).then_inc(vector_out, vector_at.next("read", "mv", tt))
            for j in range(4):
                unit_done("fq", j)
                V.tensor_scalar(fq[:, j, :], bank[(FIRST["fq"] + j) % RING][:], col("b_fq", j), 64 ** -0.5, ALU.add, ALU.mult).then_inc(vector_out, vector_at.next("read", "fq", j))
            for tt in range(TILES):
                unit_done("fv", COUNT["fv"] - 1)
                for e in range(2):
                    dst = fv[:, tt, :, :].rearrange("p (c e) d -> p c e d", e=2)[:, :, e, 64 * e:64 * e + 64]
                    src = bank[tt][:].rearrange("p (c e d) -> p c e d", e=2, d=64)[:, :, e, :]
                    V.tensor_copy(dst, src).then_inc(vector_out, vector_at.next("read", "fv", tt))
            passing("mo")
            dve.wait_ge(tensor_out, tensor_at.find("gate0", "cols"))
            V.tensor_copy(small[:, 0:16], bank[4][:, 0:16]).then_inc(vector_out, vector_at.next("gate0", "cols"))
            stage_end(dve, vector_at, "in0")

            def ml_finish(st):
                h, den = st["out"], scratch[:, 12, :]
                dve.wait_ge(scalar_out, scalar_at.find("ml", "em", h))
                STT(den, bank[1][:], -1.0, scratch[:, 8 + h % 2, :], ALU.mult, ALU.max).then_inc(vector_out, vector_at.next())
                dve.wait_ge(vector_out, vector_at.n)
                V.tensor_tensor(den, bank[1][:], den, ALU.max).then_inc(vector_out, vector_at.next())
                dve.wait_ge(vector_out, vector_at.n)
                V.reciprocal(den, den).then_inc(vector_out, vector_at.next())
                dve.wait_ge(vector_out, vector_at.n)
                V.tensor_tensor(MIX[:, h, :], bank[0][:], den, ALU.mult).then_inc(vector_out, vector_at.next("ml", "fin", h))
                vector_at.mark("hn", "x", h)

            decayed("ml", ml_steps, ml_finish)
            dve.wait_ge(vector_out, vector_at.n)

            def item_norms(name, items, xs, mean, write, tmp):
                for k in range(items + 1):
                    if k < items and mean:
                        dve.wait_ge(tensor_out, tensor_at.find(name, "mean", k))
                        V.tensor_tensor(xs(k), xs(k), bank[6][:], ALU.subtract).then_inc(vector_out, vector_at.next(name, "xc", k))
                        vector_at.mark(name, "centred", k)
                    if k >= 1:
                        dve.wait_ge(scalar_out, scalar_at.find(name, "root", k - 1))
                        V.reciprocal(tmp(k - 1), tmp(k - 1)).then_inc(vector_out, vector_at.next())
                        dve.wait_ge(vector_out, vector_at.n)
                        write(k - 1, tmp(k - 1))
                        vector_at.mark(name, "out", k - 1)

            item_norms("hn", 4, lambda k: MIX[:, k, :], True,
                       lambda k, r: STT(MIX[:, k, :], MIX[:, k, :], col("ml_norm", k), r, ALU.mult, ALU.mult).then_inc(vector_out, vector_at.next("hn", "out", k)),
                       lambda k: scratch[:, 10 + k % 2, :])
            stage_end(dve, vector_at, "ml")
            attention("fox", fox_steps)
            for j in range(4):
                dve.wait_ge(scalar_out, scalar_at.find("read", "mo", j))
                V.tensor_tensor(MIX[:, j, :], MIX[:, j, :], gate[:, j, :], ALU.mult).then_inc(vector_out, vector_at.next("mo", j))
            stage_end(dve, vector_at, "mix0")
            split_operand("mix0", MIX)
            residual("out0", "ln1_0", ALPHA, False)
            norm("ln1_0", DC, X, True)
            stage_end(dve, vector_at, "ln1_0")
            if on("up0"):
                ffn(0)
                residual("down0", "ln2_0", ALPHA, True)
                norm("ln2_0", DC, X, True)
                stage_end(dve, vector_at, "ln2_0")
            if on("small1"):
                absolute("gate1", ("read", "small1", 0))
                dve.wait_ge(scalar_out, scalar_at.find("gate1", "ln"))
                STT(row[58], row[56], 0.0, row[57], ALU.max, ALU.add).then_inc(vector_out, vector_at.next())
                dve.wait_ge(vector_out, vector_at.n)
                dve.wait_ge(scalar_out, scalar_at.find("ea1"))
                V.tensor_scalar(row[59][0:8, :], row[58][0:8, :], small[0:8, 208:209], -1.0, ALU.mult, ALU.mult).then_inc(vector_out, vector_at.next())
                dve.wait_ge(vector_out, vector_at.n)
                for j in range(TILES):
                    V.tensor_tensor_scan(row[60 + j][0:8, j * P:], ones[0:8, j * P:], row[59][0:8, j * P:], 0.0, ALU.mult, ALU.add).then_inc(vector_out, vector_at.next())
                vector_at.mark("gate1", "rows")
                for j in range(8):
                    split_units(FIRST["xbc"] + j + 2)
                    dve.wait_ge(scalar_out, scalar_at.find("xa", j))
                    conv("xbc", j, xbc[:, j, :], bank[(FIRST["xbc"] + j) % RING], [(s, col("xbc_conv", 5 * j + 3 - s)) for s in (1, 2, 3)])
                passing("z1")
                dve.wait_ge(tensor_out, tensor_at.find("gate1", "cols"))
                V.tensor_copy(small[:, 0:32], bank[4][:, 0:32]).then_inc(vector_out, vector_at.next())
                V.tensor_scalar(small[:, 32:64], bank[4][:, 32:64], -1.0, None, ALU.mult).then_inc(vector_out, vector_at.next("gate1", "cols"))
                dve.wait_ge(vector_out, vector_at.n)
                dve.wait_ge(gpsimd_out, gpsimd_at.find("pads1"))
                for c in range(4):
                    dve.wait_ge(tensor_out, tensor_at.find("xt", c))
                    for tt in range(TILES):
                        for e in range(2):
                            h = 2 * c + e
                            V.tensor_scalar(xpad[:, tt, h, 64 * e:64 * e + 64], bank[4 + c % 2][:, tt * P + 64 * e:tt * P + 64 * e + 64],
                                                       small[:, tt * 8 + h:tt * 8 + h + 1], None, ALU.mult).then_inc(vector_out, vector_at.next("xp", c))
                for g, w in enumerate(POOL_WINDOWS):
                    dve.wait_ge(scalar_out, scalar_at.find("read", "pool", g))
                    u, cur, s, n = pbuf[g], pbuf[g], 1, 0
                    while s < w:
                        dst = pbuf[4 + n % 2]
                        V.tensor_tensor(dst[:, 16:16 + SEQ], cur[:, 16:16 + SEQ], cur[:, 16 - s:16 - s + SEQ], ALU.add).then_inc(vector_out, vector_at.next())
                        dve.wait_ge(vector_out, vector_at.n)
                        cur, s, n = dst, 2 * s, n + 1
                    pooled = U[:, 4 + g, :]
                    STT(pooled, cur[:, 16:16 + SEQ], 1.0 / w, u[:, 16:16 + SEQ], ALU.mult, ALU.subtract).then_inc(vector_out, vector_at.next())
                    V.tensor_tensor(small[:, 64:80], cur[:, 16:32], con[:, K_CNT + 16 * g:K_CNT + 16 * g + 16], ALU.mult).then_inc(vector_out, vector_at.next())
                    dve.wait_ge(vector_out, vector_at.n)
                    V.tensor_tensor(pooled[:, 0:16], small[:, 64:80], u[:, 16:32], ALU.subtract).then_inc(vector_out, vector_at.next("pooled", g))
                for g in range(4):
                    dve.wait_ge(tensor_out, tensor_at.find("poolmm", g))
                    V.tensor_scalar(MIX[:, 4 + g, :], bank[6][:], col("pool_b", g), col("pool_s", g), ALU.add, ALU.mult).then_inc(vector_out, vector_at.next("poolout", g))
                stage_end(dve, vector_at, "in1")

                def ssm_finish(st):
                    c = st["out"]
                    STT(ys[:, c, :], xbc[:, c, :], col("d_skip", c), bank[st["num"]][:], ALU.mult, ALU.add).then_inc(vector_out, vector_at.next("ssd", "fin", c))

                decayed("ssd", ssm_steps, ssm_finish)
                for j in range(4):
                    dve.wait_ge(scalar_out, scalar_at.find("read", "z1", j))
                    dve.wait_ge(vector_out, vector_at.n)
                    V.tensor_tensor(ys[:, j, :], ys[:, j, :], gate[:, j, :], ALU.mult).then_inc(vector_out, vector_at.next("ssmn", "x", j))
                norm("ssmn", 4, ys, False, "ssm_norm", MIX)
                stage_end(dve, vector_at, "mix1")
                split_operand("mix1", MIX)
                residual("out1", "ln1_1", ALPHA, False)
                norm("ln1_1", DC, X, True)
                stage_end(dve, vector_at, "ln1_1")
            if on("up1"):
                ffn(1)
                residual("down1", "ln2_1", ALPHA, True)
                norm("ln2_1", DC, X, True)
                stage_end(dve, vector_at, "ln2_1")
            if on("small2"):
                for k in range(DC):
                    vector_at.mark("rms1", "x", k)
                norm("rms1", DC, X, False, "norm1", U)
                split_operand("rms1", U)
                stage_end(dve, vector_at, "rms1")
                absolute("gate2", ("pre2",))
                dve.wait_ge(scalar_out, scalar_at.find("gate2", "ln"))
                STT(row[58], row[56], 0.0, row[57], ALU.max, ALU.add).then_inc(vector_out, vector_at.next())
                dve.wait_ge(vector_out, vector_at.n)
                dve.wait_ge(scalar_out, scalar_at.find("ea2"))
                V.tensor_scalar(row[61][0:8, :], row[58][0:8, :], small[0:8, 208:209], -1.0, ALU.mult, ALU.mult).then_inc(vector_out, vector_at.next())
                dve.wait_ge(vector_out, vector_at.n)
                for c in range(TILES):
                    V.tensor_tensor_scan(row[62][0:8, c * P:(c + 1) * P], ones[0:8, 0:P], row[61][0:8, c * P:(c + 1) * P], 0.0, ALU.mult, ALU.add).then_inc(vector_out, vector_at.next())
                    dve.wait_ge(vector_out, vector_at.n)
                    V.tensor_scalar(row[63][0:8, c * P:(c + 1) * P], row[62][0:8, c * P:(c + 1) * P], -1.0, row[62][0:8, (c + 1) * P - 1:(c + 1) * P], ALU.mult, ALU.add).then_inc(vector_out, vector_at.next())
                vector_at.mark("dG")
                dve.wait_ge(scalar_out, scalar_at.find("eG"))
                V.tensor_tensor(row[64][0:8, :], row[64][0:8, :], row[59][0:8, :], ALU.mult).then_inc(vector_out, vector_at.next("gate2", "rows"))
                unit_done("ik", 0)
                V.tensor_copy(row[65], bank[FIRST["ik"] % RING][:]).then_inc(vector_out, vector_at.next("read", "ik", 0))
                vector_at.mark("ikn", "x", 0)
                passing("iq")
                dve.wait_ge(tensor_out, tensor_at.find("gate2", "cols"))
                V.tensor_copy(small[:, 0:160], bank[4][:, 0:160]).then_inc(vector_out, vector_at.next())
                src = bank[4][:, 0:160].rearrange("p (c x) -> p c x", c=TILES)[:, :, 0:8]
                V.tensor_scalar(small[:, 160:192].rearrange("p (c x) -> p c x", c=TILES), src, -1.0, None, ALU.mult).then_inc(vector_out, vector_at.next("gate2", "cols"))
                dve.wait_ge(vector_out, vector_at.n)
                dve.wait_ge(gpsimd_out, gpsimd_at.find("pads2"))

                def ik_write(k, r):
                    for e in range(2):
                        p0 = 64 * e
                        STT(ikp[p0:p0 + 64, e, :], row[65][p0:p0 + 64, :], col("ik_norm", 0, p0, p0 + 64), r[p0:p0 + 64, :], ALU.mult, ALU.mult).then_inc(vector_out, vector_at.next("ikn", "out"))

                dve.wait_ge(vector_out, vector_at.n)
                item_norms("ikn", 1, lambda k: row[65], True, ik_write, lambda k: RSTD)
                for tt in range(TILES):
                    unit_done("dv", 1)
                    V.tensor_copy(dv[:, tt, :], bank[tt][:, 0:256]).then_inc(vector_out, vector_at.next("read", "dv", tt))
                n = 0
                for i in range(1, TILES):
                    sc = score[:, i, 0:(i + 1) * P]
                    for h in range(IDX_HEADS):
                        dve.wait_ge(scalar_out, scalar_at.find("relu", n))
                        r = arena[:, 48 + n % 4, 0:(i + 1) * P]
                        w = small[:, i * 40 + 32 + h:i * 40 + 33 + h]
                        if h == 0:
                            V.tensor_scalar(sc, r, w, None, ALU.mult).then_inc(vector_out, vector_at.next("sc", n))
                            dve.wait_ge(vector_out, vector_at.n)
                        else:
                            STT(sc, r, w, sc, ALU.mult, ALU.add).then_inc(vector_out, vector_at.next("sc", n))
                            dve.wait_ge(vector_out, vector_at.n)
                        n += 1
                    V.tensor_tensor(score[:, i, i * P:(i + 1) * P], score[:, i, i * P:(i + 1) * P], con[:, K_MQ:K_MQ + P], ALU.add).then_inc(vector_out, vector_at.next())
                    dve.wait_ge(vector_out, vector_at.n)
                for rnd in range(TOPK // 8):
                    for i in range(1, TILES):
                        V.max(small[:, 216 + 8 * i:224 + 8 * i], score[:, i, 0:(i + 1) * P]).then_inc(vector_out, vector_at.next("top", rnd, i))
                    for i in range(1, TILES):
                        dve.wait_ge(vector_out, vector_at.find("top", rnd, i))
                        sc = score[:, i, 0:(i + 1) * P]
                        V.match_replace(sc, small[:, 216 + 8 * i:224 + 8 * i], sc, TAKEN).then_inc(vector_out, vector_at.next())
                    dve.wait_ge(vector_out, vector_at.n)
                for i in range(1, TILES):
                    V.tensor_scalar(madd[:, i, 0:(i + 1) * P], score[:, i, 0:(i + 1) * P], -2e38, NEG, ALU.is_ge, ALU.mult).then_inc(vector_out, vector_at.next())
                stage_end(dve, vector_at, "topk")
                attention("dsa", dsa_steps)
                for j in range(DC):
                    split_units(FIRST["gateb"] + j + 2)
                    dve.wait_ge(scalar_out, scalar_at.find("read", "gateb", j))
                    V.tensor_tensor(MIX[:, j, :], MIX[:, j, :], arena[:, 48 + j % 4, :], ALU.mult).then_inc(vector_out, vector_at.next("gateb", j))
                stage_end(dve, vector_at, "dsa")
            if on("gqkv"):
                for j in range(24):
                    split_units(FIRST["gqkv"] + j + 2)
                    dve.wait_ge(scalar_out, scalar_at.find("ga", j))
                    conv("gqkv", j, arena[:, 24 + j, :], bank[(FIRST["gqkv"] + j) % RING], [(s, col("gqkv_conv", 4 * j + 3 - s)) for s in (1, 2, 3)])

                def l2_write(k, r):
                    x = arena[:, 24 + k, :]
                    STT(x, x, P ** -0.5 if k < 8 else 1.0, r, ALU.mult, ALU.mult).then_inc(vector_out, vector_at.next())

                item_norms("l2", 16, None, False, l2_write, lambda k: arena[:, 50 + k % 2, :])
                stage_end(dve, vector_at, "gqkv")
                for c in range(TILES):
                    cs = slice(c * P, (c + 1) * P)
                    for g in range(2):
                        t, G = (c, g), GW

                        def every(ap):
                            return ap.rearrange("p (a n) -> p a n", a=1).to_broadcast([P, 4, P])

                        def lev(r):
                            return every(con[:, K_LEV + r * P:K_LEV + (r + 1) * P])

                        dve.wait_ge(tensor_out, tensor_at.find("bb", t))
                        V.tensor_tensor(G["kb"], gk[:, 4 * g:4 * g + 4, cs], tile(2), ALU.mult).then_inc(vector_out, vector_at.next("kb", t))
                        dve.wait_ge(tensor_out, tensor_at.find("kk", t))
                        dve.wait_ge(scalar_out, scalar_at.find("gam", t))
                        V.tensor_tensor(G["at"], tile(6), G["gam"], ALU.mult).then_inc(vector_out, vector_at.next("at", t))
                        dve.wait_ge(vector_out, vector_at.n)
                        V.tensor_tensor(G["lt"], G["at"], lev(0), ALU.mult).then_inc(vector_out, vector_at.next("lt", t, 0))
                        dve.wait_ge(vector_out, vector_at.n)
                        V.tensor_tensor(G["u"], every(ident), G["lt"], ALU.subtract).then_inc(vector_out, vector_at.next("u", t, 0))
                        dve.wait_ge(tensor_out, tensor_at.find("kq", t))
                        V.tensor_tensor(G["att"], tile(3), G["gam"], ALU.mult).then_inc(vector_out, vector_at.next("att", t))
                        dve.wait_ge(scalar_out, scalar_at.find("eg", t))
                        V.tensor_tensor(G["qg"], gq[:, 4 * g:4 * g + 4, cs], G["eg"], ALU.mult).then_inc(vector_out, vector_at.next("qg", t))
                        dve.wait_ge(tensor_out, tensor_at.find("l0", t))
                        V.tensor_tensor(G["t"], every(ident), tile(7), ALU.subtract).then_inc(vector_out, vector_at.next("t", t, 0))
                        for r in range(1, LEVELS):
                            if r > 1:
                                dve.wait_ge(tensor_out, tensor_at.find("x", t, r - 1))
                            dve.wait_ge(vector_out, vector_at.n)
                            V.tensor_tensor(G["lt"], G["at"], lev(r), ALU.mult).then_inc(vector_out, vector_at.next("lt", t, r))
                            dve.wait_ge(tensor_out, tensor_at.find("y", t, r))
                            dve.wait_ge(vector_out, vector_at.n)
                            if r < LEVELS - 1:
                                V.tensor_tensor(G["t"], G["t"], tile(2), ALU.subtract).then_inc(vector_out, vector_at.next("t", t, r))
                            V.tensor_tensor(G["u"], G["u"], tile(1), ALU.subtract).then_inc(vector_out, vector_at.next("u", t, r))
                        dve.wait_ge(tensor_out, tensor_at.find("s", t))
                        for hh in range(4):
                            if c:
                                STT(state[:, g, hh, :], state[:, g, hh, :], G["eg"][:, hh, P - 1:P], tile(6)[:, hh, :], ALU.mult, ALU.add).then_inc(vector_out, vector_at.next("s", t))
                            else:
                                V.tensor_copy(state[:, g, hh, :], tile(6)[:, hh, :]).then_inc(vector_out, vector_at.next("s", t))
                stage_end(dve, vector_at, "gdn")
                split_operand("again", U)
                item_norms("gn", 8, None, False,
                           lambda k, r: STT(go[:, k, :], go[:, k, :], col("gdn_norm"), r, ALU.mult, ALU.mult).then_inc(vector_out, vector_at.next("gn", "out", k)),
                           lambda k: arena[:, 34 + k % 2, :])
                for j in range(DC):
                    split_units(FIRST["z2"] + j + 2)
                    dve.wait_ge(scalar_out, scalar_at.find("read", "z2", j))
                    dve.wait_ge(vector_out, vector_at.find("gn", "out", j))
                    V.tensor_tensor(go[:, j, :], go[:, j, :], arena[:, 24 + j, :], ALU.mult).then_inc(vector_out, vector_at.next("z2", j))
                for j in range(DC):
                    split_units(FIRST["gatea"] + j + 2)
                    dve.wait_ge(scalar_out, scalar_at.find("read", "gatea", j))
                    dve.wait_ge(vector_out, vector_at.find("z2", j))
                    V.tensor_tensor(go[:, j, :], go[:, j, :], arena[:, 24 + j, :], ALU.mult).then_inc(vector_out, vector_at.next())
                    dve.wait_ge(vector_out, vector_at.n)
                    V.tensor_tensor(MIX[:, j, :], MIX[:, j, :], go[:, j, :], ALU.add).then_inc(vector_out, vector_at.next())
                stage_end(dve, vector_at, "mix2")
                split_operand("mix2", MIX)
                residual("out2", "rms2", 1.0, False)
                norm("rms2", DC, X, False, "norm2", U)
                split_operand("rms2", U)
                stage_end(dve, vector_at, "rms2")
            if on("up2"):
                ffn(2)
                residual("down2", "rmsf", 1.0, True)
                norm("rmsf", DC, X, False, "final", U)


LAST_STAGE = None


def lay_out(inp):
    f = {k: np.asarray(v) for k, v in inp.items()}
    units = []

    def stationary(w, padded=None):
        k, n = w.shape
        for j in range(n // P):
            units.append(w[:, j * P:(j + 1) * P].reshape(DC, P, P).transpose(1, 0, 2).reshape(P, 8 * P))

    def moving(w, q):
        n = w.shape[1]
        w = w.reshape(DC, P, n)
        for j in range(DC // q):
            units.append(w[j * q:(j + 1) * q].transpose(1, 0, 2).reshape(P, 8 * P))

    def rows(parts, shape):
        w = np.zeros(shape + (P,), np.float32)
        for x, part in enumerate(parts):
            w[..., 32 * x:32 * x + part.shape[-1]] = part
        return w

    def up(w, gate_first):
        a, b = (w[:, :D_FF], w[:, D_FF:]) if gate_first else (w[:, D_FF:], w[:, :D_FF])
        for j in range(FC):
            stationary(a[:, j * P:(j + 1) * P])
            stationary(b[:, j * P:(j + 1) * P])

    def down(w):
        for j in range(FC):
            units.append(w[j * P:(j + 1) * P, :])

    we, be = f["ev_w_in"][0], f["ev_b_in"][0]
    H = HALF
    o = [0, H, 2 * H, 3 * H, 4 * H, 4 * H + 4, 4 * H + 8, 5 * H + 8, 6 * H + 8, 7 * H + 8, 7 * H + 16]
    e = [we[:, o[i]:o[i + 1]] for i in range(10)]
    eb = [be[o[i]:o[i + 1]] for i in range(10)]
    stationary(rows([e[4], e[5], e[9]], (DM,)))
    stationary(e[0]); stationary(e[1]); moving(e[2], 2)
    stationary(e[6]); stationary(e[7]); moving(e[8], 2)
    stationary(e[3])
    stationary(f["ev_w_out"][0])
    up(f["ffn_w_up"][0], False); down(f["ffn_w_down"][0])
    wo = f["od_w_in"][0]
    stationary(rows([wo[:, 1536:1544]], (DM,)))
    stationary(wo[:, 512:1536]); stationary(wo[:, 1544:2056]); stationary(wo[:, 0:512])
    stationary(f["od_w_out"][0])
    up(f["ffn_w_up"][1], False); down(f["ffn_w_down"][1])
    w2 = f["w_in_2"][0]
    cut = lambda a, b: w2[:, a:b]
    stationary(rows([cut(4096, 4104), cut(4104, 4112), cut(6224, 6232)], (DM,)))
    stationary(np.concatenate([cut(6160, 6224)] * 2, 1))
    stationary(cut(5648, 6160)); stationary(cut(4112, 5136)); stationary(cut(5136, 5392)); moving(cut(5392, 5648), 4)
    stationary(cut(7256, 8280))
    stationary(cut(0, 3072)); stationary(cut(3072, 4096)); stationary(cut(6232, 7256))
    stationary(f["w_out_2"][0])
    up(f["ffn_w_up_2"][0], True); down(f["ffn_w_down_2"][0])
    assert len(units) == UNITS
    units += [np.zeros((P, 8 * P), np.float32)] * 2
    stream = np.ascontiguousarray(np.stack(units))

    cols = {n: [] for n, _ in COLS}

    def put(name, v):
        cols[name] += list(np.asarray(v).reshape(-1, P))

    put("b_small0", rows([eb[4], eb[5], eb[9]], ()))
    for n, x in (("b_mq", 0), ("b_mk", 1), ("b_fq", 6), ("b_fk", 7), ("b_mo", 3)):
        put(n, eb[x])
    put("ml_norm", f["ev_ml_norm"][0])
    for l in range(2):
        for n in ("ln1_g", "ln1_b", "ln2_g", "ln2_b"):
            put(f"{n}{l}", f[n][l])
    put("dt_bias", rows([f["od_dt_bias"][0]], ()))
    put("a_log", rows([f["od_a_log"][0]], ()))
    cw = f["od_conv_w"][0]
    put("xbc_conv", np.concatenate([cw, f["od_conv_b"]], 0).reshape(5, 8, P).transpose(1, 0, 2))
    put("d_skip", np.repeat(f["od_d_skip"][0], 64))
    put("ssm_norm", f["od_ssm_norm"][0]); put("pool_b", f["od_pool_b"][0]); put("pool_s", f["od_pool_scale"][0])

    def ffn_cols(name, w, b, gate_first):
        x = np.concatenate([w, b[None]], 0).reshape(4, 2, FC, P).transpose(2, 1, 0, 3)
        put(name, x if gate_first else x[:, ::-1])

    ffn_cols("ffn0", f["ffn_conv_w"][0], f["ffn_conv_b"][0], False)
    ffn_cols("ffn1", f["ffn_conv_w"][1], f["ffn_conv_b"][1], False)
    ffn_cols("ffn2", f["ffn_conv_w_2"][0], f["ffn_conv_b_2"][0], True)
    put("norm1", f["norm1_g_2"][0]); put("norm2", f["norm2_g_2"][0]); put("final", f["final_g_2"])
    put("g_dt_bias", rows([f["gdn_dt_bias_2"][0]], ())); put("g_a_log", rows([f["gdn_a_log_2"][0]], ()))
    put("gqkv_conv", f["gdn_conv_w_2"][0].reshape(4, 24, P).transpose(1, 0, 2))
    put("gdn_norm", f["gdn_norm_g_2"][0]); put("ik_norm", np.concatenate([f["idx_k_norm_g_2"][0]] * 2)); put("gate_b", f["branch_gate_b_2"][0])
    for n, c in COLS:
        assert len(cols[n]) == c, (n, len(cols[n]))
    params = np.ascontiguousarray(np.stack([v for n, _ in COLS for v in cols[n]], 1))

    con = np.zeros((P, NCONST), np.float32)
    i = np.arange(P)
    con[:, K_ID:K_ID + P] = np.eye(P)
    con[:, K_MT:K_MT + P] = np.where(i[None, :] >= i[:, None], 0.0, NEG)
    con[:, K_MQ:K_MQ + P] = np.where(i[None, :] <= i[:, None], 0.0, NEG)
    for r in range(LEVELS):
        b = 1 << r
        same = (i[:, None] // (2 * b) == i[None, :] // (2 * b)) & (i[:, None] // b % 2 == 0) & (i[None, :] // b % 2 == 1)
        con[:, K_LEV + r * P:K_LEV + (r + 1) * P] = same
    for g, w in enumerate(POOL_WINDOWS):
        con[:, K_CNT + 16 * g:K_CNT + 16 * g + 16] = 1.0 / np.minimum(np.arange(16) + 1, w)
    for h in range(8):
        con[h, K_SEL + h * P:K_SEL + (h + 1) * P] = 1.0

    xt = np.ascontiguousarray(f["x"][0].T.reshape(DC, P, SEQ).transpose(1, 0, 2))
    brow = np.ascontiguousarray(np.concatenate([eb[2], eb[8]])[None])
    poolw = np.ascontiguousarray(f["od_pool_w"][0].transpose(1, 0, 2))
    return {"stream": stream, "params": params, "brow": brow, "poolw": poolw, "consts": con, "xt": xt}


def kernel(**inputs):
    import concourse.bacc as _bacc
    from concourse.bass_utils import run_bass_kernel_spmd as _run

    arrays = lay_out(inputs)
    marks = {}
    for _ in range(2):
        nc = _bacc.Bacc("TRN2", target_bir_lowering=False, num_devices=1)
        args = [nc.dram_tensor(k, v.shape, F32, kind="ExternalInput").ap() for k, v in arrays.items()]
        args.append(nc.dram_tensor("out", (P, DC, SEQ), F32, kind="ExternalOutput").ap())
        build_program(nc, *args, marks, LAST_STAGE)
    r = _run(nc, [arrays], core_ids=[0])
    got = r.results[0]["out"]
    return np.ascontiguousarray(got.transpose(1, 0, 2).reshape(1, DM, SEQ).transpose(0, 2, 1))
```

```python
from contextlib import ExitStack

import numpy as np
import concourse.bass as bass
from concourse import mybir

ALU = mybir.AluOpType
ACT = mybir.ActivationFunctionType
F32 = mybir.dt.float32
BF16 = mybir.dt.bfloat16
F32R = mybir.dt.float32r
AX_X = mybir.AxisListType.X

P = 128
SEQ = 512
TILES = SEQ // P
DM = 1024
DC = DM // P
D_FF = 2816
FC = D_FF // P
HALF = 512
DEPTH = 2
ALPHA = (2.0 * DEPTH) ** 0.25
LN_EPS = 1e-5
RMS_EPS = 1e-6
NEG = -1e30
TAKEN = -3e38
TOPK = min(256, SEQ // 4)
RING = 4
ML_HEADS, FOX_HEADS, SSM_HEADS, GDN_HEADS, DSA_HEADS, IDX_HEADS = 4, 8, 8, 8, 8, 8
POOL_WINDOWS = (2, 4, 8, 16)
LEVELS = 7

RUNS = [
    ("small0", 1), ("mq", 4), ("mk", 4), ("mv", 4), ("fq", 4), ("fk", 4), ("fv", 4), ("mo", 4), ("out0", 8),
    ("up0", 2 * FC), ("down0", FC),
    ("small1", 1), ("xbc", 8), ("pool", 4), ("z1", 4), ("out1", 8),
    ("up1", 2 * FC), ("down1", FC),
    ("small2", 1), ("ik", 1), ("iq", 4), ("dq", 8), ("dk", 2), ("dv", 2), ("gateb", 8),
    ("gqkv", 24), ("z2", 8), ("gatea", 8), ("out2", 8),
    ("up2", 2 * FC), ("down2", FC),
]
FIRST, _u = {}, 0
for _name, _n in RUNS:
    FIRST[_name] = _u
    _u += _n
COUNT = dict(RUNS)
UNITS = _u

COLS = [
    ("b_small0", 1), ("b_mq", 4), ("b_mk", 4), ("b_fq", 4), ("b_fk", 4), ("b_mo", 4), ("ml_norm", 4),
    ("ln1_g0", 8), ("ln1_b0", 8), ("ln2_g0", 8), ("ln2_b0", 8), ("ln1_g1", 8), ("ln1_b1", 8), ("ln2_g1", 8), ("ln2_b1", 8),
    ("dt_bias", 1), ("a_log", 1), ("xbc_conv", 8 * 5), ("d_skip", 4), ("ssm_norm", 4), ("pool_b", 4), ("pool_s", 4),
    ("ffn0", 2 * FC * 4), ("ffn1", 2 * FC * 4), ("ffn2", 2 * FC * 4),
    ("norm1", 8), ("norm2", 8), ("final", 8), ("g_dt_bias", 1), ("g_a_log", 1), ("gqkv_conv", 24 * 4),
    ("gdn_norm", 1), ("ik_norm", 1), ("gate_b", 16),
]
COL, _c = {}, 0
for _name, _n in COLS:
    COL[_name] = _c
    _c += _n
NCOL = _c

K_ID, K_MT, K_MQ, K_LEV, K_CNT, K_SEL = 0, P, 2 * P, 3 * P, (3 + LEVELS) * P, (3 + LEVELS) * P + 64
K_PICK = K_SEL + 8 * P
NCONST = K_PICK + 16


class Counts:

    def __init__(self, marks):
        self.marks, self.n = marks, 0

    def next(self, *key):
        self.n += 1
        if key:
            self.marks[key] = self.n
        return 1

    def mark(self, *key):
        self.marks[key] = self.n

    def find(self, *key):
        return self.marks.get(key, 1)


def build_program(nc, stream, params, brow, poolw, consts, xt, out, marks, last_stage):
    with ExitStack() as ctx:
        def sb(name, shape, dt=F32):
            return ctx.enter_context(nc.sbuf_tensor(name, shape, dt))

        def sem(name):
            return ctx.enter_context(nc.semaphore(name))

        arena = sb("arena", [P, 62, SEQ])
        ring = sb("ring", [P, RING, 8 * P])
        whi, wlo = sb("whi", [P, 2, 8 * P], F32R), sb("wlo", [P, 2, 8 * P], F32R)
        with nc.sbuf_tensor("scratch", [P, 16, SEQ], F32) as scratch:
            pass
        xs = sb("xs", [P, 16, SEQ], F32R)
        xhi, xlo = xs[:, 0:8, :], xs[:, 8:16, :]
        par = sb("par", [P, NCOL])
        con = sb("con", [P, NCONST])
        idb = sb("idb", [P, P], BF16)
        mtb = sb("mtb", [P, P], BF16)
        mqb = sb("mqb", [P, P], BF16)
        ones = sb("ones", [P, SEQ])
        inv = {n: sb(f"inv{n}", [P, P]) for n in (128, 512, 1024)}
        small = sb("small", [P, 256])
        pw = sb("pw", [P, TILES, P])
        bank = [ctx.enter_context(nc.psum_tensor(f"bank{b}", [P, SEQ], F32)) for b in range(8)]

        ident = con[:, K_ID:K_ID + P]
        ident8 = con[0:8, K_ID:K_ID + 8]

        def sel(h, n=8):
            return con[0:n, K_SEL + h * P:K_SEL + (h + 1) * P]

        def pick(k):
            return con[:, K_PICK + 8 - k:K_PICK + 16 - k]

        def col(name, j=0, p0=0, p1=P):
            return par[p0:p1, COL[name] + j:COL[name] + j + 1]

        X, U, MIX = arena[:, 0:8, :], arena[:, 8:16, :], arena[:, 16:24, :]

        in_sem = sem("in_sem")
        ring_sem = [sem(f"ring_loaded{s}") for s in range(RING)]
        units_done, whi_done, wlo_done = sem("units_done"), sem("weights_high_done"), sem("weights_low_done")
        tensor_out, scalar_out, vector_out, gpsimd_out = sem("tensor_out"), sem("scalar_out"), sem("vector_out"), sem("gpsimd_out")
        tensor_at, scalar_at, vector_at, gpsimd_at = (Counts(marks.setdefault(n, {})) for n in ("tensor", "scalar", "vector", "gpsimd"))
        SCALAR, VECTOR = (scalar_out, scalar_at), (vector_out, vector_at)
        acc_done, tap_done, conv_done = sem("ffn_acc_done"), sem("ffn_tap_done"), sem("ffn_conv_done")
        gate_done, hid_done = sem("ffn_gate_done"), sem("ffn_hidden_done")
        hhi_done, hlo_done = sem("hidden_high_done"), sem("hidden_low_done")
        out_sem = sem("out_sem")
        x_sem = [sem(f"input_loaded{q}") for q in range(4)]
        nloads = 4

        ctx.enter_context(nc.allow_low_precision(reason="0/1 and mask constants"))
        block = ctx.enter_context(nc.Block())
        last_unit = UNITS if last_stage is None else FIRST[last_stage] + COUNT[last_stage]

        def on(stage):
            return FIRST[stage] < last_unit

        @block.sync
        def _(sp):
            sp.dma_start(ring[:, 0, :], stream[0]).then_inc(ring_sem[0], 16)
            for q in range(4):
                sp.dma_start(X[:, 2 * q:2 * q + 2, :], xt[:, 2 * q:2 * q + 2, :]).then_inc(x_sem[q], 16)
            sp.dma_start(ring[:, 1, :], stream[1]).then_inc(ring_sem[1], 16)
            sp.dma_start(par[:], params).then_inc(in_sem, 16)
            sp.dma_start(con[:], consts).then_inc(in_sem, 16)
            sp.dma_start(pw[:], poolw).then_inc(in_sem, 16)
            sp.dma_start(arena[0:1, 20:22, :], brow.rearrange("a (c n) -> a c n", c=2)).then_inc(in_sem, 16)
            for s in range(2, RING):
                sp.dma_start(ring[:, s, :], stream[s]).then_inc(ring_sem[s], 16)
            loads = last_unit + 2
            rounds = loads // RING
            with sp.Fori(1, rounds) as i:
                for s in range(RING):
                    sp.wait_ge(wlo_done, (i - 1) * RING + s + 1)
                    sp.dma_start(ring[:, s, :], stream[i * RING + s]).then_inc(ring_sem[s], 16)
            for u in range(rounds * RING, loads):
                sp.wait_ge(wlo_done, u - RING + 1)
                sp.dma_start(ring[:, u % RING, :], stream[u]).then_inc(ring_sem[u % RING], 16)

        def stage_end(eng, mine, name):
            mine.mark("stage", name)
            eng.wait_ge(tensor_out, tensor_at.find("stage", name))
            eng.wait_ge(scalar_out, scalar_at.find("stage", name))
            eng.wait_ge(vector_out, vector_at.find("stage", name))
            eng.wait_ge(gpsimd_out, gpsimd_at.find("stage", name))

        mq, mk, mv = arena[:, 24:28, :], arena[:, 28:32, :], arena[:, 32:36, :]
        fq, fk = arena[:, 36:40, :], arena[:, 40:48, :]
        fv = arena[:, 48:56, :].rearrange("p (t a) n -> p t (a n)", a=2).rearrange("p t (h d) -> p t h d", h=FOX_HEADS)
        row = {j: arena[:, c, :] for j, c in {56: 16, 57: 17, 58: 18, 65: 19, 59: 56, 60: 57, 61: 58, 62: 59, 63: 60, 64: 61}.items()}
        RSTD = arena[:, 55, :]
        gate = arena[:, 8:12, :]
        bias_v = arena[0:1, 20:22, :]
        hid, acc, sg = arena[:, 24:24 + FC, :], arena[:, 46:50, :], arena[:, 50:52, :]
        xbc, ys = arena[:, 24:32, :], arena[:, 32:36, :]
        xpad = arena[:, 36:44, :].rearrange("p (t a) n -> p t (a n)", a=2).rearrange("p t (h d) -> p t h d", h=SSM_HEADS)
        pbuf = [arena[:, 44 + 2 * g:46 + 2 * g, :].rearrange("p a n -> p (a n)") for g in range(6)]
        iq, ikp, dq, dk = arena[:, 24:28, :], arena[:, 28:30, :], arena[:, 30:38, :], arena[:, 38:40, :]
        dv = arena[:, 40:42, :].rearrange("p a n -> p (a n)").rearrange("p (t n) -> p t n", t=TILES)
        madd = arena[:, 42:44, :].rearrange("p a n -> p (a n)").bitcast(BF16).rearrange("p (t n) -> p t n", t=TILES)
        score = arena[:, 44:48, :]
        gq, gk, gv = arena[:, 24:32, :], arena[:, 32:40, :], arena[:, 40:48, :]
        go = gv
        gdn_space = [scratch[:, i, :] for i in range(16)] + [arena[:, i, :] for i in range(48, 54)]
        gdn_names = ["gam", "eg", "kb", "at", "att", "qg", "u", "xs", "kbe", "kd", "vb"]
        gdn_work = [{n: gdn_space[11 * g + i].rearrange("p (h n) -> p h n", h=4) for i, n in enumerate(gdn_names)} for g in range(2)]
        for G in gdn_work:
            G["t"], G["lt"], G["vn"], G["nw"] = G["gam"], G["kb"], G["kb"], G["xs"]
        state = arena[:, 57:59, :].rearrange("p g (h n) -> p g h n", h=4)

        def tile(b):
            return bank[b][:, :].rearrange("p (h n) -> p h n", h=4)

        l2_spread = {13 + i: [2 * i, 2 * i + 1] for i in range(4)} | {21: [8, 9, 10], 22: [11, 12, 13], 23: [14, 15]}
        gn_spread = {3 + i: [2 * i, 2 * i + 1] for i in range(4)}

        parts_space = {layer: [arena[:, c, :].bitcast(BF16) for c in chunks] for layer, chunks in ((0, (12, 13)), (1, (61, 19, 55)), (2, (54, 55)))}

        def spread_rows(layer, h):
            return parts_space[layer][0][0:72, h * P:(h + 1) * P]

        def parts(layer, which):
            return parts_space[layer][1 + which // 2][:, which % 2 * SEQ:(which % 2 + 1) * SEQ]

        ml_steps = [dict(j=j, sel=spread_rows(0, h), rows=parts(0, 0)[0:72, j * P:], bias=small[:, j * 4 + h:j * 4 + h + 1], k=mk[:, h, j * P:(j + 1) * P],
                         q=mq[:, h, j * P:], v=mv[:, j, h * P:(h + 1) * P], num=h % 2, den=h, first=j == 0, last=j == TILES - 1, out=h)
                    for h in range(ML_HEADS) for j in range(TILES)]
        ssm_steps = [dict(j=j, sel=spread_rows(1, h), rows=parts(1, j)[0:72, j * P:], bias=small[:, 32 + j * 8 + h:33 + j * 8 + h], k=xbc[:, 4 + h // 4, j * P:(j + 1) * P],
                          q=xbc[:, 6 + h // 4, j * P:], v=xpad[:, j, h, :], num=h // 2 % 2, den=None, first=j == 0 and h % 2 == 0,
                          kept=8 + h // 4 * 4 + j, fresh=h % 4 == 0, at=(h // 4, j),
                          last=j == TILES - 1 and h % 2 == 1, out=h // 2)
                     for h in range(SSM_HEADS) for j in range(TILES)]
        fox_steps = [dict(w=(i + 1) * P, q=fq[:, h // 2, i * P:(i + 1) * P], k=fk[:, h, 0:(i + 1) * P],
                          more=[(spread_rows(0, h), parts(0, 1)[0:72, 0:(i + 1) * P], 0, (i + 1) * P), (idb[:], mqb[:], i * P, (i + 1) * P)],
                          v=[fv[:, j, h, :] for j in range(i + 1)], ob=c % 2, oc=i * P, start=h % 2 == 0, stop=h % 2 == 1,
                          claim=i == 0 and h % 2 == 0, last=i == TILES - 1 and h % 2 == 1, o=c, dst=4 + c)
                     for c in range(4) for i in range(TILES) for h in (2 * c, 2 * c + 1)]
        dsa_steps = [dict(w=(i + 1) * P, q=dq[:, h, i * P:(i + 1) * P], k=dk[:, h // 4, 0:(i + 1) * P],
                          more=[(idb[:], madd[:, i, 0:(i + 1) * P] if i else mqb[:], 0, (i + 1) * P)],
                          v=[dv[:, j, (h // 4) * P:(h // 4 + 1) * P] for j in range(i + 1)], ob=h % 2, oc=i * P, start=True, stop=True,
                          claim=i == 0, last=i == TILES - 1, o=h, dst=h)
                     for h in range(DSA_HEADS) for i in range(TILES)]
        for steps, work in ((fox_steps, scratch[:, 0:7, :]), (dsa_steps, arena[:, 48:55, :])):
            for n, st in enumerate(steps):
                st["ps"], st["ts"] = work[:, n % 4, :], work[:, 4 + n % 3, :]

        @block.tensor
        def _(pe):
            reader = {}

            def claim(b):
                if b in reader:
                    (semaphore, at), key = reader[b]
                    pe.wait_ge(semaphore, at.find(*key))

            def unit_split(u):
                pe.wait_ge(wlo_done, u + 1)

            def products(out, wcols, xs3, first, last):
                (ah, al), (bh, bl) = wcols, xs3
                nc.tensor.matmul(out, ah, bh, start=first, stop=False)
                nc.tensor.matmul(out, ah, bl, start=False, stop=False)
                return nc.tensor.matmul(out, al, bh, start=False, stop=last)

            def run_units(name, prog, operand=None, after=None):
                for j in range(COUNT[name]):
                    u = FIRST[name] + j
                    claim(u % RING)
                    unit_split(u)
                    for k in range(DC):
                        if operand is not None and j == 0:
                            pe.wait_ge(vector_out, vector_at.find("xl", operand, k))
                        w = slice(k * P, (k + 1) * P)
                        m = products(bank[u % RING][:], (whi[:, u % 2, w], wlo[:, u % 2, w]), (xhi[:, k, :], xlo[:, k, :]), k == 0, k == DC - 1)
                    m.then_inc(units_done, 1)
                    reader[u % RING] = (prog, ("read", name, j))
                    if after is not None:
                        after(j)

            def run_moving(name, n, bias_row):
                kk = 8 * P // n
                for tt in range(TILES):
                    claim(tt)
                    if bias_row is not None:
                        nc.tensor.matmul(bank[tt][:, 0:n], ones[0:1, 0:P], bias_row, start=True, stop=False)
                for j in range(COUNT[name]):
                    u = FIRST[name] + j
                    unit_split(u)
                    for tt in range(TILES):
                        for q in range(kk):
                            k, t, w = j * kk + q, slice(tt * P, (tt + 1) * P), slice(q * n, (q + 1) * n)
                            m = products(bank[tt][:, 0:n], (xhi[:, k, t], xlo[:, k, t]), (whi[:, u % 2, w], wlo[:, u % 2, w]), k == 0 and bias_row is None, k == DC - 1)
                    m.then_inc(units_done, 1)
                for tt in range(TILES):
                    reader[tt] = (VECTOR, ("read", name, tt))

            def norm(name, chunks, n, xs, sq, mean):
                if mean:
                    claim(6)
                    for k in range(chunks):
                        pe.wait_ge(vector_out, vector_at.find(name, "x", k))
                        m = nc.tensor.matmul(bank[6][:], inv[n][:], xs[:, k, :], start=k == 0, stop=k == chunks - 1)
                    m.then_inc(tensor_out, tensor_at.next(name, "mean"))
                    reader[6] = (VECTOR, (name, "centred"))
                claim(7)
                for k in range(chunks):
                    pe.wait_ge(scalar_out, scalar_at.find(name, "sq", k))
                    m = nc.tensor.matmul(bank[7][:], inv[n][:], sq[:, k, :], start=k == 0, stop=k == chunks - 1)
                m.then_inc(tensor_out, tensor_at.next(name, "ms"))
                reader[7] = (SCALAR, (name, "root"))

            def head_sum(name, k, sq):
                if k % 8 == 0:
                    claim(4)
                pe.wait_ge(scalar_out, scalar_at.find(name, "sq", k))
                m = nc.tensor.matmul(bank[4][0:8, :], pick(k % 8), sq, start=k % 8 == 0, stop=k % 8 == 7)
                m.then_inc(tensor_out, tensor_at.next(name, "sum", k))
                reader[4] = (SCALAR, (name, "root", k // 8))

            def head_spread(name, k, factors):
                claim(5 + k % 3)
                pe.wait_ge(vector_out, vector_at.find(name, "factors", k // 8))
                m = nc.tensor.matmul(bank[5 + k % 3][:], sel(k % 8), factors, start=True, stop=True)
                m.then_inc(tensor_out, tensor_at.next(name, "spread", k))
                reader[5 + k % 3] = (VECTOR, (name, "out", k))

            def attention(name, steps, between=None):
                N = len(steps)
                for n in range(N + 3):
                    if n < N:
                        st, b = steps[n], 2 + n % 3
                        claim(b)
                        W = st["w"]
                        nc.tensor.matmul(bank[b][:, 0:W], st["q"], st["k"], start=True, stop=False)
                        for x, (l, r, c0, c1) in enumerate(st["more"]):
                            m = nc.tensor.matmul(bank[b][:, c0:c1], l, r, start=False, stop=x == len(st["more"]) - 1)
                        m.then_inc(tensor_out, tensor_at.next(name, "logits", n))
                        reader[b] = (SCALAR, (name, "exp", n))
                    if 2 <= n < N + 2:
                        k, st = n - 2, steps[n - 2]
                        b = 5 + k % 2
                        claim(b)
                        pe.wait_ge(vector_out, vector_at.find(name, "p", k))
                        for j in range(st["w"] // P):
                            m = nc.tensor.transpose(bank[b][:, j * P:(j + 1) * P], st["ps"][:, j * P:(j + 1) * P], ident)
                        m.then_inc(tensor_out, tensor_at.next(name, "t", k))
                        reader[b] = (SCALAR, (name, "pt", k))
                    if n >= 3:
                        k, st = n - 3, steps[n - 3]
                        b = st["ob"]
                        if st["claim"]:
                            claim(b)
                        pe.wait_ge(scalar_out, scalar_at.find(name, "pt", k))
                        J = st["w"] // P
                        for j in range(J):
                            m = nc.tensor.matmul(bank[b][:, st["oc"]:st["oc"] + P], st["v"][j], st["ts"][:, j * P:(j + 1) * P],
                                                 start=st["start"] and j == 0, stop=st["stop"] and j == J - 1)
                        m.then_inc(tensor_out, tensor_at.next(name, "pv", k))
                        if st["last"]:
                            reader[b] = (VECTOR if name == "dsa" else SCALAR, (name, "o", st["o"]))
                    if between is not None:
                        between(n)

            def decayed(name, steps):
                N = len(steps)
                for n in range(N + 2):
                    if n < N:
                        st = steps[n]
                        c0 = st["j"] * P
                        W = SEQ - c0
                        b = 2 + n % 2
                        claim(b)
                        nc.tensor.matmul(bank[b][:, 0:W], st["sel"], st["rows"], start=True, stop=False)
                        m = nc.tensor.matmul(bank[b][:, 0:P], idb[:], mtb[:], start=False, stop=True)
                        m.then_inc(tensor_out, tensor_at.next(name, "e", n))
                        reader[b] = (SCALAR, (name, "w", n))
                        if st.get("fresh", True):
                            b = 4 + n % 2
                            claim(b)
                            m = nc.tensor.matmul(bank[b][:, 0:W], st["k"], st["q"], start=True, stop=True)
                            m.then_inc(tensor_out, tensor_at.next(name, "s", n))
                            reader[b] = (SCALAR, (name, "kept", st["at"])) if "kept" in st else (VECTOR, (name, "p", n))
                    if n >= 2:
                        k, st = n - 2, steps[n - 2]
                        c0 = st["j"] * P
                        if st["first"]:
                            claim(st["num"])
                            if st["den"] == 0:
                                claim(7)
                        pe.wait_ge(vector_out, vector_at.find(name, "p", k))
                        p = scratch[:, 3 + k % 3, 0:SEQ - c0]
                        m = nc.tensor.matmul(bank[st["num"]][:, c0:], st["v"], p, start=st["first"], stop=st["last"])
                        if st["den"] is not None:
                            m = nc.tensor.matmul(bank[7][0:8, c0:], pick(st["den"]), p, start=k == 0, stop=k == N - 1)
                        m.then_inc(tensor_out, tensor_at.next(name, "pv", k))
                        if st["last"]:
                            reader[st["num"]] = (VECTOR if st["den"] is None else SCALAR, (name, "fin", st["out"]))
                            reader[7] = (VECTOR, (name, "den"))

            def ffn(l, operand):
                up, down = f"up{l}", f"down{l}"
                u0, d0 = FIRST[up], FIRST[down]
                for s in range(RING):
                    claim(s)
                with pe.Fori(0, 2 * FC // RING) as i:
                    for s in range(RING):
                        b, t = (u0 + s) % RING, (u0 + s) % 2
                        pe.wait_ge(wlo_done, RING * i + (u0 + s + 1))
                        pe.wait_ge(conv_done, RING * i + l * 2 * FC + s + 1)
                        for k in range(DC):
                            if s == 0:
                                pe.wait_ge(vector_out, vector_at.find("xl", operand, k))
                            w = slice(k * P, (k + 1) * P)
                            m = products(bank[b][:], (whi[:, t, w], wlo[:, t, w]), (xhi[:, k, :], xlo[:, k, :]), k == 0, k == DC - 1)
                        m.then_inc(units_done, 1)
                pe.wait_ge(conv_done, RING + (l + 1) * 2 * FC)
                for b in range(4, 8):
                    claim(b)

                def unit(u, weights, hidden, h, start, stop):
                    pe.wait_ge(wlo_done, weights)
                    pe.wait_ge(hlo_done, hidden)
                    for n in range(DC):
                        w = slice(n * P, (n + 1) * P)
                        m = products(bank[n][:], (whi[:, u % 2, w], wlo[:, u % 2, w]), (xhi[:, h, :], xlo[:, h, :]), start, stop)
                        if stop and n < DC - 1:
                            m.then_inc(tensor_out, tensor_at.next(down, "sum", n))
                    m.then_inc(units_done, 1)

                unit(d0, d0 + 1, l * FC + 1, 0, True, False)
                with pe.Fori(0, (FC - 2) // RING) as i:
                    for s in range(RING):
                        unit(d0 + 1 + s, RING * i + (d0 + 2 + s), RING * i + (l * FC + 2 + s), (1 + s) % 2, False, False)
                unit(d0 + FC - 1, d0 + FC, (l + 1) * FC, (FC - 1) % 2, False, True)
                for b in range(8):
                    reader[b] = (VECTOR, ("read", down, b))

            def columns(name, parts, n):
                claim(4)
                pe.wait_ge(vector_out, vector_at.find(name, "rows"))
                pe.wait_ge(scalar_out, scalar_at.find(name, "rows"))
                for c0, src in parts:
                    m = nc.tensor.matmul(bank[4][:, c0:c0 + n], src, con[0:n, K_ID:K_ID + n], start=True, stop=True)
                m.then_inc(tensor_out, tensor_at.next(name, "cols"))
                reader[4] = (VECTOR, (name, "cols"))

            run_units("small0", SCALAR, "x")
            pe.wait_ge(in_sem, 16 * nloads)
            pe.wait_ge(gpsimd_out, gpsimd_at.find("setup"))
            pe.wait_ge(vector_out, vector_at.find("setup"))
            run_units("mq", VECTOR)
            run_units("mk", SCALAR)
            run_moving("mv", HALF, bias_v[:, 0, :])
            run_units("fq", VECTOR)
            run_units("fk", SCALAR)
            run_moving("fv", HALF, bias_v[:, 1, :])
            run_units("mo", SCALAR)
            columns("gate0", [(tt * 4, row[62][0:4, tt * P:(tt + 1) * P]) for tt in range(TILES)], 4)
            stage_end(pe, tensor_at, "in0")

            def head_norms(n):
                h = (n - 2) // 2
                if n in (2, 4, 6, 8):
                    claim(7)
                    pe.wait_ge(vector_out, vector_at.find("ml", "factors"))
                    nc.tensor.matmul(bank[7][:], sel(h), scratch[0:8, 9, :], start=True, stop=True).then_inc(tensor_out, tensor_at.next("ml", "spread", h))
                    reader[7] = (VECTOR, ("ml", "divided", h))
                elif n in (3, 5, 7, 9):
                    claim(7)
                    nc.tensor.matmul(bank[7][:], inv[128][:], MIX[:, h, :], start=True, stop=True).then_inc(tensor_out, tensor_at.next("hn", "mean", h))
                    reader[7] = (VECTOR, ("hn", "xc", h))
                elif n == 11:
                    claim(7)
                    for h in range(4):
                        pe.wait_ge(scalar_out, scalar_at.find("hn", "sq", h))
                        m = nc.tensor.matmul(bank[7][0:8, :], pick(h), scratch[:, 10 + h, :], start=h == 0, stop=h == 3)
                    m.then_inc(tensor_out, tensor_at.next("hn", "ms"))
                    reader[7] = (SCALAR, ("hn", "root"))
                elif 15 <= n < 19:
                    h = n - 15
                    claim(7)
                    pe.wait_ge(vector_out, vector_at.find("hn", "factors"))
                    nc.tensor.matmul(bank[7][:], sel(h), scratch[0:8, 14, :], start=True, stop=True).then_inc(tensor_out, tensor_at.next("hn", "spread", h))
                    reader[7] = (VECTOR, ("hn", "out", h))

            decayed("ml", ml_steps)
            tensor_at.mark("stage", "ml")
            attention("fox", fox_steps, head_norms)
            stage_end(pe, tensor_at, "mix0")
            run_units("out0", VECTOR, "mix0")
            norm("ln1_0", DC, 1024, X, MIX, True)
            tensor_at.mark("stage", "ln1_0")
            if on("up0"):
                ffn(0, "ln1_0")
                norm("ln2_0", DC, 1024, X, MIX, True)
                tensor_at.mark("stage", "ln2_0")
            if on("small1"):
                run_units("small1", SCALAR, "ln2_0")
                run_units("xbc", VECTOR)
                run_units("pool", SCALAR)

                def values_and_pool(j):
                    if j == 0:
                        gates_1()
                    claim(4 + j % 2)
                    pe.wait_ge(scalar_out, scalar_at.find("xbc", j))
                    for tt in range(TILES):
                        m = nc.tensor.transpose(bank[4 + j % 2][:, tt * P:(tt + 1) * P], xbc[:, j, tt * P:(tt + 1) * P], ident)
                    m.then_inc(tensor_out, tensor_at.next("xt", j))
                    reader[4 + j % 2] = (VECTOR, ("xp", j))
                    claim(6 + j % 2)
                    pe.wait_ge(vector_out, vector_at.find("pooled", j))
                    m = nc.tensor.matmul(bank[6 + j % 2][:], pw[:, j, :], U[:, 4 + j, :], start=True, stop=True)
                    m.then_inc(tensor_out, tensor_at.next("poolmm", j))
                    reader[6 + j % 2] = (VECTOR, ("poolout", j))

                def gates_1():
                    columns("gate1", [(tt * 8, row[58][0:8, tt * P:(tt + 1) * P]) for tt in range(TILES)]
                            + [(32 + tt * 8, row[60 + tt][0:8, tt * P:(tt + 1) * P]) for tt in range(TILES)], 8)

                run_units("z1", SCALAR, after=values_and_pool)
                stage_end(pe, tensor_at, "in1")
                decayed("ssd", ssm_steps)
                norm("ssmn", 4, 512, ys, MIX, False)
                stage_end(pe, tensor_at, "mix1")
                run_units("out1", VECTOR, "mix1")
                norm("ln1_1", DC, 1024, X, MIX, True)
                tensor_at.mark("stage", "ln1_1")
            if on("up1"):
                ffn(1, "ln1_1")
                norm("ln2_1", DC, 1024, X, MIX, True)
                tensor_at.mark("stage", "ln2_1")
            if on("small2"):
                norm("rms1", DC, 1024, X, MIX, False)
                tensor_at.mark("stage", "rms1")
                run_units("small2", SCALAR, "rms1")
                run_units("ik", VECTOR)
                run_units("iq", SCALAR)

                def between_dq(j):
                    if j == 1:
                        columns("gate2", [(c * 40 + 8 * x, row[r][0:8, c * P:(c + 1) * P]) for x, r in enumerate((62, 64, 63, 59, 60)) for c in range(TILES)], 8)
                    if j == 2:
                        claim(6)
                        nc.tensor.matmul(bank[6][:], inv[128][:], row[65], start=True, stop=True).then_inc(tensor_out, tensor_at.next("ikn", "mean"))
                        reader[6] = (VECTOR, ("ikn", "xc"))
                    if j == 5:
                        claim(7)
                        pe.wait_ge(scalar_out, scalar_at.find("ikn", "sq"))
                        nc.tensor.matmul(bank[7][:], inv[128][:], arena[:, 52, :], start=True, stop=True).then_inc(tensor_out, tensor_at.next("ikn", "ms"))
                        reader[7] = (SCALAR, ("ikn", "root"))

                run_units("dq", SCALAR, after=between_dq)
                run_units("dk", SCALAR)
                run_moving("dv", 256, None)
                pe.wait_ge(vector_out, vector_at.find("ikn", "out"))
                n = 0
                for i in range(1, TILES):
                    for h in range(IDX_HEADS):
                        claim(4 + n % 4)
                        m = nc.tensor.matmul(bank[4 + n % 4][:, 0:(i + 1) * P], iq[:, h // 2, i * P:(i + 1) * P], ikp[:, h % 2, 0:(i + 1) * P], start=True, stop=True)
                        m.then_inc(tensor_out, tensor_at.next("idx", n))
                        reader[4 + n % 4] = (SCALAR, ("relu", n))
                        n += 1
                run_units("gateb", SCALAR)
                stage_end(pe, tensor_at, "topk")
                attention("dsa", dsa_steps)
                stage_end(pe, tensor_at, "dsa")
            if on("gqkv"):
                def l2_norms(j):
                    if 2 <= j < 18:
                        head_sum("l2", j - 2, arena[:, 48 + j % 3, :])
                    for k in l2_spread.get(j, ()):
                        head_spread("l2", k, row[63 + k // 8][0:8, :])

                run_units("gqkv", VECTOR, after=l2_norms)
                stage_end(pe, tensor_at, "gqkv")

                def four(b, l, r, start=True, stop=True):
                    for hh in range(4):
                        m = nc.tensor.matmul(tile(b)[:, hh, :], l(hh), r(hh), start=start, stop=stop)
                    return m

                for c in range(TILES):
                    cs = slice(c * P, (c + 1) * P)
                    for g, G in enumerate(gdn_work):
                        t, b = (c, g), 4 * g
                        claim(b)
                        for hh in range(4):
                            nc.tensor.matmul(tile(b)[:, hh, :], spread_rows(2, 4 * g + hh), parts(2, 0)[0:72, cs], start=True, stop=False)
                            m = nc.tensor.matmul(tile(b)[:, hh, :], idb[:], mtb[:], start=False, stop=True)
                        m.then_inc(tensor_out, tensor_at.next("gb", t))
                        reader[b] = (SCALAR, ("gam", t))
                        claim(b + 1)
                        four(b + 1, lambda hh: spread_rows(2, 4 * g + hh), lambda hh: parts(2, 1)[0:72, cs]).then_inc(tensor_out, tensor_at.next("bb", t))
                        reader[b + 1] = (VECTOR, ("kb", t))
                        claim(b + 2)
                        four(b + 2, lambda hh: spread_rows(2, 4 * g + hh), lambda hh: parts(2, 0)[0:72, cs]).then_inc(tensor_out, tensor_at.next("ge", t))
                        reader[b + 2] = (SCALAR, ("eg", t))
                        claim(b + 3)
                        four(b + 3, lambda hh: gk[:, 4 * g + hh, cs], lambda hh: gq[:, 4 * g + hh, cs]).then_inc(tensor_out, tensor_at.next("kq", t))
                        reader[b + 3] = (VECTOR, ("att", t))
                    for g, G in enumerate(gdn_work):
                        t, b = (c, g), 4 * g
                        claim(b + 1)
                        pe.wait_ge(vector_out, vector_at.find("kb", t))
                        four(b + 1, lambda hh: gk[:, 4 * g + hh, cs], lambda hh: G["kb"][:, hh, :]).then_inc(tensor_out, tensor_at.next("kk", t))
                        reader[b + 1] = (VECTOR, ("at", t))
                        claim(b)
                        for hh in range(4):
                            m = nc.tensor.transpose(tile(b)[:, hh, :], gk[:, 4 * g + hh, cs], ident)
                        m.then_inc(tensor_out, tensor_at.next("kt", t))
                        reader[b] = (SCALAR, ("kd", t))
                        claim(b + 2)
                        for hh in range(4):
                            m = nc.tensor.transpose(tile(b + 2)[:, hh, :], gv[:, 4 * g + hh, cs], ident)
                        m.then_inc(tensor_out, tensor_at.next("vt", t))
                        reader[b + 2] = (SCALAR, ("vb", t))
                    for g, G in enumerate(gdn_work):
                        t, b = (c, g), 4 * g
                        claim(b + 3)
                        pe.wait_ge(vector_out, vector_at.find("lt", t, 0))
                        for hh in range(4):
                            m = nc.tensor.transpose(tile(b + 3)[:, hh, :], G["lt"][:, hh, :], ident)
                        m.then_inc(tensor_out, tensor_at.next("l0", t))
                        reader[b + 3] = (VECTOR, ("t", t, 0))
                    for r in range(1, LEVELS):
                        for g, G in enumerate(gdn_work):
                            t, b = (c, g), 4 * g
                            claim(b)
                            pe.wait_ge(vector_out, vector_at.find("lt", t, r))
                            pe.wait_ge(vector_out, vector_at.find("t", t, r - 1))
                            four(b, lambda hh: G["lt"][:, hh, :], lambda hh: G["t"][:, hh, :]).then_inc(tensor_out, tensor_at.next("x", t, r))
                            reader[b] = (SCALAR, ("xs", t, r))
                        for g, G in enumerate(gdn_work):
                            t, b = (c, g), 4 * g
                            pe.wait_ge(scalar_out, scalar_at.find("xs", t, r))
                            pe.wait_ge(vector_out, vector_at.find("u", t, r - 1))
                            if r < LEVELS - 1:
                                claim(b + 2)
                                four(b + 2, lambda hh: G["u"][:, hh, :], lambda hh: G["xs"][:, hh, :]).then_inc(tensor_out, tensor_at.next("yt", t, r))
                                reader[b + 2] = (VECTOR, ("t", t, r))
                            claim(b + 1)
                            four(b + 1, lambda hh: G["xs"][:, hh, :], lambda hh: G["u"][:, hh, :]).then_inc(tensor_out, tensor_at.next("y", t, r))
                            reader[b + 1] = (VECTOR, ("u", t, r))
                    for g, G in enumerate(gdn_work):
                        t, b = (c, g), 4 * g
                        claim(b + 3)
                        pe.wait_ge(scalar_out, scalar_at.find("kd", t))
                        pe.wait_ge(vector_out, vector_at.find("u", t, LEVELS - 1))
                        four(b + 3, lambda hh: G["kbe"][:, hh, :], lambda hh: G["u"][:, hh, :]).then_inc(tensor_out, tensor_at.next("w", t))
                        reader[b + 3] = (SCALAR, ("nw", t))
                    for g, G in enumerate(gdn_work):
                        t, b = (c, g), 4 * g
                        claim(b)
                        pe.wait_ge(scalar_out, scalar_at.find("nw", t))
                        for hh in range(4):
                            m = nc.tensor.matmul(tile(b)[:, hh, :], G["u"][:, hh, :], G["vb"][:, hh, :], start=True, stop=c == 0)
                            if c:
                                m = nc.tensor.matmul(tile(b)[:, hh, :], G["nw"][:, hh, :], state[:, g, hh, :], start=False, stop=True)
                        m.then_inc(tensor_out, tensor_at.next("vn", t))
                        reader[b] = (SCALAR, ("vn", t))
                    for g, G in enumerate(gdn_work):
                        t, b = (c, g), 4 * g
                        claim(b + 1)
                        claim(b + 2)
                        pe.wait_ge(scalar_out, scalar_at.find("vn", t))
                        pe.wait_ge(vector_out, vector_at.find("qg", t))
                        for hh in range(4):
                            m = nc.tensor.matmul(tile(b + 1)[:, hh, :], G["vn"][:, hh, :], G["att"][:, hh, :], start=True, stop=c == 0)
                            if c:
                                m = nc.tensor.matmul(tile(b + 1)[:, hh, :], state[:, g, hh, :], G["qg"][:, hh, :], start=False, stop=True)
                        m.then_inc(tensor_out, tensor_at.next("o", t))
                        reader[b + 1] = (SCALAR, ("o", t))
                        four(b + 2, lambda hh: G["kd"][:, hh, :], lambda hh: G["vn"][:, hh, :]).then_inc(tensor_out, tensor_at.next("s", t))
                        reader[b + 2] = (VECTOR, ("s", t))
                stage_end(pe, tensor_at, "gdn")

                def gn_norms(j):
                    if j == 0:
                        for k in range(8):
                            head_sum("gn", k, arena[:, 32 + k, :])
                    for k in gn_spread.get(j, ()):
                        head_spread("gn", k, row[63][0:8, :])

                run_units("z2", SCALAR, "again", after=gn_norms)
                run_units("gatea", SCALAR)
                tensor_at.mark("stage", "mix2")
                run_units("out2", VECTOR, "mix2")
                norm("rms2", DC, 1024, X, gq, False)
                tensor_at.mark("stage", "rms2")
            if on("up2"):
                ffn(2, "rms2")
                norm("rmsf", DC, 1024, X, MIX, False)

        @block.scalar
        def _(act):
            A = nc.scalar.activation

            split = [0]

            def split_units(end):
                for v in range(split[0], min(end, last_unit + 1) + 1):
                    act.wait_ge(ring_sem[v % RING], 16 * (v // RING + 1))
                    if v >= 2:
                        act.wait_ge(units_done, v - 1)
                    A(whi[:, v % 2, :], ring[:, v % RING, :], ACT.Copy).then_inc(whi_done, 1)
                split[0] = max(split[0], end + 1)

            def passing(name):
                split_units(FIRST[name] + COUNT[name] + 1)

            def unit_done(name, j):
                split_units(FIRST[name] + j + 2)
                act.wait_ge(units_done, FIRST[name] + j + 1)

            def split_operand(name, src, ready=None):
                for k in range(DC):
                    if ready is not None:
                        act.wait_ge(vector_out, vector_at.find(*ready, k))
                    A(xhi[:, k, :], src[:, k, :], ACT.Copy).then_inc(scalar_out, scalar_at.next("xh", name, k))

            def evac(name, func, dst, bias=0.0, scale=1.0, wait=None):
                for j in range(COUNT[name]):
                    unit_done(name, j)
                    if wait is not None:
                        wait(j)
                    b = bias(j) if callable(bias) else bias
                    A(dst(j), bank[(FIRST[name] + j) % RING][:], func, bias=b, scale=scale).then_inc(scalar_out, scalar_at.next("read", name, j))

            def root(b, dst, eps, *key):
                e = small[:, 250:251] if eps == LN_EPS else small[:, 251:252]
                A(dst, bank[b][:], ACT.Sqrt, bias=e).then_inc(scalar_out, scalar_at.next(*key))

            def norm(name, chunks, xs, sq, mean, eps, affine=None, operand=True):
                A(small[:, 252:253], small[:, 250:251], ACT.Sqrt).then_inc(scalar_out, scalar_at.next())
                for k in range(chunks):
                    if name == "rms1":
                        act.wait_ge(scalar_out, scalar_at.find("ln2_1", "out", k))
                    else:
                        act.wait_ge(vector_out, vector_at.find(name, "xc" if mean else "x", k))
                    A(sq[:, k, :], xs[:, k, :], ACT.Square).then_inc(scalar_out, scalar_at.next(name, "sq", k))
                act.wait_ge(tensor_out, tensor_at.find(name, "ms"))
                root(7, RSTD, eps, name, "root")
                if affine is not None:
                    for k in range(chunks):
                        act.wait_ge(vector_out, vector_at.find(name, "scaled", k))
                        A(X[:, k, :], U[:, k, :], ACT.Identity, bias=col(affine[1], k), scale=col(affine[0], k)).then_inc(scalar_out, scalar_at.next(name, "out", k))
                        if operand:
                            A(xhi[:, k, :], U[:, k, :], ACT.Identity, bias=col(affine[1], k), scale=col(affine[0], k)).then_inc(scalar_out, scalar_at.next("xh", name, k))

            def attention(name, steps, between=None):
                N = len(steps)
                for n in range(N + 3):
                    if n < N:
                        st, W = steps[n], steps[n]["w"]
                        act.wait_ge(vector_out, vector_at.find(name, "max", n))
                        if n >= 4:
                            act.wait_ge(tensor_out, tensor_at.find(name, "t", n - 4))
                        A(st["ps"][:, 0:W], bank[2 + n % 3][:, 0:W], ACT.Exp, bias=small[:, 200 + n % 4:201 + n % 4],
                                     accum_out=small[:, 204 + n % 4:205 + n % 4]).then_inc(scalar_out, scalar_at.next(name, "exp", n))
                    if 2 <= n < N + 2:
                        k, st = n - 2, steps[n - 2]
                        act.wait_ge(tensor_out, tensor_at.find(name, "t", k))
                        if k >= 3:
                            act.wait_ge(tensor_out, tensor_at.find(name, "pv", k - 3))
                        A(st["ts"][:, 0:st["w"]], bank[5 + k % 2][:, 0:st["w"]], ACT.Copy).then_inc(scalar_out, scalar_at.next(name, "pt", k))
                    if name != "dsa" and n >= 3 and steps[n - 3]["last"]:
                        st = steps[n - 3]
                        act.wait_ge(tensor_out, tensor_at.find(name, "pv", n - 3))
                        A(MIX[:, st["dst"], :], bank[st["ob"]][:], ACT.Copy).then_inc(scalar_out, scalar_at.next(name, "o", st["o"]))
                    if between is not None:
                        between(n)

            def decayed(name, steps):
                N = len(steps)
                for n in range(N + 3):
                    if n < N:
                        st, W = steps[n], SEQ - steps[n]["j"] * P
                        act.wait_ge(tensor_out, tensor_at.find(name, "e", n))
                        if n >= 3:
                            act.wait_ge(vector_out, vector_at.find(name, "p", n - 3))
                        A(scratch[:, n % 3, 0:W], bank[2 + n % 2][:, 0:W], ACT.Exp, bias=st["bias"]).then_inc(scalar_out, scalar_at.next(name, "w", n))
                        if st.get("fresh"):
                            act.wait_ge(tensor_out, tensor_at.find(name, "s", n))
                            A(scratch[:, st["kept"], 0:W], bank[4 + n % 2][:, 0:W], ACT.Copy).then_inc(scalar_out, scalar_at.next(name, "kept", st["at"]))
                    if n >= 3 and steps[n - 3]["last"] and steps[n - 3]["den"] is not None:
                        st = steps[n - 3]
                        act.wait_ge(tensor_out, tensor_at.find(name, "pv", n - 3))
                        A(MIX[:, st["out"], :], bank[st["num"]][:], ACT.Copy).then_inc(scalar_out, scalar_at.next(name, "fin", st["out"]))

            def ffn(l):
                u0, d0, c0 = FIRST[f"up{l}"], FIRST[f"down{l}"], COL[f"ffn{l}"]
                split_units(u0 + 1)

                def weights(v, n, done):
                    act.wait_ge(ring_sem[v % RING], n * 16 + 16 * (v // RING + 1))
                    act.wait_ge(units_done, done)
                    A(whi[:, v % 2, :], ring[:, v % RING, :], ACT.Copy).then_inc(whi_done, 1)

                with act.Fori(0, 2 * FC // RING) as i:
                    for s in range(RING):
                        b = (u0 + s) % RING
                        weights(u0 + s + 2, i, RING * i + (u0 + s + 1))
                        act.wait_ge(hid_done, 2 * i + 1 + l * FC + s // 2)
                        A(acc[:, s, :], bank[b][:], ACT.Identity, bias=par[:, bass.ds(4 * RING * i + (c0 + 4 * s + 3), 1)],
                          scale=par[:, bass.ds(4 * RING * i + (c0 + 4 * s + 2), 1)]).then_inc(acc_done, 1)
                        if s % 2:
                            act.wait_ge(conv_done, RING * i + (4 + 2 * l * FC + s))
                            A(sg[:, s // 2, :], acc[:, s - 1, :], ACT.Silu).then_inc(gate_done, 1)
                for k in range(2):
                    act.wait_ge(hid_done, 3 + l * FC + k)
                    A(xhi[:, k, :], hid[:, k, :], ACT.Copy).then_inc(hhi_done, 1)
                weights(d0 + 2, 0, d0 + 1)
                act.wait_ge(hid_done, 2 + (l + 1) * FC)
                with act.Fori(0, (FC - 2) // RING) as i:
                    for s in range(RING):
                        act.wait_ge(units_done, RING * i + (d0 + s + 1))
                        A(xhi[:, s % 2, :], hid[:, bass.ds(RING * i + s + 2, 1), :].rearrange("p a n -> p (a n)"), ACT.Copy).then_inc(hhi_done, 1)
                        weights(d0 + s + 3, i, RING * i + (d0 + s + 2))
                split[0] = d0 + FC + 1
                split_units(d0 + FC + 1)

            def softplus_tail(name):
                act.wait_ge(vector_out, vector_at.find(name, "abs"))
                A(row[57], row[57], ACT.Exp).then_inc(scalar_out, scalar_at.next())
                act.wait_ge(scalar_out, scalar_at.n)
                A(row[57], row[57], ACT.Ln, bias=1.0).then_inc(scalar_out, scalar_at.next(name, "ln"))

            split_units(0)
            for k in range(DC):
                act.wait_ge(x_sem[k // 2], 16)
                A(xhi[:, k, :], X[:, k, :], ACT.Copy).then_inc(scalar_out, scalar_at.next("xh", "x", k))
            split_units(1)
            act.wait_ge(in_sem, 16 * nloads)
            act.wait_ge(gpsimd_out, gpsimd_at.find("setup"))
            evac("small0", ACT.Identity, lambda j: row[56], bias=lambda j: col("b_small0"))
            softplus_tail("gate0")
            scalar_at.mark("gate0", "rows")
            for j in range(4):
                unit_done("mk", j)
                A(mk[:, j, :], bank[(FIRST["mk"] + j) % RING][:], ACT.Identity, bias=col("b_mk", j)).then_inc(scalar_out, scalar_at.next("read", "mk", j))
            for j in range(4):
                unit_done("fk", j)
                for e in range(2):
                    p0 = 64 * e
                    A(fk[p0:p0 + 64, 2 * j + e, :], bank[(FIRST["fk"] + j) % RING][p0:p0 + 64, :], ACT.Identity, bias=col("b_fk", j, p0, p0 + 64)).then_inc(scalar_out, scalar_at.next("read", "fk", j))
            evac("mo", ACT.Sigmoid, lambda j: gate[:, j, :], bias=lambda j: col("b_mo", j))
            stage_end(act, scalar_at, "in0")

            def head_norms(n):
                if n in (3, 5, 7, 9):
                    h = (n - 3) // 2
                    act.wait_ge(vector_out, vector_at.find("hn", "xc", h))
                    A(scratch[:, 10 + h, :], MIX[:, h, :], ACT.Square).then_inc(scalar_out, scalar_at.next("hn", "sq", h))
                elif n == 12:
                    act.wait_ge(tensor_out, tensor_at.find("hn", "ms"))
                    A(scratch[0:8, 14, :], bank[7][0:8, :], ACT.Sqrt, bias=small[0:8, 250:251], scale=1.0 / P).then_inc(scalar_out, scalar_at.next("hn", "root"))

            A(scratch[0:4, 8, :], row[60][0:4, :], ACT.Exp).then_inc(scalar_out, scalar_at.next("ml", "em"))
            decayed("ml", ml_steps)
            scalar_at.mark("stage", "ml")
            attention("fox", fox_steps, head_norms)
            stage_end(act, scalar_at, "mix0")
            split_operand("mix0", MIX)
            passing("out0")
            norm("ln1_0", DC, U, MIX, True, LN_EPS, ("ln1_g0", "ln1_b0"))
            scalar_at.mark("stage", "ln1_0")
            if on("up0"):
                ffn(0)
                norm("ln2_0", DC, U, MIX, True, LN_EPS, ("ln2_g0", "ln2_b0"))
                scalar_at.mark("stage", "ln2_0")
            if on("small1"):
                A(small[0:8, 208:209], par[0:8, COL["a_log"]:COL["a_log"] + 1], ACT.Exp).then_inc(scalar_out, scalar_at.next("ea1"))
                evac("small1", ACT.Identity, lambda j: row[56], bias=lambda j: col("dt_bias"))
                softplus_tail("gate1")
                scalar_at.mark("gate1", "rows")
                for j in range(8 + 1):
                    if j < 8:
                        unit_done("xbc", j)
                        A(xbc[:, j, :], bank[(FIRST["xbc"] + j) % RING][:], ACT.Identity, bias=col("xbc_conv", 5 * j + 4), scale=col("xbc_conv", 5 * j + 3)).then_inc(scalar_out, scalar_at.next("xa", j))
                    if j >= 1:
                        act.wait_ge(vector_out, vector_at.find("read", "xbc", j - 1))
                        A(xbc[:, j - 1, :], xbc[:, j - 1, :], ACT.Silu).then_inc(scalar_out, scalar_at.next("xbc", j - 1))
                act.wait_ge(gpsimd_out, gpsimd_at.find("pads1"))
                evac("pool", ACT.Copy, lambda j: pbuf[j][:, 16:16 + SEQ])
                evac("z1", ACT.Silu, lambda j: gate[:, j, :])
                stage_end(act, scalar_at, "in1")
                decayed("ssd", ssm_steps)
                norm("ssmn", 4, ys, MIX, False, LN_EPS)
                stage_end(act, scalar_at, "mix1")
                split_operand("mix1", MIX)
                passing("out1")
                norm("ln1_1", DC, U, MIX, True, LN_EPS, ("ln1_g1", "ln1_b1"))
                scalar_at.mark("stage", "ln1_1")
            if on("up1"):
                ffn(1)
                norm("ln2_1", DC, U, MIX, True, LN_EPS, ("ln2_g1", "ln2_b1"), operand=False)
                scalar_at.mark("stage", "ln2_1")
            if on("small2"):
                norm("rms1", DC, X, MIX, False, RMS_EPS)
                split_operand("rms1", U, ("rms1", "out"))
                scalar_at.mark("stage", "rms1")
                A(small[0:8, 208:209], par[0:8, COL["g_a_log"]:COL["g_a_log"] + 1], ACT.Exp).then_inc(scalar_out, scalar_at.next("ea2"))
                unit_done("small2", 0)
                b = bank[FIRST["small2"] % RING]
                A(row[56], b[:], ACT.Identity, bias=col("g_dt_bias")).then_inc(scalar_out, scalar_at.next("pre2"))
                A(row[60][0:8, :], b[64:72, :], ACT.Copy, scale=(IDX_HEADS ** -0.5) * (64 ** -0.5)).then_inc(scalar_out, scalar_at.next())
                A(row[59][0:8, :], b[32:40, :], ACT.Sigmoid).then_inc(scalar_out, scalar_at.next("read", "small2", 0))
                softplus_tail("gate2")
                evac("iq", ACT.Copy, lambda j: iq[:, j, :])
                act.wait_ge(vector_out, vector_at.find("dG"))
                A(row[63][0:8, :], row[63][0:8, :], ACT.Exp).then_inc(scalar_out, scalar_at.next())
                A(row[64][0:8, :], row[62][0:8, :], ACT.Exp).then_inc(scalar_out, scalar_at.next("eG"))
                scalar_at.mark("gate2", "rows")

                def key_norm(j):
                    if j == 4:
                        act.wait_ge(vector_out, vector_at.find("ikn", "xc"))
                        A(arena[:, 52, :], row[65], ACT.Square).then_inc(scalar_out, scalar_at.next("ikn", "sq"))
                    if j == 6:
                        act.wait_ge(tensor_out, tensor_at.find("ikn", "ms"))
                        root(7, RSTD, RMS_EPS, "ikn", "root")

                evac("dq", ACT.Copy, lambda j: dq[:, j, :], scale=P ** -0.5, wait=key_norm)
                evac("dk", ACT.Copy, lambda j: dk[:, j, :])
                passing("dv")
                n = 0
                for i in range(1, TILES):
                    for h in range(IDX_HEADS):
                        act.wait_ge(tensor_out, tensor_at.find("idx", n))
                        if n >= 4:
                            act.wait_ge(vector_out, vector_at.find("sc", n - 4))
                        A(arena[:, 48 + n % 4, 0:(i + 1) * P], bank[4 + n % 4][:, 0:(i + 1) * P], ACT.Relu).then_inc(scalar_out, scalar_at.next("relu", n))
                        n += 1
                evac("gateb", ACT.Sigmoid, lambda j: MIX[:, j, :], bias=lambda j: col("gate_b", 8 + j))
                stage_end(act, scalar_at, "topk")
                attention("dsa", dsa_steps)
                stage_end(act, scalar_at, "dsa")
            if on("gqkv"):
                for j in range(24 + 1):
                    if j < 24:
                        unit_done("gqkv", j)
                        A(arena[:, 24 + j, :], bank[(FIRST["gqkv"] + j) % RING][:], ACT.Copy, scale=col("gqkv_conv", 4 * j + 3)).then_inc(scalar_out, scalar_at.next("ga", j))
                    if j >= 1:
                        act.wait_ge(vector_out, vector_at.find("read", "gqkv", j - 1))
                        A(arena[:, 23 + j, :], arena[:, 23 + j, :], ACT.Silu).then_inc(scalar_out, scalar_at.next("gqkv", j - 1))
                    if 1 <= j <= 16:
                        k = j - 1
                        act.wait_ge(scalar_out, scalar_at.find("gqkv", k))
                        if k >= 3:
                            act.wait_ge(tensor_out, tensor_at.find("l2", "sum", k - 3))
                        A(arena[:, 48 + (k + 2) % 3, :], arena[:, 24 + k, :], ACT.Square).then_inc(scalar_out, scalar_at.next("l2", "sq", k))
                    if j in (10, 18):
                        act.wait_ge(tensor_out, tensor_at.find("l2", "sum", j - 3))
                        A(row[63 + j // 18][0:8, :], bank[4][0:8, :], ACT.Sqrt, bias=small[0:8, 251:252]).then_inc(scalar_out, scalar_at.next("l2", "root", j // 18))
                stage_end(act, scalar_at, "gqkv")
                for c in range(TILES):

                    def cc(x, g, hh):
                        return small[:, c * 40 + 8 * x + 4 * g + hh:c * 40 + 8 * x + 4 * g + hh + 1]

                    for g, G in enumerate(gdn_work):
                        t, b = (c, g), 4 * g
                        act.wait_ge(tensor_out, tensor_at.find("gb", t))
                        if c:
                            act.wait_ge(vector_out, vector_at.find("s", (c - 1, g)))
                        for hh in range(4):
                            ng = small[:, 160 + c * 8 + 4 * g + hh:161 + c * 8 + 4 * g + hh]
                            A(G["gam"][:, hh, :], tile(b)[:, hh, :], ACT.Exp, bias=ng).then_inc(scalar_out, scalar_at.next("gam", t))
                        act.wait_ge(tensor_out, tensor_at.find("ge", t))
                        A(G["eg"], tile(b + 2), ACT.Exp).then_inc(scalar_out, scalar_at.next("eg", t))
                    for g, G in enumerate(gdn_work):
                        t, b = (c, g), 4 * g
                        act.wait_ge(tensor_out, tensor_at.find("kt", t))
                        for hh in range(4):
                            A(G["kbe"][:, hh, :], tile(b)[:, hh, :], ACT.Copy, scale=cc(1, g, hh)).then_inc(scalar_out, scalar_at.next())
                            A(G["kd"][:, hh, :], tile(b)[:, hh, :], ACT.Copy, scale=cc(2, g, hh)).then_inc(scalar_out, scalar_at.next("kd", t))
                        act.wait_ge(tensor_out, tensor_at.find("vt", t))
                        for hh in range(4):
                            A(G["vb"][:, hh, :], tile(b + 2)[:, hh, :], ACT.Copy, scale=cc(3, g, hh)).then_inc(scalar_out, scalar_at.next("vb", t))
                    for r in range(1, LEVELS):
                        for g, G in enumerate(gdn_work):
                            t, b = (c, g), 4 * g
                            act.wait_ge(tensor_out, tensor_at.find("x", t, r))
                            A(G["xs"], tile(b), ACT.Copy).then_inc(scalar_out, scalar_at.next("xs", t, r))
                    for g, G in enumerate(gdn_work):
                        t, b = (c, g), 4 * g
                        act.wait_ge(tensor_out, tensor_at.find("w", t))
                        A(G["nw"], tile(b + 3), ACT.Copy, scale=-1.0).then_inc(scalar_out, scalar_at.next("nw", t))
                    for g, G in enumerate(gdn_work):
                        t, b = (c, g), 4 * g
                        act.wait_ge(tensor_out, tensor_at.find("vn", t))
                        A(G["vn"], tile(b), ACT.Copy).then_inc(scalar_out, scalar_at.next("vn", t))
                    for g, G in enumerate(gdn_work):
                        t, b = (c, g), 4 * g
                        act.wait_ge(tensor_out, tensor_at.find("o", t))
                        A(go[:, 4 * g:4 * g + 4, c * P:(c + 1) * P], tile(b + 1), ACT.Copy).then_inc(scalar_out, scalar_at.next("o", t))
                stage_end(act, scalar_at, "gdn")
                split_operand("again", U)
                for k in range(8):
                    A(arena[:, 32 + k, :], go[:, k, :], ACT.Square).then_inc(scalar_out, scalar_at.next("gn", "sq", k))

                def gn_root(j):
                    if j == 1:
                        act.wait_ge(tensor_out, tensor_at.find("gn", "sum", 7))
                        A(row[63][0:8, :], bank[4][0:8, :], ACT.Sqrt, bias=small[0:8, 251:252], scale=1.0 / P).then_inc(scalar_out, scalar_at.next("gn", "root", 0))

                evac("z2", ACT.Silu, lambda j: arena[:, 24 + j, :], wait=gn_root)
                evac("gatea", ACT.Sigmoid, lambda j: arena[:, 24 + j, :], bias=lambda j: col("gate_b", j), wait=lambda j: act.wait_ge(vector_out, vector_at.find("z2", j)))
                scalar_at.mark("stage", "mix2")
                act.wait_ge(units_done, FIRST["gatea"] + DC)
                split_operand("mix2", MIX, ("mixed",))
                passing("out2")
                norm("rms2", DC, X, gq, False, RMS_EPS)
                split_operand("rms2", U, ("rms2", "out"))
                scalar_at.mark("stage", "rms2")
            if on("up2"):
                ffn(2)
                norm("rmsf", DC, X, MIX, False, RMS_EPS)
            src = U if on("up2") else X
            act.wait_ge(scalar_out, scalar_at.n)
            for k in range(DC):
                if on("up2"):
                    act.wait_ge(vector_out, vector_at.find("rmsf", "out", k))
                act.dma_start(out[:, k, :], src[:, k, :]).then_inc(out_sem, 16)
            act.wait_ge(out_sem, 16 * DC)

        @block.gpsimd
        def _(pool):
            for n in (128, 512, 1024):
                nc.gpsimd.memset(inv[n][:], 1.0 / n).then_inc(gpsimd_out, gpsimd_at.next())
            nc.gpsimd.memset(ones[:], 1.0).then_inc(gpsimd_out, gpsimd_at.next())
            nc.gpsimd.memset(small[:, 250:251], LN_EPS).then_inc(gpsimd_out, gpsimd_at.next())
            nc.gpsimd.memset(small[:, 251:252], RMS_EPS).then_inc(gpsimd_out, gpsimd_at.next())
            nc.gpsimd.memset(arena[:, 40:56, :], 0.0).then_inc(gpsimd_out, gpsimd_at.next("setup"))
            gpsimd_at.mark("stage", "in0")
            for st in ("ml", "mix0", "ln1_0"):
                gpsimd_at.mark("stage", st)
            if on("up0"):
                gpsimd_at.mark("stage", "ln2_0")
            if on("small1"):
                pool.wait_ge(tensor_out, tensor_at.find("stage", "ln2_0"))
                pool.wait_ge(scalar_out, scalar_at.find("stage", "ln2_0"))
                pool.wait_ge(vector_out, vector_at.find("stage", "ln2_0"))
                nc.gpsimd.memset(arena[:, 36:56, :], 0.0).then_inc(gpsimd_out, gpsimd_at.next("pads1"))
                for st in ("in1", "mix1", "ln1_1", "ln2_1", "rms1"):
                    gpsimd_at.mark("stage", st)
            if on("small2"):
                pool.wait_ge(tensor_out, tensor_at.find("stage", "rms1"))
                pool.wait_ge(scalar_out, scalar_at.find("stage", "rms1"))
                pool.wait_ge(vector_out, vector_at.find("stage", "rms1"))
                nc.gpsimd.memset(ikp, 0.0).then_inc(gpsimd_out, gpsimd_at.next("pads2"))
                for st in ("topk", "dsa", "gqkv", "gdn", "mix2", "rms2"):
                    gpsimd_at.mark("stage", st)

        @block.vector
        def _(dve):
            V = nc.vector
            STT = nc.vector.scalar_tensor_tensor

            split = [0]

            def split_units(end):
                for v in range(split[0], min(end, last_unit + 1) + 1):
                    dve.wait_ge(whi_done, v + 1)
                    V.tensor_tensor(wlo[:, v % 2, :], ring[:, v % RING, :], whi[:, v % 2, :], ALU.subtract).then_inc(wlo_done, 1)
                split[0] = max(split[0], end + 1)

            def passing(name):
                split_units(FIRST[name] + COUNT[name] + 1)

            def unit_done(name, j):
                split_units(FIRST[name] + j + 1)
                dve.wait_ge(units_done, FIRST[name] + j + 1)

            def split_operand(name, src):
                for k in range(DC):
                    dve.wait_ge(scalar_out, scalar_at.find("xh", name, k))
                    V.tensor_tensor(xlo[:, k, :], src[:, k, :], xhi[:, k, :], ALU.subtract).then_inc(vector_out, vector_at.next("xl", name, k))

            def norm(name, chunks, xs, mean, gain=None, dst=None, before=None, operand=None):
                if mean:
                    dve.wait_ge(tensor_out, tensor_at.find(name, "mean"))
                    for k in range(chunks):
                        V.tensor_tensor(U[:, k, :], xs[:, k, :], bank[6][:], ALU.subtract).then_inc(vector_out, vector_at.next(name, "xc", k))
                    vector_at.mark(name, "centred")
                if before is not None:
                    passing(before)
                dve.wait_ge(scalar_out, scalar_at.find(name, "root"))
                V.reciprocal(RSTD, RSTD).then_inc(vector_out, vector_at.next())
                dve.wait_ge(vector_out, vector_at.n)
                for k in range(chunks + 2):
                    if k < chunks:
                        if mean:
                            V.tensor_tensor(U[:, k, :], U[:, k, :], RSTD, ALU.mult).then_inc(vector_out, vector_at.next(name, "scaled", k))
                        else:
                            STT(dst[:, k, :], xs[:, k, :], col(gain, k), RSTD, ALU.mult, ALU.mult).then_inc(vector_out, vector_at.next(name, "out", k))
                    if operand is not None and k >= 2:
                        dve.wait_ge(scalar_out, scalar_at.find("xh", name, k - 2))
                        V.tensor_tensor(xlo[:, k - 2, :], operand[:, k - 2, :], xhi[:, k - 2, :], ALU.subtract).then_inc(vector_out, vector_at.next("xl", name, k - 2))

            def residual(name, nxt, factor, last_unit_only):
                for j in range(DC):
                    if not last_unit_only:
                        b = (FIRST[name] + j) % RING
                        dve.wait_ge(units_done, FIRST[name] + j + 1)
                    elif j < DC - 1:
                        b = j
                        dve.wait_ge(tensor_out, tensor_at.find(name, "sum", j))
                    else:
                        b = j
                        dve.wait_ge(units_done, FIRST[name] + COUNT[name])
                    STT(X[:, j, :], X[:, j, :], factor, bank[b][:], ALU.mult, ALU.add).then_inc(vector_out, vector_at.next("read", name, j))
                    vector_at.mark(nxt, "x", j)
                    if not last_unit_only and j < DC - 1:
                        split_units(FIRST[name] + j + 2)

            def conv(name, j, dst, u, taps):
                for n, (shift, w) in enumerate(taps):
                    STT(dst[:, shift:], u[:, 0:SEQ - shift], w, dst[:, shift:], ALU.mult, ALU.add).then_inc(vector_out, vector_at.next())
                    if n < len(taps) - 1:
                        dve.wait_ge(vector_out, vector_at.n)
                vector_at.mark("read", name, j)

            def attention(name, steps, between=None):
                N = len(steps)
                for n in range(N + 4):
                    if name == "dsa" and n >= 4 and steps[n - 4]["last"]:
                        st = steps[n - 4]
                        dve.wait_ge(tensor_out, tensor_at.find(name, "pv", n - 4))
                        V.tensor_tensor(MIX[:, st["dst"], :], MIX[:, st["dst"], :], bank[st["ob"]][:], ALU.mult).then_inc(vector_out, vector_at.next(name, "o", st["o"]))
                    if n < N:
                        dve.wait_ge(tensor_out, tensor_at.find(name, "logits", n))
                        if n >= 4:
                            dve.wait_ge(scalar_out, scalar_at.find(name, "exp", n - 4))
                        V.tensor_reduce(small[:, 200 + n % 4:201 + n % 4], bank[2 + n % 3][:, 0:steps[n]["w"]], AX_X, ALU.max, negate=True).then_inc(vector_out, vector_at.next(name, "max", n))
                    if 1 <= n <= N:
                        k, st = n - 1, steps[n - 1]
                        dve.wait_ge(scalar_out, scalar_at.find(name, "exp", k))
                        V.reciprocal(small[:, 204 + k % 4:205 + k % 4], small[:, 204 + k % 4:205 + k % 4]).then_inc(vector_out, vector_at.next())
                        dve.wait_ge(vector_out, vector_at.n)
                        p = st["ps"][:, 0:st["w"]]
                        V.tensor_scalar(p, p, small[:, 204 + k % 4:205 + k % 4], None, ALU.mult).then_inc(vector_out, vector_at.next(name, "p", k))
                    if between is not None:
                        between(n)

            def decayed(name, steps, finish):
                N = len(steps)
                for n in range(N + 2):
                    if n < N:
                        W = SEQ - steps[n]["j"] * P
                        dve.wait_ge(scalar_out, scalar_at.find(name, "w", n))
                        if "kept" in steps[n]:
                            dve.wait_ge(scalar_out, scalar_at.find(name, "kept", steps[n]["at"]))
                            scores = scratch[:, steps[n]["kept"], 0:W]
                        else:
                            dve.wait_ge(tensor_out, tensor_at.find(name, "s", n))
                            scores = bank[4 + n % 2][:, 0:W]
                        if n >= 3:
                            dve.wait_ge(tensor_out, tensor_at.find(name, "pv", n - 3))
                        V.tensor_tensor(scratch[:, 3 + n % 3, 0:W], scratch[:, n % 3, 0:W], scores, ALU.mult).then_inc(vector_out, vector_at.next(name, "p", n))
                    if n >= 2 and steps[n - 2]["last"]:
                        dve.wait_ge(tensor_out, tensor_at.find(name, "pv", n - 2))
                        finish(steps[n - 2])

            def ffn(l):
                c0 = COL[f"ffn{l}"]
                u0, d0 = FIRST[f"up{l}"], FIRST[f"down{l}"]
                split_units(u0 + 1)

                def weights(v, high):
                    dve.wait_ge(whi_done, high)
                    V.tensor_tensor(wlo[:, v % 2, :], ring[:, v % RING, :], whi[:, v % 2, :], ALU.subtract).then_inc(wlo_done, 1)

                with dve.Fori(0, 2 * FC // RING) as i:
                    for s in range(RING):
                        weights(u0 + s + 2, RING * i + (u0 + s + 3))
                        u = bank[(u0 + s) % RING]
                        dve.wait_ge(acc_done, RING * i + (2 * l * FC + s + 1))
                        STT(acc[:, s, 1:], u[:, 0:SEQ - 1], par[:, bass.ds(4 * RING * i + (c0 + 4 * s + 1), 1)], acc[:, s, 1:], ALU.mult, ALU.add).then_inc(tap_done, 1)
                        dve.wait_ge(tap_done, RING * i + (2 * l * FC + s + 1))
                        STT(acc[:, s, 2:], u[:, 0:SEQ - 2], par[:, bass.ds(4 * RING * i + (c0 + 4 * s), 1)], acc[:, s, 2:], ALU.mult, ALU.add).then_inc(conv_done, 1)
                        if s % 2:
                            dve.wait_ge(conv_done, RING * i + (4 + 2 * l * FC + s + 1))
                            dve.wait_ge(gate_done, 2 * i + (l * FC + s // 2 + 1))
                            V.tensor_tensor(hid[:, bass.ds(2 * i + s // 2, 1), :].rearrange("p a n -> p (a n)"), sg[:, s // 2, :], acc[:, s, :], ALU.mult).then_inc(hid_done, 1)
                for k in range(2):
                    dve.wait_ge(hhi_done, l * FC + k + 1)
                    V.tensor_tensor(xlo[:, k, :], hid[:, k, :], xhi[:, k, :], ALU.subtract).then_inc(hlo_done, 1)
                weights(d0 + 2, d0 + 3)
                with dve.Fori(0, (FC - 2) // RING) as i:
                    for s in range(RING):
                        dve.wait_ge(hhi_done, RING * i + (l * FC + s + 3))
                        V.tensor_tensor(xlo[:, s % 2, :], hid[:, bass.ds(RING * i + s + 2, 1), :].rearrange("p a n -> p (a n)"), xhi[:, s % 2, :], ALU.subtract).then_inc(hlo_done, 1)
                        weights(d0 + s + 3, RING * i + (d0 + s + 4))
                split[0] = d0 + FC + 1

            def clear_parts(layer):
                V.tensor_copy(parts_space[layer][0], con[:, K_SEL:K_SEL + 8 * P]).then_inc(vector_out, vector_at.next())
                for space in parts_space[layer][1:]:
                    V.memset(space, 0.0).then_inc(vector_out, vector_at.next())

            def split_rows(layer, which, src, n, c0, rest, mid):
                to, src, rest, mid = parts(layer, which)[:, c0:], src[0:n, c0:], rest[0:n, c0:], mid[0:n, c0:SEQ]
                dve.wait_ge(vector_out, vector_at.n)
                V.tensor_copy(to[0:n, :], src).then_inc(vector_out, vector_at.next())
                dve.wait_ge(vector_out, vector_at.n)
                V.tensor_tensor(rest, src, to[0:n, :], ALU.subtract).then_inc(vector_out, vector_at.next())
                dve.wait_ge(vector_out, vector_at.n)
                V.tensor_copy(mid, rest).then_inc(vector_out, vector_at.next())
                dve.wait_ge(vector_out, vector_at.n)
                V.tensor_tensor(rest, rest, mid, ALU.subtract).then_inc(vector_out, vector_at.next())
                V.tensor_copy(to[32:32 + n, :], mid).then_inc(vector_out, vector_at.next())
                dve.wait_ge(vector_out, vector_at.n)
                V.tensor_copy(to[64:64 + n, :], rest).then_inc(vector_out, vector_at.next("parts", layer))

            def absolute(name, key):
                dve.wait_ge(scalar_out, scalar_at.find(*key))
                STT(row[57], row[56], -1.0, row[56], ALU.mult, ALU.min).then_inc(vector_out, vector_at.next(name, "abs"))

            split_units(0)
            for k in range(DC):
                dve.wait_ge(x_sem[k // 2], 16)
                dve.wait_ge(scalar_out, scalar_at.find("xh", "x", k))
                V.tensor_tensor(xlo[:, k, :], X[:, k, :], xhi[:, k, :], ALU.subtract).then_inc(vector_out, vector_at.next("xl", "x", k))
            split_units(1)
            dve.wait_ge(in_sem, 16 * nloads)
            V.tensor_copy(idb[:], ident).then_inc(vector_out, vector_at.next())
            V.tensor_copy(mtb[:], con[:, K_MT:K_MT + P]).then_inc(vector_out, vector_at.next())
            V.tensor_copy(mqb[:], con[:, K_MQ:K_MQ + P]).then_inc(vector_out, vector_at.next("setup"))
            for n in range(RING):
                V.memset(small[:, 210 + n:211 + n], 0.0).then_inc(conv_done, 1)
            for n in range(2):
                V.memset(small[:, 214 + n:215 + n], 0.0).then_inc(hid_done, 1)
            dve.wait_ge(gpsimd_out, gpsimd_at.find("setup"))
            absolute("gate0", ("read", "small0", 0))
            dve.wait_ge(scalar_out, scalar_at.find("gate0", "ln"))
            STT(row[58], row[56], 0.0, row[57], ALU.min, ALU.subtract).then_inc(vector_out, vector_at.next())
            dve.wait_ge(vector_out, vector_at.n)
            V.tensor_tensor_scan(row[59], ones[:], row[58], 0.0, ALU.mult, ALU.add).then_inc(vector_out, vector_at.next())
            dve.wait_ge(vector_out, vector_at.n)
            V.tensor_scalar(row[61][0:8, :], row[59][64:72, :], -1.0, None, ALU.mult).then_inc(vector_out, vector_at.next())
            V.tensor_copy(row[60][0:4, :], row[59][32:36, :]).then_inc(vector_out, vector_at.next())
            dve.wait_ge(vector_out, vector_at.n)
            V.tensor_tensor(row[62][0:4, :], row[56][0:4, :], row[60][0:4, :], ALU.subtract).then_inc(vector_out, vector_at.next())
            dve.wait_ge(vector_out, vector_at.n)
            V.tensor_tensor_scan(row[63][0:4, :], row[62][0:4, :], row[62][0:4, :], 0.0, ALU.max, ALU.max).then_inc(vector_out, vector_at.next())
            dve.wait_ge(vector_out, vector_at.n)
            V.tensor_scalar(row[64][0:4, :], row[63][0:4, :], -1.0, None, ALU.mult).then_inc(vector_out, vector_at.next())
            STT(row[60][0:4, :], row[60][0:4, :], -1.0, row[63][0:4, :], ALU.mult, ALU.subtract).then_inc(vector_out, vector_at.next("gate0", "rows"))
            for j in range(4):
                unit_done("mq", j)
                V.tensor_scalar(mq[:, j, :], bank[(FIRST["mq"] + j) % RING][:], col("b_mq", j), P ** -0.5, ALU.add, ALU.mult).then_inc(vector_out, vector_at.next("read", "mq", j))
            for tt in range(TILES):
                unit_done("mv", COUNT["mv"] - 1)
                V.tensor_copy(mv[:, tt, :], bank[tt][:]).then_inc(vector_out, vector_at.next("read", "mv", tt))
            for j in range(4):
                unit_done("fq", j)
                V.tensor_scalar(fq[:, j, :], bank[(FIRST["fq"] + j) % RING][:], col("b_fq", j), 64 ** -0.5, ALU.add, ALU.mult).then_inc(vector_out, vector_at.next("read", "fq", j))
            for tt in range(TILES):
                unit_done("fv", COUNT["fv"] - 1)
                for e in range(2):
                    dst = fv[:, tt, :, :].rearrange("p (c e) d -> p c e d", e=2)[:, :, e, 64 * e:64 * e + 64]
                    src = bank[tt][:].rearrange("p (c e d) -> p c e d", e=2, d=64)[:, :, e, :]
                    V.tensor_copy(dst, src).then_inc(vector_out, vector_at.next("read", "fv", tt))
            passing("mo")
            dve.wait_ge(tensor_out, tensor_at.find("gate0", "cols"))
            V.tensor_copy(small[:, 0:16], bank[4][:, 0:16]).then_inc(vector_out, vector_at.next("gate0", "cols"))
            clear_parts(0)
            split_rows(0, 0, row[64], 4, 0, arena[:, 14, :], arena[:, 15, :].bitcast(BF16))
            split_rows(0, 1, row[61], 8, 0, arena[:, 14, :], arena[:, 15, :].bitcast(BF16))
            stage_end(dve, vector_at, "in0")

            V.memset(scratch[0:8, 9, :], 1.0).then_inc(vector_out, vector_at.next())
            decayed("ml", ml_steps, lambda st: None)
            vector_at.mark("stage", "ml")
            den = scratch[0:4, 9, :]
            dve.wait_ge(tensor_out, tensor_at.find("ml", "pv", len(ml_steps) - 1))
            dve.wait_ge(scalar_out, scalar_at.find("ml", "em"))
            dve.wait_ge(vector_out, vector_at.n)
            STT(den, bank[7][0:4, :], -1.0, scratch[0:4, 8, :], ALU.mult, ALU.max).then_inc(vector_out, vector_at.next())
            dve.wait_ge(vector_out, vector_at.n)
            V.tensor_tensor(den, bank[7][0:4, :], den, ALU.max).then_inc(vector_out, vector_at.next("ml", "den"))
            dve.wait_ge(vector_out, vector_at.n)
            V.reciprocal(den, den).then_inc(vector_out, vector_at.next("ml", "factors"))

            def head_norms(n):
                h = (n - 2) // 2
                if n in (2, 4, 6, 8):
                    dve.wait_ge(tensor_out, tensor_at.find("ml", "spread", h))
                    dve.wait_ge(scalar_out, scalar_at.find("ml", "fin", h))
                    V.tensor_tensor(MIX[:, h, :], MIX[:, h, :], bank[7][:], ALU.mult).then_inc(vector_out, vector_at.next("ml", "divided", h))
                elif n in (3, 5, 7, 9):
                    dve.wait_ge(tensor_out, tensor_at.find("hn", "mean", h))
                    V.tensor_tensor(MIX[:, h, :], MIX[:, h, :], bank[7][:], ALU.subtract).then_inc(vector_out, vector_at.next("hn", "xc", h))
                elif n == 13:
                    dve.wait_ge(scalar_out, scalar_at.find("hn", "root"))
                    V.reciprocal(scratch[0:8, 14, :], scratch[0:8, 14, :]).then_inc(vector_out, vector_at.next("hn", "factors"))
                elif 15 <= n < 19:
                    h = n - 15
                    dve.wait_ge(tensor_out, tensor_at.find("hn", "spread", h))
                    STT(MIX[:, h, :], MIX[:, h, :], col("ml_norm", h), bank[7][:], ALU.mult, ALU.mult).then_inc(vector_out, vector_at.next("hn", "out", h))

            attention("fox", fox_steps, head_norms)
            for j in range(4):
                dve.wait_ge(scalar_out, scalar_at.find("read", "mo", j))
                V.tensor_tensor(MIX[:, j, :], MIX[:, j, :], gate[:, j, :], ALU.mult).then_inc(vector_out, vector_at.next("mo", j))
            stage_end(dve, vector_at, "mix0")
            split_operand("mix0", MIX)
            residual("out0", "ln1_0", ALPHA, False)
            norm("ln1_0", DC, X, True, before="out0", operand=X)
            vector_at.mark("stage", "ln1_0")
            if on("up0"):
                ffn(0)
                residual("down0", "ln2_0", ALPHA, True)
                norm("ln2_0", DC, X, True, before="down0", operand=X)
                vector_at.mark("stage", "ln2_0")
            if on("small1"):
                absolute("gate1", ("read", "small1", 0))
                dve.wait_ge(scalar_out, scalar_at.find("gate1", "ln"))
                STT(row[58], row[56], 0.0, row[57], ALU.max, ALU.add).then_inc(vector_out, vector_at.next())
                dve.wait_ge(vector_out, vector_at.n)
                dve.wait_ge(scalar_out, scalar_at.find("ea1"))
                V.tensor_scalar(row[59][0:8, :], row[58][0:8, :], small[0:8, 208:209], -1.0, ALU.mult, ALU.mult).then_inc(vector_out, vector_at.next())
                dve.wait_ge(vector_out, vector_at.n)
                for j in range(TILES):
                    V.tensor_tensor_scan(row[60 + j][0:8, j * P:], ones[0:8, j * P:], row[59][0:8, j * P:], 0.0, ALU.mult, ALU.add).then_inc(vector_out, vector_at.next())
                vector_at.mark("gate1", "rows")
                for j in range(8):
                    split_units(FIRST["xbc"] + j + 2)
                    dve.wait_ge(scalar_out, scalar_at.find("xa", j))
                    conv("xbc", j, xbc[:, j, :], bank[(FIRST["xbc"] + j) % RING], [(s, col("xbc_conv", 5 * j + 3 - s)) for s in (1, 2, 3)])
                    if j == 0:
                        dve.wait_ge(gpsimd_out, gpsimd_at.find("pads1"))
                        clear_parts(1)
                    if j % 2:
                        split_rows(1, j // 2, row[60 + j // 2], 8, j // 2 * P, arena[:, 32, :], arena[:, 33, :].bitcast(BF16))
                dve.wait_ge(gpsimd_out, gpsimd_at.find("pads1"))
                for g, w in enumerate(POOL_WINDOWS):
                    split_units(FIRST["pool"] + g + 2)
                    dve.wait_ge(scalar_out, scalar_at.find("read", "pool", g))
                    u, cur, s, n = pbuf[g], pbuf[g], 1, 0
                    while s < w:
                        dst = pbuf[4 + n % 2]
                        V.tensor_tensor(dst[:, 16:16 + SEQ], cur[:, 16:16 + SEQ], cur[:, 16 - s:16 - s + SEQ], ALU.add).then_inc(vector_out, vector_at.next())
                        dve.wait_ge(vector_out, vector_at.n)
                        cur, s, n = dst, 2 * s, n + 1
                    pooled = U[:, 4 + g, :]
                    STT(pooled, cur[:, 16:16 + SEQ], 1.0 / w, u[:, 16:16 + SEQ], ALU.mult, ALU.subtract).then_inc(vector_out, vector_at.next())
                    V.tensor_tensor(small[:, 64 + 16 * g:80 + 16 * g], cur[:, 16:32], con[:, K_CNT + 16 * g:K_CNT + 16 * g + 16], ALU.mult).then_inc(vector_out, vector_at.next())
                    dve.wait_ge(vector_out, vector_at.n)
                    V.tensor_tensor(pooled[:, 0:16], small[:, 64 + 16 * g:80 + 16 * g], u[:, 16:32], ALU.subtract).then_inc(vector_out, vector_at.next("pooled", g))
                split_units(FIRST["z1"] + 2)
                dve.wait_ge(tensor_out, tensor_at.find("gate1", "cols"))
                V.tensor_copy(small[:, 0:32], bank[4][:, 0:32]).then_inc(vector_out, vector_at.next())
                V.tensor_scalar(small[:, 32:64], bank[4][:, 32:64], -1.0, None, ALU.mult).then_inc(vector_out, vector_at.next("gate1", "cols"))
                dve.wait_ge(vector_out, vector_at.n)
                for c in range(4):
                    split_units(FIRST["z1"] + c + 2)
                    dve.wait_ge(tensor_out, tensor_at.find("xt", c))
                    for tt in range(TILES):
                        for e in range(2):
                            h = 2 * c + e
                            V.tensor_scalar(xpad[:, tt, h, 64 * e:64 * e + 64], bank[4 + c % 2][:, tt * P + 64 * e:tt * P + 64 * e + 64],
                                                       small[:, tt * 8 + h:tt * 8 + h + 1], None, ALU.mult).then_inc(vector_out, vector_at.next("xp", c))
                    dve.wait_ge(tensor_out, tensor_at.find("poolmm", c))
                    V.tensor_scalar(MIX[:, 4 + c, :], bank[6 + c % 2][:], col("pool_b", c), col("pool_s", c), ALU.add, ALU.mult).then_inc(vector_out, vector_at.next("poolout", c))
                stage_end(dve, vector_at, "in1")

                def ssm_finish(st):
                    c = st["out"]
                    STT(ys[:, c, :], xbc[:, c, :], col("d_skip", c), bank[st["num"]][:], ALU.mult, ALU.add).then_inc(vector_out, vector_at.next("ssd", "fin", c))

                decayed("ssd", ssm_steps, ssm_finish)
                for j in range(4):
                    dve.wait_ge(scalar_out, scalar_at.find("read", "z1", j))
                    dve.wait_ge(vector_out, vector_at.n)
                    V.tensor_tensor(ys[:, j, :], ys[:, j, :], gate[:, j, :], ALU.mult).then_inc(vector_out, vector_at.next("ssmn", "x", j))
                norm("ssmn", 4, ys, False, "ssm_norm", MIX)
                stage_end(dve, vector_at, "mix1")
                split_operand("mix1", MIX)
                residual("out1", "ln1_1", ALPHA, False)
                norm("ln1_1", DC, X, True, before="out1", operand=X)
                vector_at.mark("stage", "ln1_1")
            if on("up1"):
                ffn(1)
                residual("down1", "ln2_1", ALPHA, True)
                norm("ln2_1", DC, X, True, before="down1")
                vector_at.mark("stage", "ln2_1")
            if on("small2"):
                norm("rms1", DC, X, False, "norm1", U, operand=U)
                vector_at.mark("stage", "rms1")
                split_units(FIRST["ik"] + 1)
                absolute("gate2", ("pre2",))
                dve.wait_ge(scalar_out, scalar_at.find("gate2", "ln"))
                STT(row[58], row[56], 0.0, row[57], ALU.max, ALU.add).then_inc(vector_out, vector_at.next())
                unit_done("ik", 0)
                V.tensor_copy(row[65], bank[FIRST["ik"] % RING][:]).then_inc(vector_out, vector_at.next("read", "ik", 0))
                dve.wait_ge(vector_out, vector_at.n)
                dve.wait_ge(scalar_out, scalar_at.find("ea2"))
                V.tensor_scalar(row[61][0:8, :], row[58][0:8, :], small[0:8, 208:209], -1.0, ALU.mult, ALU.mult).then_inc(vector_out, vector_at.next())
                dve.wait_ge(vector_out, vector_at.n)
                for c in range(TILES):
                    split_units(FIRST["iq"] + c + 1)
                    V.tensor_tensor_scan(row[62][0:8, c * P:(c + 1) * P], ones[0:8, 0:P], row[61][0:8, c * P:(c + 1) * P], 0.0, ALU.mult, ALU.add).then_inc(vector_out, vector_at.next())
                    dve.wait_ge(vector_out, vector_at.n)
                    V.tensor_scalar(row[63][0:8, c * P:(c + 1) * P], row[62][0:8, c * P:(c + 1) * P], -1.0, row[62][0:8, (c + 1) * P - 1:(c + 1) * P], ALU.mult, ALU.add).then_inc(vector_out, vector_at.next())
                vector_at.mark("dG")
                passing("iq")
                dve.wait_ge(scalar_out, scalar_at.find("eG"))
                V.tensor_tensor(row[64][0:8, :], row[64][0:8, :], row[59][0:8, :], ALU.mult).then_inc(vector_out, vector_at.next("gate2", "rows"))
                split_units(FIRST["dq"] + 2)
                dve.wait_ge(tensor_out, tensor_at.find("gate2", "cols"))
                V.tensor_copy(small[:, 0:160], bank[4][:, 0:160]).then_inc(vector_out, vector_at.next())
                src = bank[4][:, 0:160].rearrange("p (c x) -> p c x", c=TILES)[:, :, 0:8]
                V.tensor_scalar(small[:, 160:192].rearrange("p (c x) -> p c x", c=TILES), src, -1.0, None, ALU.mult).then_inc(vector_out, vector_at.next("gate2", "cols"))
                dve.wait_ge(vector_out, vector_at.n)
                for j in range(3, 8):
                    split_units(FIRST["dq"] + j)
                    if j == 4:
                        dve.wait_ge(tensor_out, tensor_at.find("ikn", "mean"))
                        V.tensor_tensor(row[65], row[65], bank[6][:], ALU.subtract).then_inc(vector_out, vector_at.next("ikn", "xc"))
                passing("dq")
                dve.wait_ge(scalar_out, scalar_at.find("ikn", "root"))
                dve.wait_ge(gpsimd_out, gpsimd_at.find("pads2"))
                V.reciprocal(RSTD, RSTD).then_inc(vector_out, vector_at.next())
                dve.wait_ge(vector_out, vector_at.n)
                for e in range(2):
                    p0 = 64 * e
                    STT(ikp[p0:p0 + 64, e, :], row[65][p0:p0 + 64, :], col("ik_norm", 0, p0, p0 + 64), RSTD[p0:p0 + 64, :], ALU.mult, ALU.mult).then_inc(vector_out, vector_at.next("ikn", "out"))
                for tt in range(TILES):
                    unit_done("dv", 1)
                    V.tensor_copy(dv[:, tt, :], bank[tt][:, 0:256]).then_inc(vector_out, vector_at.next("read", "dv", tt))
                n = 0
                for i in range(1, TILES):
                    sc = score[:, i, 0:(i + 1) * P]
                    for h in range(IDX_HEADS):
                        dve.wait_ge(scalar_out, scalar_at.find("relu", n))
                        r = arena[:, 48 + n % 4, 0:(i + 1) * P]
                        w = small[:, i * 40 + 32 + h:i * 40 + 33 + h]
                        if h == 0:
                            V.tensor_scalar(sc, r, w, None, ALU.mult).then_inc(vector_out, vector_at.next("sc", n))
                            dve.wait_ge(vector_out, vector_at.n)
                        else:
                            STT(sc, r, w, sc, ALU.mult, ALU.add).then_inc(vector_out, vector_at.next("sc", n))
                            dve.wait_ge(vector_out, vector_at.n)
                        n += 1
                    V.tensor_tensor(score[:, i, i * P:(i + 1) * P], score[:, i, i * P:(i + 1) * P], con[:, K_MQ:K_MQ + P], ALU.add).then_inc(vector_out, vector_at.next())
                    dve.wait_ge(vector_out, vector_at.n)
                for rnd in range(TOPK // 8):
                    for i in range(1, TILES):
                        V.max(small[:, 216 + 8 * i:224 + 8 * i], score[:, i, 0:(i + 1) * P]).then_inc(vector_out, vector_at.next("top", rnd, i))
                    for i in range(1, TILES):
                        dve.wait_ge(vector_out, vector_at.find("top", rnd, i))
                        sc = score[:, i, 0:(i + 1) * P]
                        V.match_replace(sc, small[:, 216 + 8 * i:224 + 8 * i], sc, TAKEN).then_inc(vector_out, vector_at.next())
                    if rnd % 2:
                        split_units(FIRST["gateb"] + rnd // 2 + 2)
                    dve.wait_ge(vector_out, vector_at.n)
                for i in range(1, TILES):
                    V.tensor_scalar(madd[:, i, 0:(i + 1) * P], score[:, i, 0:(i + 1) * P], -2e38, NEG, ALU.is_ge, ALU.mult).then_inc(vector_out, vector_at.next())
                stage_end(dve, vector_at, "topk")
                passing("gateb")
                attention("dsa", dsa_steps)
                stage_end(dve, vector_at, "dsa")
            if on("gqkv"):
                for j in range(24):
                    split_units(FIRST["gqkv"] + j + 2)
                    dve.wait_ge(scalar_out, scalar_at.find("ga", j))
                    conv("gqkv", j, arena[:, 24 + j, :], bank[(FIRST["gqkv"] + j) % RING], [(s, col("gqkv_conv", 4 * j + 3 - s)) for s in (1, 2, 3)])
                    if j == 3:
                        clear_parts(2)
                        split_rows(2, 0, row[62], 8, 0, arena[:, 51, :], arena[:, 52, :].bitcast(BF16))
                        split_rows(2, 1, row[59], 8, 0, arena[:, 51, :], arena[:, 52, :].bitcast(BF16))
                    if j in (11, 19):
                        r = row[63 + j // 19][0:8, :]
                        dve.wait_ge(scalar_out, scalar_at.find("l2", "root", j // 19))
                        V.reciprocal(r, r).then_inc(vector_out, vector_at.next("l2", "factors", j // 19))
                    for k in l2_spread.get(j, ()):
                        dve.wait_ge(tensor_out, tensor_at.find("l2", "spread", k))
                        STT(arena[:, 24 + k, :], arena[:, 24 + k, :], P ** -0.5 if k < 8 else 1.0, bank[5 + k % 3][:], ALU.mult, ALU.mult).then_inc(vector_out, vector_at.next("l2", "out", k))
                stage_end(dve, vector_at, "gqkv")
                def every(ap):
                    return ap.rearrange("p (a n) -> p a n", a=1).to_broadcast([P, 4, P])

                def lev(r):
                    return every(con[:, K_LEV + r * P:K_LEV + (r + 1) * P])

                for c in range(TILES):
                    cs = slice(c * P, (c + 1) * P)
                    for g, G in enumerate(gdn_work):
                        t, b = (c, g), 4 * g
                        dve.wait_ge(tensor_out, tensor_at.find("bb", t))
                        V.tensor_tensor(G["kb"], gk[:, 4 * g:4 * g + 4, cs], tile(b + 1), ALU.mult).then_inc(vector_out, vector_at.next("kb", t))
                    for g, G in enumerate(gdn_work):
                        t, b = (c, g), 4 * g
                        dve.wait_ge(tensor_out, tensor_at.find("kk", t))
                        dve.wait_ge(scalar_out, scalar_at.find("gam", t))
                        V.tensor_tensor(G["at"], tile(b + 1), G["gam"], ALU.mult).then_inc(vector_out, vector_at.next("at", t))
                        dve.wait_ge(vector_out, vector_at.n)
                        V.tensor_tensor(G["lt"], G["at"], lev(0), ALU.mult).then_inc(vector_out, vector_at.next("lt", t, 0))
                        dve.wait_ge(vector_out, vector_at.n)
                        V.tensor_tensor(G["u"], every(ident), G["lt"], ALU.subtract).then_inc(vector_out, vector_at.next("u", t, 0))
                        V.tensor_tensor(G["att"], tile(b + 3), G["gam"], ALU.mult).then_inc(vector_out, vector_at.next("att", t))
                    for g, G in enumerate(gdn_work):
                        t, b = (c, g), 4 * g
                        dve.wait_ge(tensor_out, tensor_at.find("l0", t))
                        dve.wait_ge(vector_out, vector_at.find("att", t))
                        V.tensor_tensor(G["t"], every(ident), tile(b + 3), ALU.subtract).then_inc(vector_out, vector_at.next("t", t, 0))
                        V.tensor_tensor(G["lt"], G["at"], lev(1), ALU.mult).then_inc(vector_out, vector_at.next("lt", t, 1))
                    for g, G in enumerate(gdn_work):
                        t, b = (c, g), 4 * g
                        dve.wait_ge(scalar_out, scalar_at.find("eg", t))
                        V.tensor_tensor(G["qg"], gq[:, 4 * g:4 * g + 4, cs], G["eg"], ALU.mult).then_inc(vector_out, vector_at.next("qg", t))
                    for r in range(1, LEVELS):
                        for g, G in enumerate(gdn_work):
                            if r < LEVELS - 1:
                                dve.wait_ge(tensor_out, tensor_at.find("x", (c, g), r))
                                V.tensor_tensor(G["lt"], G["at"], lev(r + 1), ALU.mult).then_inc(vector_out, vector_at.next("lt", (c, g), r + 1))
                        for g, G in enumerate(gdn_work):
                            t, b = (c, g), 4 * g
                            if r < LEVELS - 1:
                                dve.wait_ge(tensor_out, tensor_at.find("yt", t, r))
                                V.tensor_tensor(G["t"], G["t"], tile(b + 2), ALU.subtract).then_inc(vector_out, vector_at.next("t", t, r))
                            dve.wait_ge(tensor_out, tensor_at.find("y", t, r))
                            V.tensor_tensor(G["u"], G["u"], tile(b + 1), ALU.subtract).then_inc(vector_out, vector_at.next("u", t, r))
                    for g, G in enumerate(gdn_work):
                        t, b = (c, g), 4 * g
                        dve.wait_ge(tensor_out, tensor_at.find("s", t))
                        for hh in range(4):
                            if c:
                                STT(state[:, g, hh, :], state[:, g, hh, :], G["eg"][:, hh, P - 1:P], tile(b + 2)[:, hh, :], ALU.mult, ALU.add).then_inc(vector_out, vector_at.next("s", t))
                            else:
                                V.tensor_copy(state[:, g, hh, :], tile(b + 2)[:, hh, :]).then_inc(vector_out, vector_at.next("s", t))
                stage_end(dve, vector_at, "gdn")
                split_operand("again", U)
                for j in range(DC):
                    split_units(FIRST["z2"] + j + 2)
                    if j == 2:
                        dve.wait_ge(scalar_out, scalar_at.find("gn", "root", 0))
                        V.reciprocal(row[63][0:8, :], row[63][0:8, :]).then_inc(vector_out, vector_at.next("gn", "factors", 0))
                    for k in gn_spread.get(j, ()):
                        dve.wait_ge(tensor_out, tensor_at.find("gn", "spread", k))
                        STT(go[:, k, :], go[:, k, :], col("gdn_norm"), bank[5 + k % 3][:], ALU.mult, ALU.mult).then_inc(vector_out, vector_at.next("gn", "out", k))
                    for k in gn_spread.get(j - 1, ()):
                        dve.wait_ge(scalar_out, scalar_at.find("read", "z2", k))
                        dve.wait_ge(vector_out, vector_at.find("gn", "out", k))
                        V.tensor_tensor(go[:, k, :], go[:, k, :], arena[:, 24 + k, :], ALU.mult).then_inc(vector_out, vector_at.next("z2", k))
                for j in range(DC):
                    split_units(FIRST["gatea"] + j + 2)
                    dve.wait_ge(scalar_out, scalar_at.find("read", "gatea", j))
                    dve.wait_ge(vector_out, vector_at.find("z2", j))
                    V.tensor_tensor(go[:, j, :], go[:, j, :], arena[:, 24 + j, :], ALU.mult).then_inc(vector_out, vector_at.next())
                    dve.wait_ge(vector_out, vector_at.n)
                    V.tensor_tensor(MIX[:, j, :], MIX[:, j, :], go[:, j, :], ALU.add).then_inc(vector_out, vector_at.next("mixed", j))
                vector_at.mark("stage", "mix2")
                split_operand("mix2", MIX)
                residual("out2", "rms2", 1.0, False)
                norm("rms2", DC, X, False, "norm2", U, before="out2", operand=U)
                vector_at.mark("stage", "rms2")
            if on("up2"):
                ffn(2)
                residual("down2", "rmsf", 1.0, True)
                norm("rmsf", DC, X, False, "final", U)


LAST_STAGE = None


def lay_out(inp):
    f = {k: np.asarray(v) for k, v in inp.items()}
    units = []

    def stationary(w, padded=None):
        k, n = w.shape
        for j in range(n // P):
            units.append(w[:, j * P:(j + 1) * P].reshape(DC, P, P).transpose(1, 0, 2).reshape(P, 8 * P))

    def moving(w, q):
        n = w.shape[1]
        w = w.reshape(DC, P, n)
        for j in range(DC // q):
            units.append(w[j * q:(j + 1) * q].transpose(1, 0, 2).reshape(P, 8 * P))

    def rows(parts, shape):
        w = np.zeros(shape + (P,), np.float32)
        for x, part in enumerate(parts):
            w[..., 32 * x:32 * x + part.shape[-1]] = part
        return w

    def up(w, gate_first):
        a, b = (w[:, :D_FF], w[:, D_FF:]) if gate_first else (w[:, D_FF:], w[:, :D_FF])
        for j in range(FC):
            stationary(a[:, j * P:(j + 1) * P])
            stationary(b[:, j * P:(j + 1) * P])

    def down(w):
        for j in range(FC):
            units.append(w[j * P:(j + 1) * P, :])

    we, be = f["ev_w_in"][0], f["ev_b_in"][0]
    H = HALF
    o = [0, H, 2 * H, 3 * H, 4 * H, 4 * H + 4, 4 * H + 8, 5 * H + 8, 6 * H + 8, 7 * H + 8, 7 * H + 16]
    e = [we[:, o[i]:o[i + 1]] for i in range(10)]
    eb = [be[o[i]:o[i + 1]] for i in range(10)]
    stationary(rows([e[4], e[5], e[9]], (DM,)))
    stationary(e[0]); stationary(e[1]); moving(e[2], 2)
    stationary(e[6]); stationary(e[7]); moving(e[8], 2)
    stationary(e[3])
    stationary(f["ev_w_out"][0])
    up(f["ffn_w_up"][0], False); down(f["ffn_w_down"][0])
    wo = f["od_w_in"][0]
    stationary(rows([wo[:, 1536:1544]], (DM,)))
    stationary(wo[:, 512:1536]); stationary(wo[:, 1544:2056]); stationary(wo[:, 0:512])
    stationary(f["od_w_out"][0])
    up(f["ffn_w_up"][1], False); down(f["ffn_w_down"][1])
    w2 = f["w_in_2"][0]
    cut = lambda a, b: w2[:, a:b]
    stationary(rows([cut(4096, 4104), cut(4104, 4112), cut(6224, 6232)], (DM,)))
    stationary(np.concatenate([cut(6160, 6224)] * 2, 1))
    stationary(cut(5648, 6160)); stationary(cut(4112, 5136)); stationary(cut(5136, 5392)); moving(cut(5392, 5648), 4)
    stationary(cut(7256, 8280))
    stationary(cut(0, 3072)); stationary(cut(3072, 4096)); stationary(cut(6232, 7256))
    stationary(f["w_out_2"][0])
    up(f["ffn_w_up_2"][0], True); down(f["ffn_w_down_2"][0])
    assert len(units) == UNITS
    units += [np.zeros((P, 8 * P), np.float32)] * 2
    stream = np.ascontiguousarray(np.stack(units))

    cols = {n: [] for n, _ in COLS}

    def put(name, v):
        cols[name] += list(np.asarray(v).reshape(-1, P))

    put("b_small0", rows([eb[4], eb[5], eb[9]], ()))
    for n, x in (("b_mq", 0), ("b_mk", 1), ("b_fq", 6), ("b_fk", 7), ("b_mo", 3)):
        put(n, eb[x])
    put("ml_norm", f["ev_ml_norm"][0])
    for l in range(2):
        for n in ("ln1_g", "ln1_b", "ln2_g", "ln2_b"):
            put(f"{n}{l}", f[n][l])
    put("dt_bias", rows([f["od_dt_bias"][0]], ()))
    put("a_log", rows([f["od_a_log"][0]], ()))
    cw = f["od_conv_w"][0]
    put("xbc_conv", np.concatenate([cw, f["od_conv_b"]], 0).reshape(5, 8, P).transpose(1, 0, 2))
    put("d_skip", np.repeat(f["od_d_skip"][0], 64))
    put("ssm_norm", f["od_ssm_norm"][0]); put("pool_b", f["od_pool_b"][0]); put("pool_s", f["od_pool_scale"][0])

    def ffn_cols(name, w, b, gate_first):
        x = np.concatenate([w, b[None]], 0).reshape(4, 2, FC, P).transpose(2, 1, 0, 3)
        put(name, x if gate_first else x[:, ::-1])

    ffn_cols("ffn0", f["ffn_conv_w"][0], f["ffn_conv_b"][0], False)
    ffn_cols("ffn1", f["ffn_conv_w"][1], f["ffn_conv_b"][1], False)
    ffn_cols("ffn2", f["ffn_conv_w_2"][0], f["ffn_conv_b_2"][0], True)
    put("norm1", f["norm1_g_2"][0]); put("norm2", f["norm2_g_2"][0]); put("final", f["final_g_2"])
    put("g_dt_bias", rows([f["gdn_dt_bias_2"][0]], ())); put("g_a_log", rows([f["gdn_a_log_2"][0]], ()))
    put("gqkv_conv", f["gdn_conv_w_2"][0].reshape(4, 24, P).transpose(1, 0, 2))
    put("gdn_norm", f["gdn_norm_g_2"][0]); put("ik_norm", np.concatenate([f["idx_k_norm_g_2"][0]] * 2)); put("gate_b", f["branch_gate_b_2"][0])
    for n, c in COLS:
        assert len(cols[n]) == c, (n, len(cols[n]))
    params = np.ascontiguousarray(np.stack([v for n, _ in COLS for v in cols[n]], 1))

    con = np.zeros((P, NCONST), np.float32)
    i = np.arange(P)
    con[:, K_ID:K_ID + P] = np.eye(P)
    con[:, K_MT:K_MT + P] = np.where(i[None, :] >= i[:, None], 0.0, NEG)
    con[:, K_MQ:K_MQ + P] = np.where(i[None, :] <= i[:, None], 0.0, NEG)
    for r in range(LEVELS):
        b = 1 << r
        same = (i[:, None] // (2 * b) == i[None, :] // (2 * b)) & (i[:, None] // b % 2 == 0) & (i[None, :] // b % 2 == 1)
        con[:, K_LEV + r * P:K_LEV + (r + 1) * P] = same
    for g, w in enumerate(POOL_WINDOWS):
        con[:, K_CNT + 16 * g:K_CNT + 16 * g + 16] = 1.0 / np.minimum(np.arange(16) + 1, w)
    con[:, K_PICK + 8] = 1.0
    for h in range(8):
        for part in (0, 32, 64):
            con[part + h, K_SEL + h * P:K_SEL + (h + 1) * P] = 1.0

    xt = np.ascontiguousarray(f["x"][0].T.reshape(DC, P, SEQ).transpose(1, 0, 2))
    brow = np.ascontiguousarray(np.concatenate([eb[2], eb[8]])[None])
    poolw = np.ascontiguousarray(f["od_pool_w"][0].transpose(1, 0, 2))
    return {"stream": stream, "params": params, "brow": brow, "poolw": poolw, "consts": con, "xt": xt}


def kernel(**inputs):
    import concourse.bacc as _bacc
    from concourse.bass_utils import run_bass_kernel_spmd as _run

    arrays = lay_out(inputs)
    marks = {}
    for _ in range(2):
        nc = _bacc.Bacc("TRN2", target_bir_lowering=False, num_devices=1)
        args = [nc.dram_tensor(k, v.shape, F32, kind="ExternalInput").ap() for k, v in arrays.items()]
        args.append(nc.dram_tensor("out", (P, DC, SEQ), F32, kind="ExternalOutput").ap())
        build_program(nc, *args, marks, LAST_STAGE)
    r = _run(nc, [arrays], core_ids=[0])
    got = r.results[0]["out"]
    return np.ascontiguousarray(got.transpose(1, 0, 2).reshape(1, DM, SEQ).transpose(0, 2, 1))
```
